# Optimizing a Trainium2 kernel written in Bass

```python
import math
import jax, jax.numpy as jnp
from jax import lax
import numpy as np

D_MODEL = 1024
BATCH = 1
SEQ = 256
DEPTH = 2
DEC_BATCH = 8
DEC_SEQ = 4
PAST_LEN = 2048
PAGE_SIZE = 128

D_A = D_MODEL
NA_BLOCKS = 16
CONV_W = 4
LRU_C = 8.0
H_B = 8
HD_B = D_MODEL // H_B
D_B = H_B * HD_B
ROT_DIM = HD_B // 4
ROPE_THETA = 500000.0
DILATIONS = ((128, 1), (512, 4), (2048, 16))
MAX_WINDOW = 2048
QBLOCK = 128
D_C = 2 * D_MODEL
NH_C = 4
DH_C = D_C // NH_C
QKV_BLOCK = 4
MLSTM_CHUNK = 64
D_FF = 4 * D_MODEL
N_EVEN = (DEPTH + 1) // 2
N_ODD = DEPTH // 2
EPS = 1e-6
F32 = jnp.float32

kernel_name = 'hawk_longnet_mlstm_hybrid_step'

def rmsnorm(x, g):
    xf = x.astype(F32)
    y = xf * lax.rsqrt(jnp.mean(xf * xf, axis=-1, keepdims=True) + EPS)
    return (y * g.astype(F32)).astype(x.dtype)

def causal_dwconv(x, buf, w, b):
    L = x.shape[1]
    xp = jnp.concatenate([buf.astype(x.dtype), x], axis=1)
    y = b
    for j in range(CONV_W):
        y = y + w[j] * xp[:, j:j + L]
    return y, xp[:, -(CONV_W - 1):]

def block_diag(x, w):
    nb, bi, bo = w.shape
    xr = x.reshape(x.shape[:-1] + (nb, bi))
    return jnp.einsum('...ni,nio->...no', xr, w).reshape(x.shape[:-1] + (nb * bo,))

def rglru(x, h0, wa, ba, wx, bx, lam):
    xf = x.astype(F32)
    r = jax.nn.sigmoid(block_diag(xf, wa.astype(F32)) + ba.astype(F32))
    i = jax.nn.sigmoid(block_diag(xf, wx.astype(F32)) + bx.astype(F32))
    log_a = -LRU_C * r * jax.nn.softplus(-lam.astype(F32))
    a = jnp.exp(log_a)
    b = jnp.sqrt(-jnp.expm1(2.0 * log_a)) * (i * xf)
    b = b.at[:, 0].add(a[:, 0] * h0.astype(F32))

    def comb(left, right):
        a1, b1 = left
        a2, b2 = right
        return a1 * a2, a2 * b1 + b2

    _, h = lax.associative_scan(comb, (a, b), axis=1)
    return h, h[:, -1]

def rope(x, pos):
    half = ROT_DIM // 2
    inv = ROPE_THETA ** (-jnp.arange(0, ROT_DIM, 2, dtype=F32) / ROT_DIM)
    ang = pos.astype(F32)[:, None] * inv[None, :]
    cos = jnp.cos(ang)[None, :, None, :]
    sin = jnp.sin(ang)[None, :, None, :]
    x1, x2, rest = x[..., :half], x[..., half:ROT_DIM], x[..., ROT_DIM:]
    return jnp.concatenate([x1 * cos - x2 * sin, x1 * sin + x2 * cos, rest], axis=-1)

def dilated_group_prompt(q, k, v, window, dilation):
    B, S, H, E = q.shape
    d = dilation
    back = window // dilation
    L = S // d
    nb = -(-L // QBLOCK)
    Lp = nb * QBLOCK

    def split(t):
        return jnp.swapaxes(t.reshape(B, L, d, H, E), 1, 2)

    qb = jnp.pad(split(q), ((0, 0), (0, 0), (0, Lp - L), (0, 0), (0, 0))).reshape(B, d, nb, QBLOCK, H, E)

    def kblocks(t):
        tp = jnp.pad(split(t), ((0, 0), (0, 0), (QBLOCK, Lp - L), (0, 0), (0, 0)))
        tp = tp.reshape(B, d, nb + 1, QBLOCK, H, E)
        return jnp.concatenate([tp[:, :, :-1], tp[:, :, 1:]], axis=3)

    kk, vv = kblocks(k), kblocks(v)
    s = jnp.einsum('bdnqhe,bdnkhe->bdnhqk', qb, kk)
    qi = jnp.arange(QBLOCK)[:, None]
    ki = jnp.arange(2 * QBLOCK)[None, :]
    dist = qi + QBLOCK - ki
    blk = jnp.arange(nb)[:, None, None]
    valid = (dist >= 0) & (dist <= back) & (blk * QBLOCK - QBLOCK + ki >= 0)
    s = jnp.where(valid[None, None, :, None], s, -jnp.inf)
    m = jnp.max(s, axis=-1)
    p = jnp.exp(s - m[..., None])
    den = jnp.sum(p, axis=-1)
    acc = jnp.einsum('bdnhqk,bdnkhe->bdnqhe', p, vv)

    def merge(t):
        rest = t.shape[4:]
        t = t.reshape((B, d, Lp) + rest)[:, :, :L]
        return jnp.swapaxes(t, 1, 2).reshape((B, S) + rest)

    return merge(jnp.swapaxes(m, -1, -2)), merge(jnp.swapaxes(den, -1, -2)), merge(acc)

def dilated_group_sample(q, k_all, v_all, window, dilation, wb):
    T = q.shape[1]
    back = window // dilation
    idx = wb + jnp.arange(T)[:, None] - dilation * jnp.arange(back + 1)[None, :]
    valid = idx >= 0
    idxc = jnp.maximum(idx, 0)
    kg = k_all[:, idxc]
    vg = v_all[:, idxc]
    s = jnp.einsum('bthe,btjhe->bthj', q, kg)
    s = jnp.where(valid[None, :, None, :], s, -jnp.inf)
    m = jnp.max(s, axis=-1)
    p = jnp.exp(s - m[..., None])
    den = jnp.sum(p, axis=-1)
    acc = jnp.einsum('bthj,btjhe->bthe', p, vg)
    return m, den, acc

def merge_dilation_groups(parts):
    ms = jnp.stack([pt[0] for pt in parts])
    dens = jnp.stack([pt[1] for pt in parts])
    accs = jnp.stack([pt[2] for pt in parts])
    w = jnp.exp(ms - jnp.max(ms, axis=0))
    return jnp.sum(w[..., None] * accs, axis=0) / jnp.sum(w * dens, axis=0)[..., None]

def hybrid_ab_mixer(xn, pos, conv_buf, h0, k_buf, v_buf, w_in, conv_w, conv_b, wa, ba, wx, bx, lam, w_out):
    B, L, _ = xn.shape
    xa, ga, q, k, v = jnp.split(xn @ w_in, [D_A, 2 * D_A, 2 * D_A + D_B, 2 * D_A + 2 * D_B], axis=-1)
    xc, new_conv = causal_dwconv(xa, conv_buf, conv_w, conv_b)
    h, h_last = rglru(xc, h0, wa, ba, wx, bx, lam)
    ya = h * jax.nn.gelu(ga.astype(F32))
    q = rope(q.reshape(B, L, H_B, HD_B).astype(F32), pos) * (HD_B ** -0.5)
    k = rope(k.reshape(B, L, H_B, HD_B).astype(F32), pos)
    v = v.reshape(B, L, H_B, HD_B).astype(F32)
    if k_buf is None:
        parts = [dilated_group_prompt(q, k, v, w, d) for (w, d) in DILATIONS]
        wb = min(MAX_WINDOW, L)
        new_k, new_v = k[:, L - wb:], v[:, L - wb:]
    else:
        wb = k_buf.shape[1]
        k_all = jnp.concatenate([k_buf.astype(F32), k], axis=1)
        v_all = jnp.concatenate([v_buf.astype(F32), v], axis=1)
        parts = [dilated_group_sample(q, k_all, v_all, w, d, wb) for (w, d) in DILATIONS]
        new_k, new_v = k, v
    yb = merge_dilation_groups(parts).reshape(B, L, D_B)
    y = jnp.concatenate([ya, yb], axis=-1).astype(xn.dtype) @ w_out
    return y, new_conv, h_last, new_k, new_v

def mlstm_chunkwise(q, k, v, i_pre, f_pre, C0, n0, m0):
    B, L, NH, DH = q.shape
    c = math.gcd(L, MLSTM_CHUNK)
    nc = L // c

    def to_chunks(t):
        return jnp.moveaxis(t.reshape((B, nc, c) + t.shape[2:]), 1, 0)

    xs = tuple(to_chunks(t) for t in (q, k, v, i_pre, f_pre))
    causal = jnp.tril(jnp.ones((c, c), dtype=bool))

    def step(carry, inp):
        C, n, m = carry
        qc, kc, vc, ic, fc = inp
        bcum = jnp.cumsum(jax.nn.log_sigmoid(fc), axis=1)
        log_intra = bcum[:, :, None, :] - bcum[:, None, :, :] + ic[:, None, :, :]
        log_intra = jnp.where(causal[None, :, :, None], log_intra, -jnp.inf)
        log_inter = bcum + m[:, None, :]
        m_t = jnp.maximum(log_inter, jnp.max(log_intra, axis=2))
        w_intra = jnp.exp(log_intra - m_t[:, :, None, :]) * jnp.einsum('bthd,bshd->btsh', qc, kc)
        w_inter = jnp.exp(log_inter - m_t)
        num = jnp.einsum('btsh,bshe->bthe', w_intra, vc) + w_inter[..., None] * jnp.einsum('bthd,bhde->bthe', qc, C)
        den = jnp.sum(w_intra, axis=2) + w_inter * jnp.einsum('bthd,bhd->bth', qc, n)
        h = num / jnp.maximum(jnp.abs(den), jnp.exp(-m_t))[..., None]
        m_new = m_t[:, -1]
        w_state = jnp.exp(bcum[:, -1:, :] - bcum + ic - m_new[:, None, :])
        decay = jnp.exp(bcum[:, -1] + m - m_new)
        kw = kc * w_state[..., None]
        C_new = decay[..., None, None] * C + jnp.einsum('bshd,bshe->bhde', kw, vc)
        n_new = decay[..., None] * n + jnp.sum(kw, axis=1)
        return (C_new, n_new, m_new), h

    (C, n, m), hs = lax.scan(step, (C0, n0, m0), xs)
    h = jnp.moveaxis(hs, 0, 1).reshape(B, L, NH, DH)
    return h, C, n, m

def mlstm_mixer(xn, conv_buf, C0, n0, m0, w_in, conv_w, conv_b, wq, wk, wv, w_gate, b_gate, norm_w, skip, w_out):
    B, L, _ = xn.shape
    xm, z = jnp.split(xn @ w_in, 2, axis=-1)
    xc, new_conv = causal_dwconv(xm, conv_buf, conv_w, conv_b)
    xc = jax.nn.silu(xc)
    q = block_diag(xc, wq)
    k = block_diag(xc, wk)
    v = block_diag(xm, wv)
    gates = (jnp.concatenate([q, k, v], axis=-1) @ w_gate + b_gate).astype(F32)
    i_pre, f_pre = gates[..., :NH_C], gates[..., NH_C:]

    def heads(t):
        return t.reshape(B, L, NH_C, DH_C).astype(F32)

    h, C, n, m = mlstm_chunkwise(heads(q), heads(k) * (DH_C ** -0.5), heads(v), i_pre, f_pre,
                                 C0.astype(F32), n0.astype(F32), m0.astype(F32))
    h = h * lax.rsqrt(jnp.mean(h * h, axis=-1, keepdims=True) + EPS)
    h = h.reshape(B, L, D_C) * norm_w.astype(F32)
    y = (h + skip * xc) * jax.nn.silu(z)
    return y.astype(xn.dtype) @ w_out, new_conv, C, n, m

def run_trunk(x, pos, conv_a0, h_a0, k_buf, v_buf, conv_c0, C0, n0, m0, p):
    new = [[] for _ in range(8)]
    for layer in range(DEPTH):
        xn = rmsnorm(x, p['norm_mix_pre'][layer])
        if layer % 2 == 0:
            e = layer // 2
            y, *st = hybrid_ab_mixer(
                xn, pos, conv_a0[e], h_a0[e],
                None if k_buf is None else k_buf[e], None if v_buf is None else v_buf[e],
                p['w_in_ab'][e], p['conv_a_w'][e], p['conv_a_b'][e], p['lru_wa'][e], p['lru_ba'][e],
                p['lru_wx'][e], p['lru_bx'][e], p['lru_lambda'][e], p['w_out_ab'][e])
            for j, s in enumerate(st):
                new[j].append(s)
        else:
            o = layer // 2
            y, *st = mlstm_mixer(
                xn, conv_c0[o], C0[o], n0[o], m0[o],
                p['w_in_c'][o], p['conv_c_w'][o], p['conv_c_b'][o], p['mlstm_wq'][o], p['mlstm_wk'][o],
                p['mlstm_wv'][o], p['mlstm_w_gate'][o], p['mlstm_b_gate'][o], p['mlstm_norm'][o],
                p['mlstm_skip'][o], p['w_out_c'][o])
            for j, s in enumerate(st):
                new[4 + j].append(s)
        x = x + rmsnorm(y, p['norm_mix_post'][layer])
        xn = rmsnorm(x, p['norm_ffn_pre'][layer])
        hid = jnp.square(jax.nn.relu(xn @ p['w_ffn_up'][layer]))
        x = x + rmsnorm(hid @ p['w_ffn_down'][layer], p['norm_ffn_post'][layer])
    return x, [jnp.stack(s) for s in new]

def setup_inputs(seed: int = 0) -> dict:
    key = jax.random.key(seed)
    ks = iter(jax.random.split(key, 48))

    def nrm(shape, scale):
        return scale * jax.random.normal(next(ks), shape, F32)

    def gain(shape):
        return 1.0 + nrm(shape, 0.05)

    wb = min(MAX_WINDOW, PAST_LEN)
    u = jax.random.uniform(next(ks), (N_EVEN, D_A), F32, 0.9, 0.999)
    lam = jnp.log(u) - jnp.log1p(-u)
    b_gate = jnp.concatenate([
        nrm((N_ODD, NH_C), 0.1),
        jnp.broadcast_to(jnp.linspace(3.0, 6.0, NH_C, dtype=F32), (N_ODD, NH_C)) + nrm((N_ODD, NH_C), 0.01)], axis=-1)
    d_in_ab = 2 * D_A + 3 * D_B
    return {
        'x_prompt': nrm((BATCH, SEQ, D_MODEL), 1.0),
        'x_sample': nrm((DEC_BATCH, DEC_SEQ, D_MODEL), 1.0),
        'state_rglru_conv': nrm((N_EVEN, DEC_BATCH, CONV_W - 1, D_A), 1.0),
        'state_rglru_h': nrm((N_EVEN, DEC_BATCH, D_A), 0.5),
        'cache_swa_k': nrm((N_EVEN, DEC_BATCH, wb, H_B, HD_B), 1.0),
        'cache_swa_v': nrm((N_EVEN, DEC_BATCH, wb, H_B, HD_B), 1.0),
        'state_mlstm_conv': nrm((N_ODD, DEC_BATCH, CONV_W - 1, D_C), 1.0),
        'state_mlstm_C': nrm((N_ODD, DEC_BATCH, NH_C, DH_C, DH_C), 0.02),
        'state_mlstm_n': nrm((N_ODD, DEC_BATCH, NH_C, DH_C), 0.1),
        'state_mlstm_m': nrm((N_ODD, DEC_BATCH, NH_C), 1.0),
        'norm_mix_pre': gain((DEPTH, D_MODEL)),
        'norm_mix_post': gain((DEPTH, D_MODEL)),
        'norm_ffn_pre': gain((DEPTH, D_MODEL)),
        'norm_ffn_post': gain((DEPTH, D_MODEL)),
        'w_ffn_up': nrm((DEPTH, D_MODEL, D_FF), D_MODEL ** -0.5),
        'w_ffn_down': nrm((DEPTH, D_FF, D_MODEL), D_FF ** -0.5),
        'w_in_ab': nrm((N_EVEN, D_MODEL, d_in_ab), D_MODEL ** -0.5),
        'conv_a_w': nrm((N_EVEN, CONV_W, D_A), CONV_W ** -0.5),
        'conv_a_b': nrm((N_EVEN, D_A), 0.01),
        'lru_wa': nrm((N_EVEN, NA_BLOCKS, D_A // NA_BLOCKS, D_A // NA_BLOCKS), (D_A // NA_BLOCKS) ** -0.5),
        'lru_ba': nrm((N_EVEN, D_A), 0.01),
        'lru_wx': nrm((N_EVEN, NA_BLOCKS, D_A // NA_BLOCKS, D_A // NA_BLOCKS), (D_A // NA_BLOCKS) ** -0.5),
        'lru_bx': nrm((N_EVEN, D_A), 0.01),
        'lru_lambda': lam,
        'w_out_ab': nrm((N_EVEN, D_A + D_B, D_MODEL), (D_A + D_B) ** -0.5),
        'w_in_c': nrm((N_ODD, D_MODEL, 2 * D_C), D_MODEL ** -0.5),
        'conv_c_w': nrm((N_ODD, CONV_W, D_C), CONV_W ** -0.5),
        'conv_c_b': nrm((N_ODD, D_C), 0.01),
        'mlstm_wq': nrm((N_ODD, D_C // QKV_BLOCK, QKV_BLOCK, QKV_BLOCK), QKV_BLOCK ** -0.5),
        'mlstm_wk': nrm((N_ODD, D_C // QKV_BLOCK, QKV_BLOCK, QKV_BLOCK), QKV_BLOCK ** -0.5),
        'mlstm_wv': nrm((N_ODD, D_C // QKV_BLOCK, QKV_BLOCK, QKV_BLOCK), QKV_BLOCK ** -0.5),
        'mlstm_w_gate': nrm((N_ODD, 3 * D_C, 2 * NH_C), 0.1 * (3 * D_C) ** -0.5),
        'mlstm_b_gate': b_gate,
        'mlstm_norm': gain((N_ODD, D_C)),
        'mlstm_skip': gain((N_ODD, D_C)),
        'w_out_c': nrm((N_ODD, D_C, D_MODEL), D_C ** -0.5),
    }

def reference(x_prompt, x_sample, state_rglru_conv, state_rglru_h, cache_swa_k, cache_swa_v,
              state_mlstm_conv, state_mlstm_C, state_mlstm_n, state_mlstm_m,
              norm_mix_pre, norm_mix_post, norm_ffn_pre, norm_ffn_post, w_ffn_up, w_ffn_down,
              w_in_ab, conv_a_w, conv_a_b, lru_wa, lru_ba, lru_wx, lru_bx, lru_lambda, w_out_ab,
              w_in_c, conv_c_w, conv_c_b, mlstm_wq, mlstm_wk, mlstm_wv, mlstm_w_gate, mlstm_b_gate,
              mlstm_norm, mlstm_skip, w_out_c):
    p = {
        'norm_mix_pre': norm_mix_pre, 'norm_mix_post': norm_mix_post,
        'norm_ffn_pre': norm_ffn_pre, 'norm_ffn_post': norm_ffn_post,
        'w_ffn_up': w_ffn_up, 'w_ffn_down': w_ffn_down,
        'w_in_ab': w_in_ab, 'conv_a_w': conv_a_w, 'conv_a_b': conv_a_b,
        'lru_wa': lru_wa, 'lru_ba': lru_ba, 'lru_wx': lru_wx, 'lru_bx': lru_bx,
        'lru_lambda': lru_lambda, 'w_out_ab': w_out_ab,
        'w_in_c': w_in_c, 'conv_c_w': conv_c_w, 'conv_c_b': conv_c_b,
        'mlstm_wq': mlstm_wq, 'mlstm_wk': mlstm_wk, 'mlstm_wv': mlstm_wv,
        'mlstm_w_gate': mlstm_w_gate, 'mlstm_b_gate': mlstm_b_gate,
        'mlstm_norm': mlstm_norm, 'mlstm_skip': mlstm_skip, 'w_out_c': w_out_c,
    }
    B, S, _ = x_prompt.shape
    dt = x_prompt.dtype
    y_prompt, new_p = run_trunk(
        x_prompt, jnp.arange(S),
        jnp.zeros((N_EVEN, B, CONV_W - 1, D_A), dt), jnp.zeros((N_EVEN, B, D_A), dt), None, None,
        jnp.zeros((N_ODD, B, CONV_W - 1, D_C), dt), jnp.zeros((N_ODD, B, NH_C, DH_C, DH_C), dt),
        jnp.zeros((N_ODD, B, NH_C, DH_C), dt), jnp.zeros((N_ODD, B, NH_C), dt), p)
    y_sample, new_s = run_trunk(
        x_sample, PAST_LEN + jnp.arange(x_sample.shape[1]),
        state_rglru_conv, state_rglru_h, cache_swa_k, cache_swa_v,
        state_mlstm_conv, state_mlstm_C, state_mlstm_n, state_mlstm_m, p)
    refs = (state_rglru_conv, state_rglru_h, cache_swa_k, cache_swa_v,
            state_mlstm_conv, state_mlstm_C, state_mlstm_n, state_mlstm_m)
    p_rglru_conv, p_rglru_h, p_swa_k, p_swa_v, p_mlstm_conv, p_mlstm_C, p_mlstm_n, p_mlstm_m = [
        t.astype(r.dtype) for t, r in zip(new_p, refs)]
    s_rglru_conv, s_rglru_h, s_swa_k, s_swa_v, s_mlstm_conv, s_mlstm_C, s_mlstm_n, s_mlstm_m = [
        t.astype(r.dtype) for t, r in zip(new_s, refs)]
    return (y_prompt, y_sample,
            p_rglru_conv, s_rglru_conv, p_rglru_h, s_rglru_h,
            p_swa_k, s_swa_k, p_swa_v, s_swa_v,
            p_mlstm_conv, s_mlstm_conv, p_mlstm_C, s_mlstm_C,
            p_mlstm_n, s_mlstm_n, p_mlstm_m, s_mlstm_m)


_drawn_inputs = setup_inputs


def setup_inputs(seed=0):
    import zlib

    import numpy as np

    out = dict(_drawn_inputs(seed))
    spreads = {}
    factors = {'lru_ba': 23.4, 'lru_bx': 8.0, 'conv_c_b': 2.794, 'mlstm_skip': 4.387, 'mlstm_norm': 6.151}
    for name, (base, spread) in spreads.items():
        noise = np.random.default_rng([zlib.crc32(name.encode()), seed]).standard_normal(out[name].shape)
        drawn = base * np.exp(spread * noise) if base else spread * noise
        out[name] = __import__('jax').numpy.asarray(drawn.astype(out[name].dtype))
    for name, factor in factors.items():
        out[name] = (out[name] * factor).astype(out[name].dtype)
    return out
```

```python
from contextlib import ExitStack

import numpy as np

import concourse.bass as bass
from concourse import mybir

F32 = mybir.dt.float32
F32R = mybir.dt.float32r
ALU = mybir.AluOpType
ACT = mybir.ActivationFunctionType
AX = mybir.AxisListType

P = 128
D = 1024
SEQ = 256
NB = 8
NT = 4
NS = NB * NT
T = SEQ + NS
CW = 4
PAD = CW - 1
S0 = PAD + SEQ
LONG = PAD + NT
ROW = S0 + NB * LONG
CONV = ROW - PAD
EPS = 1e-6
MT = D // P
H = 8
HD = 128
ROT = HD // 4
THETA = 500000.0
PAST = 2048
DIL = ((128, 1), (512, 4), (2048, 16))
LRU_C = 8.0
NBLK = 16
DC = 2 * D
CT = DC // P
NH = 4
DH = DC // NH
ET = DH // P
QB = 4
FF = 4 * D
NEG = -1e30

KEYS = [p for p in range(PAST) if p >= PAST - DIL[1][0] or p % DIL[2][1] < NT]
NK = len(KEYS)
KT = NK // P
NKS = NK + NS
KV_SLOTS = 4
HALF_B = NB // 2

DENSE = [(D, 5 * D), (2 * D, D), (D, FF), (FF, D), (D, 4 * D), (2 * D, D), (D, FF), (FF, D)]
IN_AB, OUT_AB, UP0, DOWN0, IN_C, OUT_C, UP1, DOWN1 = range(8)
UK = 8
UM = 4
UNITS = [k // (UK * P) * (m // (UM * P)) for k, m in DENSE]
STEP0 = [UM * sum(UNITS[:i]) for i in range(8)]
OUT0 = [sum(m // P for _, m in DENSE[:i]) for i in range(8)]
NUNITS = sum(UNITS)
NSTEPS = UM * NUNITS
TILE = UK * P

PARTS = [("g_mix_pre", 2 * MT), ("g_mix_post", 2 * MT), ("g_ffn_pre", 2 * MT), ("g_ffn_post", 2 * MT),
         ("conv_a_w", CW * MT), ("conv_a_b", MT), ("lru_ba", MT), ("lru_bx", MT), ("lru_lambda", MT),
         ("h0", MT * NB), ("conv_a0", MT * NB * PAD),
         ("conv_c_w", CW * CT), ("conv_c_b", CT), ("norm_w", CT), ("skip", CT),
         ("n0", NH * ET * NB), ("conv_c0", CT * NB * PAD)]
NPAR = sum(w for _, w in PARTS)
AT = {name: sum(w for _, w in PARTS[:i]) for i, (name, _) in enumerate(PARTS)}
R_NEGM, R_EN, R_INTER, R_DECAY = 0, T, 2 * T, 2 * T + NS
NROWS = 2 * T + NS + NB
GH = 36
C_SLOTS = 4
HD2 = ET // 2
ITEMS = 2 * NB + 2


class Tally:

    def __init__(self, eng, sem):
        self.eng, self.sem, self.n = eng, sem, 0

    def mark(self, ins):
        ins.then_inc(self.sem, 1)
        self.n = self.n + 1

    def wait(self):
        self.eng.wait_ge(self.sem, self.n)

    def after(self, ins):
        self.mark(ins)
        self.wait()


def program(nc, A, O):
    ctx = ExitStack()
    with ctx:
        ARENA = 212000 // 32 * 32
        ctx.enter_context(nc.sbuf_tensor("arena", [P, ARENA // 4], F32))
        arena0 = nc.sbuf_base - ARENA

        def at(name, off, *dims, dt=F32, parts=P):
            off = (off + 31) // 32 * 32
            n = int(np.prod(dims))
            assert off + 4 * n <= ARENA, (name, off + 4 * n - ARENA)
            t = nc.alloc_sbuf_tensor_at(name, [parts, n], dt, offset=arena0 + off)[:, :]
            if len(dims) == 2:
                t = t.rearrange("p (a b) -> p a b", b=dims[1])
            if len(dims) == 3:
                t = t.rearrange("p (a b c) -> p a b c", b=dims[1], c=dims[2])
            return t, (off + 4 * n + 31) // 32 * 32

        par, o = at("par", 0, NPAR)
        ident, o = at("ident", o, P)
        ones, o = at("ones", o, P)
        tiny, o = at("tiny", o, 2)
        w_raw, o = at("w_raw", o, 2, UM, TILE)
        w_hi, o = at("w_hi", o, UM, TILE, dt=F32R)
        w_lo, o = at("w_lo", o, UM, TILE, dt=F32R)
        x, o = at("x", o, MT, T)
        rstd_at = o
        rstd, o = at("rstd", o, T)
        std, o = at("std", o, T)
        sqsum, o = at("sqsum", o, T)
        sq_at = o
        sq, o = at("sq", o, 2, T)
        phase = o
        y, _ = at("y", ARENA - 4 * MT * T, MT, T)
        xin_hi, o = at("xin_hi", phase, MT, T, dt=F32R)
        xin_lo, behind_xin = at("xin_lo", o, MT, T, dt=F32R)
        hid_hi, o = at("hid_hi", behind_xin, FF // P, T, dt=F32R)
        hid_lo, o = at("hid_lo", o, FF // P, T, dt=F32R)
        relu, o = at("relu", o, 2, T)
        relu2, o = at("relu2", o, 2, T)

        xa, o = at("xa", behind_xin, MT, ROW)
        behind_ga = o + 4 * MT * T
        v_at = o + 3 * 4 * MT * T
        gaqkv, o = at("gaqkv", o, 4 * MT, T)
        ga, q, k, v = (gaqkv[:, MT * i:MT * i + MT] for i in range(4))
        ya_hi, o = at("ya_hi", o, MT, T, dt=F32R)
        ya_lo, o = at("ya_lo", o, MT, T, dt=F32R)
        kv, o = at("kv", o, KV_SLOTS, NK)
        cosr, o = at("cosr", o, T, parts=ROT)
        sinr, o = at("sinr", o, T, parts=ROT)
        rotm, o = at("rotm", o, ROT, parts=ROT)
        qz, o = at("qz", o, 2, H * (32 + NT))
        qz_of = qz[:, :, 0:H * 32].rearrange("p s (h c) -> p s h c", c=32)
        qz_diag = qz.rearrange("p s (h c) -> p s h c", c=32 + NT)[:, :, :, 0:NT]
        att, o = at("att", o, 2, 8)
        pack_a, o = at("pack_a", o, MT, (1 + NB) * CW)
        lruw_at = o
        lruw, o = at("lruw", o, 2 * MT, P)
        lrut, o = at("lrut", o, 8, MT)
        HM = MT // 2
        ip, late = at("ip", o, HM, ROW)
        hp, late = at("hp", late, HM, ROW)
        gg, _ = at("gg", o, HM, T)
        rot, _ = at("rot", o, HM, T)
        xc, o = at("xc", phase, HM, ROW)
        rp, o = at("rp", o, HM, ROW)
        tp, o = at("tp", o, HM, ROW)
        assert o <= behind_xin
        gelu, _ = at("gelu", phase + 4 * HM * ROW, HM, T)
        yb_hi, o = at("yb_hi", behind_xin, H, T, dt=F32R)
        yb_lo, o = at("yb_lo", o, H, T, dt=F32R)
        assert o <= behind_ga
        vtok, o = at("vtok", phase, 3, D)
        sS, o = at("sS", o, NKS)
        assert o <= behind_xin
        pT, o = at("pT", v_at, KT + 1, 2 * P)
        assert o <= v_at + 4 * H * T
        amask, o = at("amask", lruw_at, 3 * P)
        smask, o = at("smask", o, NK + 2 * NS)
        pS, o = at("pS", o, 2, 3 * P)
        pTp, o = at("pTp", o, 2, 3 * P)

        xm, o = at("xm", behind_xin, CT, ROW)
        behind_xm = o
        z, o = at("z", o, CT, T)
        y1_hi, _ = at("y1_hi", behind_xm, CT, T, dt=F32R)
        y1_lo, _ = at("y1_lo", behind_xin, CT, T, dt=F32R)
        xms, o = at("xms", o, CT, NS)
        xcc, _ = at("xcc", phase, CT, T)
        heads = o
        qkvw, o = at("qkvw", o, 6, CT, QB)
        bmask, o = at("bmask", o, P)
        fold, o = at("fold", o, 2 * CT, GH)
        sel, o = at("sel", o, NH * P, parts=NH)
        tri, o = at("tri", o, P)
        stri, o = at("stri", o, NS, parts=NS)
        selb, o = at("selb", o, NB, parts=NS)
        gsml, o = at("gsml", o, 2 + NB, parts=NH)
        tokg, o = at("tokg", o, 3, 2 * NH)
        wmask, o = at("wmask", o, NH * NB, parts=NS)
        pack_c, o = at("pack_c", o, CT, (1 + NB) * PAD)
        pack_n, o = at("pack_n", o, NH * ET, 1 + NB)
        pack_m, o = at("pack_m", o, 1 + NB, parts=NH)
        rows, o = at("rows", o, NROWS, parts=NH)
        work = o
        wgate, _ = at("wgate", work, 3 * CT, 2 * NH)
        bdT, o = at("bdT", work + 4 * 3 * CT * 2 * NH, 3 * CT, P)
        convt, _ = at("convt", o, 4, CONV + 4)
        gi, o = at("gi", work, ROW, parts=NH)
        gf, o = at("gf", o, ROW, parts=NH)
        gt, o = at("gt", o, ROW, parts=NH)
        gb, o = at("gb", o, ROW, parts=NH)
        gg_c, o = at("gg_c", o, T, parts=NH)
        gw_c, o = at("gw_c", o, T, parts=NH)
        ghist, o = at("ghist", o, 2 * ROW, parts=NH)
        bd, o = at("bd", work, 3 * ET, P)
        qf, o = at("qf", o, ET, T)
        kf, o = at("kf", o, ET, T)
        ktok, o = at("ktok", o, 3, DH)
        vtk, o = at("vtk", o, 3, DH)
        bc, e = at("bc", rstd_at, NROWS)
        qs, e = at("qs", e, ET, NS)
        assert e <= sq_at
        ew, e = at("ew", sq_at, 3 * P + NS)
        qn, e = at("qn", e, ET, NS)
        assert e <= phase
        vb, o = at("vb", o, 2, DH)
        hT_at = o
        hT, o = at("hT", o, ET, T)
        vw, _ = at("vw", hT_at, 2, DH)
        cring, o = at("cring", o, C_SLOTS, HD2, DH)
        ps = ctx.enter_context(nc.psum_tensor("ps", [P, 8, 512], F32))

        def pcol(name, i):
            return par[:, AT[name] + i:AT[name] + i + 1]

        def samples(row_ap, lo, n):
            if len(row_ap.shape) == 2:
                return row_ap[:, S0:ROW].rearrange("p (b c) -> p b c", c=LONG)[:, :, lo:lo + n]
            return row_ap[:, :, S0:ROW].rearrange("p m (b c) -> p m b c", c=LONG)[:, :, :, lo:lo + n]

        def seqs(ap):
            return ap.rearrange("p (b t) -> p b t", t=NT)

        sems = {}

        def sem(name):
            sems[name] = ctx.enter_context(nc.semaphore(name))
            return sems[name]

        consts_in = sem("consts_in")
        x_in = sem("x_in")
        masks_in = sem("masks_in")
        consts_c_in = sem("consts_c_in")
        raw_in = [sem(f"raw_in{s}") for s in range(2)]
        hi_ready = sem("hi_ready")
        lo_ready = sem("lo_ready")
        step_done = sem("step_done")
        out_taken = sem("out_taken")
        sq_ready = sem("sq_ready")
        sq_added = sem("sq_added")
        mean_ready = sem("mean_ready")
        std_ready = sem("std_ready")
        rstd_ready = sem("rstd_ready")
        x_new = sem("x_new")
        xin_hi_ready = sem("xin_hi_ready")
        xin_ready = sem("xin_ready")
        relu2_ready = sem("relu2_ready")
        hid_hi_ready = sem("hid_hi_ready")
        hid_ready = sem("hid_ready")
        v_order = sem("v_order")
        a_order = sem("a_order")
        p_order = sem("p_order")
        tiny_ready = sem("tiny_ready")
        lam_v = sem("lam_v")
        lam_a = sem("lam_a")
        lruw_zero = sem("lruw_zero")
        lruw_in = sem("lruw_in")
        pads_ready = sem("pads_ready")
        rot_ready = sem("rot_ready")
        rot_taken = sem("rot_taken")
        rope_done = sem("rope_done")
        conv_ready = sem("conv_ready")
        gates_ready = sem("gates_ready")
        gates_taken = sem("gates_taken")
        th_ready = sem("th_ready")
        b_arg = sem("b_arg")
        b_root = sem("b_root")
        scanned = sem("scanned")
        gelu_ready = sem("gelu_ready")
        ya_full = sem("ya_full")
        ya_hi_ready = sem("ya_hi_ready")
        ya_ready = sem("ya_ready")
        vt_ready = sem("vt_ready")
        vt_taken = sem("vt_taken")
        kv_in = [sem(f"kv_in{s}") for s in range(KV_SLOTS)]
        kv_free = sem("kv_free")
        qz_ready = sem("qz_ready")
        s_ready = sem("s_ready")
        s_taken = sem("s_taken")
        max_ready = sem("max_ready")
        exp_ready = sem("exp_ready")
        p_ready = sem("p_ready")
        pt_ready = sem("pt_ready")
        pt_taken = sem("pt_taken")
        pv_ready = sem("pv_ready")
        yb_hi_ready = sem("yb_hi_ready")
        yb_ready = sem("yb_ready")
        ss_taken = sem("ss_taken")
        smax_ready = sem("smax_ready")
        sexp_ready = sem("sexp_ready")
        sp_ready = sem("sp_ready")
        spt_ready = sem("spt_ready")
        spt_taken = sem("spt_taken")
        v_stored = sem("v_stored")
        stored = sem("stored")
        bdT_ready = sem("bdT_ready")
        bdT_used = sem("bdT_used")
        fold_zero = sem("fold_zero")
        fold_ready = sem("fold_ready")
        xm_pads = sem("xm_pads")
        convc_ready = sem("convc_ready")
        xcc_ready = sem("xcc_ready")
        z_ready = sem("z_ready")
        g_ready = sem("g_ready")
        gin_ready = sem("gin_ready")
        gv = sem("gv")
        gact = sem("gact")
        gcol_ready = sem("gcol_ready")
        gcol_taken = sem("gcol_taken")
        wmask_ready = sem("wmask_ready")
        bd_ready = sem("bd_ready")
        q_psum = sem("q_psum")
        q_taken = sem("q_taken")
        k_psum = sem("k_psum")
        k_taken = sem("k_taken")
        kt_psum = sem("kt_psum")
        kt_taken = sem("kt_taken")
        vt1_psum = sem("vt1_psum")
        vt1_taken = sem("vt1_taken")
        bc_psum = sem("bc_psum")
        bc_taken = sem("bc_taken")
        ew_arg = sem("ew_arg")
        ew_exp = sem("ew_exp")
        s1_psum = sem("s1_psum")
        ew_ready = sem("ew_ready")
        qs_ready = sem("qs_ready")
        vb_ready = sem("vb_ready")
        vw_ready = sem("vw_ready")
        c_in = [sem(f"c_in{s}") for s in range(C_SLOTS)]
        c_out = [sem(f"c_out{s}") for s in range(C_SLOTS)]
        c_mm = sem("c_mm")
        c_new = sem("c_new")
        n_psum = sem("n_psum")
        n_taken = sem("n_taken")
        den_psum = sem("den_psum")
        den_abs = sem("den_abs")
        h_ready = sem("h_ready")
        h_sq = sem("h_sq")
        h_mean = sem("h_mean")
        h_std = sem("h_std")
        y1_full = sem("y1_full")
        y1_hi_ready = sem("y1_hi_ready")
        y1_ready = sem("y1_ready")

        block = ctx.enter_context(nc.Block())

        def loop(eng, n, body, peel_first=True, peel_last=False):
            a, b = (1 if peel_first else 0), (n - 1 if peel_last else n)
            if peel_first:
                body(0)
            if b - a > 1:
                with eng.Fori(a, b) as i:
                    body(i)
            elif b > a:
                body(a)
            if peel_last and n - 1 >= a:
                body(n - 1)

        def store_cols(sp, out, src):
            sp.dma_start(out, src).then_inc(stored, 16)

        @block.sync
        def _(sp):
            def const(dst, name):
                sp.dma_start(dst, A[name]).then_inc(consts_in, 16)

            def unit(u, count):
                s = count
                sp.dma_start(w_raw[:, s], A["weights"][bass.ds(u, 1)].rearrange("u p (j c) -> (u p) j c", j=UM)
                             ).then_inc(raw_in[s], 16)

            def unit_pairs(a, b):
                with sp.Fori(a, b) as i:
                    for s in range(2):
                        sp.wait_ge(lo_ready, UM * (2 * i + s - 1))
                        unit(2 * i + s, s)

            def cache(i, s):
                sp.dma_start(kv[:, s], A["kv"][bass.ds(i, 1)].rearrange("u p c -> (u p) c")
                             ).then_inc(kv_in[s], 16)

            const(par, "par")
            sp.dma_start(x, A["x"]).then_inc(x_in, 16)
            unit(0, 0)
            unit(1, 1)
            const(ident, "ident")
            const(ones, "ones")
            const(cosr, "cosr")
            const(sinr, "sinr")
            const(rotm, "rotm")
            sp.wait_ge(lruw_zero, 1)
            for g, name in enumerate(("lru_wa", "lru_wx")):
                for e in range(2):
                    src = A[name].rearrange("(m e) i o -> e i m o", e=2)[e]
                    sp.dma_start(lruw[64 * e:64 * e + 64, g * MT:(g + 1) * MT, 64 * e:64 * e + 64], src
                                 ).then_inc(lruw_in, 16)
            for s in range(KV_SLOTS):
                cache(s, s)
            unit_pairs(1, UNITS[0] // 2 + 1)
            sp.wait_ge(out_taken, OUT0[OUT_AB])
            sp.dma_start(O["v"], v.rearrange("p h t -> p (h t)")).then_inc(v_stored, 16)

            def cache_group(i):
                for s in range(KV_SLOTS):
                    sp.wait_ge(kv_free, KV_SLOTS * i + s - (KV_SLOTS - 1))
                    cache(KV_SLOTS * i + s, s)

            with sp.Fori(1, NB * H // KV_SLOTS) as i:
                cache_group(i)
            sp.wait_ge(rope_done, 4)
            store_cols(sp, O["k"], k.rearrange("p h t -> p (h t)"))
            sp.wait_ge(ya_ready, 2)
            store_cols(sp, O["pack_a"], pack_a.rearrange("p m c -> p (m c)"))
            sp.dma_start(amask, A["amask"]).then_inc(masks_in, 16)
            sp.dma_start(smask, A["smask"]).then_inc(masks_in, 16)
            with sp.Fori(NB * H // KV_SLOTS, 2 * NB * H // KV_SLOTS) as i:
                cache_group(i)
            unit_pairs(UNITS[0] // 2 + 1, STEP0[IN_C] // (2 * UM) + 1)
            sp.wait_ge(step_done, STEP0[IN_C])
            sp.wait_ge(x_new, 2 * MT)
            for dst, name in ((qkvw, "qkvw"), (bmask, "bmask"), (sel, "sel"), (tri, "tri"), (stri, "stri"),
                              (selb, "selb"), (gsml, "gsml"), (wgate, "wgate")):
                sp.dma_start(dst, A[name]).then_inc(consts_c_in, 16)
            unit_pairs(STEP0[IN_C] // (2 * UM) + 1, STEP0[OUT_C] // (2 * UM) + 1)

            def c_load(i):
                h, r = divmod(i, ITEMS)
                s = i % C_SLOTS
                if r < 2 * NB:
                    if i >= C_SLOTS:
                        sp.wait_ge(c_out[s], 16 * (i // C_SLOTS))
                    src = A["C0"][r // 2, h].rearrange("(t p) e -> p t e", p=P)
                    sp.dma_start(cring[:, s], src[:, HD2 * (r % 2):HD2 * (r % 2) + HD2]).then_inc(c_in[s], 16)

            def c_store(i):
                h, r = divmod(i, ITEMS)
                s = i % C_SLOTS
                sp.wait_ge(c_new, i + 1)
                dst = O["Cs"][r // 2, h] if r < 2 * NB else O["Cp"][h]
                dst = dst.rearrange("(t p) e -> p t e", p=P)
                sp.dma_start(dst[:, HD2 * (r % 2):HD2 * (r % 2) + HD2], cring[:, s]).then_inc(c_out[s], 16)

            sp.wait_ge(xcc_ready, CT)
            for i in range(C_SLOTS - 1):
                c_load(i)
            for i in range(NH * ITEMS):
                c_store(i)
                if i + C_SLOTS - 1 < NH * ITEMS:
                    c_load(i + C_SLOTS - 1)
            sp.wait_ge(y1_ready, NH * ET)
            store_cols(sp, O["pack_c"], pack_c.rearrange("p m c -> p (m c)"))
            store_cols(sp, O["pack_n"], pack_n.rearrange("p m c -> p (m c)"))
            store_cols(sp, O["pack_m"], pack_m)
            unit_pairs(STEP0[OUT_C] // (2 * UM) + 1, NUNITS // 2)
            sp.wait_ge(x_new, 4 * MT)
            store_cols(sp, O["x"], x.rearrange("p m t -> p (m t)"))
            sp.wait_ge(v_stored, 16)
            for s in range(C_SLOTS):
                sp.wait_ge(c_out[s], 16 * len(range(s, NH * ITEMS, C_SLOTS)))
            sp.wait_ge(stored, 16 * 6)

        @block.scalar
        def _(act):
            order = Tally(act, a_order)

            def act_hi(l, it, base):
                u = l // UM
                g = base + 8 * it + l
                if not (isinstance(g, int) and g < UM):
                    act.wait_ge(step_done, g - UM + 1)
                if l % UM == 0:
                    act.wait_ge(raw_in[u % 2], 16 * (base // 8 + it + u // 2 + 1))
                act.activation(w_hi[:, l % UM], w_raw[:, u % 2, l % UM], ACT.Copy).then_inc(hi_ready, 1)

            def steps(ph, groups, evac):
                base = STEP0[ph]

                def body(it):
                    for l in range(8 * groups):
                        if not (isinstance(it, int) and base + 8 * groups * it + l + 2 >= NSTEPS):
                            act_hi(l + 2, groups * it, base)
                        evac(it, l)
                last = ph == DOWN1
                loop(act, UNITS[ph] // (2 * groups), body, peel_first=ph == IN_AB, peel_last=last)

            def stat_squares(s, get, ready):
                for m in range(MT):
                    ready(m)
                    if 8 * s + m >= 2:
                        act.wait_ge(sq_added, 8 * s + m - 1)
                    act.activation(sq[:, m % 2], get(m), ACT.Square).then_inc(sq_ready, 1)

            def stat_std(s):
                act.wait_ge(mean_ready, s + 1)
                if s >= 1:
                    act.wait_ge(rstd_ready, s)
                act.activation(std, ps[:, 7, 0:T], ACT.Sqrt, bias=tiny[:, 0:1], scale=1.0 / D).then_inc(std_ready, 1)

            def norm_in(s, n, gain, layer):
                for m in range(MT):
                    if n:
                        act.wait_ge(x_new, MT * (n - 1) + m + 1)
                    act.activation(xin_hi[:, m], x[:, m], ACT.Copy, scale=pcol(gain, layer * MT + m)
                                   ).then_inc(xin_hi_ready, 1)
                    if 8 * s + m >= 2:
                        act.wait_ge(sq_added, 8 * s + m - 1)
                    act.activation(sq[:, m % 2], x[:, m], ACT.Square).then_inc(sq_ready, 1)
                stat_std(s)

            def block_out(ph, s, per):
                groups = max(1, per // 2)

                def evac(it, l):
                    if l // UM % per != per - 1:
                        return
                    j = l % UM
                    m = it * UM + j
                    act.wait_ge(step_done, STEP0[ph] + 8 * groups * it + l + 1)
                    act.wait_ge(sq_added, 8 * s + it * UM + j - 1)
                    act.activation(sq[:, j % 2], ps[:, j, 0:T], ACT.Square).then_inc(sq_ready, 1)
                    act.activation(y[:, bass.ds(m, 1)].rearrange("p a t -> p (a t)"), ps[:, j, 0:T], ACT.Copy
                                   ).then_inc(out_taken, 1)
                steps(ph, groups, evac)
                stat_std(s)

            def mlp_up(ph, n):
                def evac(it, l):
                    m = 8 * it + l
                    act.wait_ge(out_taken, OUT0[ph] + m + 1)
                    if not (isinstance(it, int) and 32 * n + m < 2):
                        act.wait_ge(hid_ready, 32 * n + m - 1)
                    act.activation(relu2[:, l % 2], relu[:, l % 2], ACT.Square).then_inc(relu2_ready, 1)
                    act.wait_ge(relu2_ready, 32 * n + m + 1)
                    act.activation(hid_hi[:, bass.ds(m, 1)].rearrange("p a t -> p (a t)"), relu2[:, l % 2], ACT.Copy
                                   ).then_inc(hid_hi_ready, 1)
                base = STEP0[ph]

                def body(it):
                    for l in range(8):
                        act_hi(l + 2, it, base)
                        evac(it, l)
                loop(act, UNITS[ph] // 2, body, peel_first=True)

            act.wait_ge(consts_in, 16 * 6)
            act.wait_ge(tiny_ready, 2)
            act.wait_ge(x_in, 16)
            act_hi(0, 0, 0)
            act_hi(1, 0, 0)
            norm_in(0, 0, "g_mix_pre", 0)
            act.wait_ge(lam_v, 1)
            act.activation(lrut[:, 2], lrut[:, 1], ACT.Exp, scale=-1.0).then_inc(lam_a, 1)
            act.wait_ge(lam_v, 2)
            act.activation(lrut[:, 4], lrut[:, 3], ACT.Ln).then_inc(lam_a, 1)
            steps(IN_AB, 1, lambda it, l: None)

            act.wait_ge(lam_v, 3)
            for c in range(2):
                for g, dst in ((0, rp), (1, ip)):
                    act.wait_ge(gates_ready, 2 * c + g + 1)
                    for m in range(HM):
                        act.activation(dst[:, m, PAD:ROW], ps[:, 4 + m, 0:CONV], ACT.Sigmoid,
                                       bias=pcol(("lru_ba", "lru_bx")[g], c * HM + m)).then_inc(gates_taken, 1)
                act.wait_ge(gates_taken, HM * (2 * c + 2))
                for m in range(HM):
                    order.mark(act.activation(tp[:, m, PAD:ROW], rp[:, m, PAD:ROW], ACT.Tanh,
                                              scale=lrut[:, 7, c * HM + m:c * HM + m + 1]))
                order.wait()
                for m in range(HM):
                    last = act.activation(rp[:, m, PAD:ROW], rp[:, m, PAD:ROW], ACT.Exp,
                                          scale=lrut[:, 6, c * HM + m:c * HM + m + 1])
                last.then_inc(th_ready, 1)
                act.wait_ge(b_arg, c + 1)
                act.activation(tp[:, :, PAD:ROW], tp[:, :, PAD:ROW], ACT.Sqrt, bias=tiny[:, 1:2]).then_inc(b_root, 1)
                act.wait_ge(scanned, c + 1)
                act.activation(gelu, ga[:, c * HM:c * HM + HM], ACT.Gelu_apprx_tanh).then_inc(gelu_ready, 1)
                act.wait_ge(ya_full, c + 1)
                act.activation(ya_hi[:, c * HM:c * HM + HM], gg, ACT.Copy).then_inc(ya_hi_ready, 1)

            act.wait_ge(ya_ready, 2)
            for r in range(6):
                tt, half = divmod(r, 2)
                n = P if tt < 2 else NS
                act.wait_ge(vt_ready, r + 1)
                act.activation(vtok[0:n, tt, 512 * half:512 * half + 512], ps[0:n, 4 + r % 4, :], ACT.Copy
                               ).then_inc(vt_taken, 1)

            for h in range(H):
                act.wait_ge(max_ready, h + 1)
                f = h % 2
                for i, (a, b) in enumerate(((0, P), (P, 3 * P))):
                    last = act.activation(pS[:, f, a:b], pS[:, f, a:b], ACT.Exp, bias=att[:, f, i:i + 1],
                                          accum_out=att[:, f, 2 + i:3 + i])
                last.then_inc(exp_ready, 1)
                act.wait_ge(pt_ready, h + 1)
                if h >= 2:
                    act.wait_ge(pv_ready, h - 1)
                act.activation(pTp[:, f], ps[:, 6, 0:3 * P], ACT.Copy).then_inc(pt_taken, 1)
                act.wait_ge(pv_ready, h + 1)
                act.activation(yb_hi[:, h, 0:SEQ], ps[:, 7, SEQ * f:SEQ * f + SEQ], ACT.Copy).then_inc(yb_hi_ready, 1)

            for f in range(2):
                act.wait_ge(smax_ready, f + 1)
                act.activation(sS, sS, ACT.Exp, bias=att[:, f, 4:5], accum_out=att[:, f, 5:6]).then_inc(sexp_ready, 1)
                if f == 0:
                    act.wait_ge(v_stored, 16)
                for i in range(2):
                    act.wait_ge(spt_ready, 2 * f + i + 1)
                    if i == 0:
                        act.activation(pT[:, 0:4, P * f:P * f + P], ps[:, 4, :].rearrange("p (k r) -> p k r", k=4),
                                       ACT.Copy).then_inc(spt_taken, 1)
                    else:
                        act.activation(pT[:, 4:7, P * f:P * f + P],
                                       ps[:, 5, 0:3 * P].rearrange("p (k r) -> p k r", k=3), ACT.Copy
                                       ).then_inc(spt_taken, 1)
                        act.activation(pT[0:NS, 7, P * f:P * f + P], ps[0:NS, 5, 3 * P:4 * P], ACT.Copy
                                       ).then_inc(spt_taken, 1)
            act.wait_ge(kv_free, 2 * NB * H)
            act.activation(yb_hi[:, :, SEQ:T], ps[:, 6, 0:H * NS].rearrange("p (h t) -> p h t", h=H), ACT.Copy
                           ).then_inc(yb_hi_ready, 1)

            block_out(OUT_AB, 1, 2)
            norm_in(2, 1, "g_ffn_pre", 0)
            mlp_up(UP0, 0)
            block_out(DOWN0, 3, 4)
            norm_in(4, 2, "g_mix_pre", 1)
            steps(IN_C, 1, lambda it, l: None)

            for m in range(CT):
                act.wait_ge(convc_ready, m + 1)
                c = convt[:, m % 4, 0:CONV]
                act.activation(xcc[:, m, 0:SEQ], c[:, 0:SEQ], ACT.Silu).then_inc(a_order, 1)
                act.activation(seqs(xcc[:, m, SEQ:T]),
                               convt[:, m % 4, SEQ:SEQ + NB * LONG].rearrange("p (b c) -> p b c", c=LONG)[:, :, PAD:LONG],
                               ACT.Silu).then_inc(xcc_ready, 1)
            order.n += CT
            act.activation(z, z, ACT.Silu).then_inc(z_ready, 1)
            act.wait_ge(g_ready, 1)
            act.wait_ge(gv, 1)
            for r, dst in ((0, gi), (32, gf)):
                bias = gsml[:, 0:1] if r == 0 else gsml[:, 1:2]
                order.mark(act.activation(dst[:, PAD:S0], ps[r:r + NH, 4, 0:SEQ], ACT.Identity))
                order.mark(act.activation(samples(dst, PAD, NT), seqs(ps[r:r + NH, 4, SEQ:T]), ACT.Identity))
            order.wait()
            order.mark(act.activation(gi[:, PAD:ROW], gi[:, PAD:ROW], ACT.Identity, bias=gsml[:, 0:1]))
            act.activation(gf[:, PAD:ROW], gf[:, PAD:ROW], ACT.Identity, bias=gsml[:, 1:2]).then_inc(gact, 1)
            act.wait_ge(gv, 2)
            order.after(act.activation(gt[:, PAD:ROW], gt[:, PAD:ROW], ACT.Exp, scale=-1.0))
            act.activation(gt[:, PAD:ROW], gt[:, PAD:ROW], ACT.Ln, bias=1.0).then_inc(gact, 1)
            act.wait_ge(gv, 3)
            act.activation(rows[:, R_EN:R_EN + T], rows[:, R_EN:R_EN + T], ACT.Exp)
            act.activation(rows[:, R_INTER:NROWS], rows[:, R_INTER:NROWS], ACT.Exp)
            act.activation(gw_c, gw_c, ACT.Exp).then_inc(gact, 1)
            act.wait_ge(gcol_ready, 1)
            act.activation(tokg[:, 0:2].rearrange("p a b -> p (a b)"), ps[:, 5, 0:2 * 2 * NH], ACT.Copy)
            act.activation(tokg[0:NS, 2], ps[0:NS, 5, 2 * 2 * NH:3 * 2 * NH], ACT.Copy).then_inc(gcol_taken, 1)

            for h in range(NH):
                act.wait_ge(q_psum, h + 1)
                act.activation(qf, ps[:, 0:4, 0:T], ACT.Copy).then_inc(q_taken, 1)
                act.wait_ge(k_psum, h + 1)
                act.activation(kf, ps[:, 4:8, 0:T], ACT.Copy, scale=DH ** -0.5).then_inc(k_taken, 1)
                for tt in range(3):
                    n = P if tt < 2 else NS
                    act.wait_ge(kt_psum, 3 * h + tt + 1)
                    act.activation(ktok[0:n, tt], ps[0:n, tt, :], ACT.Copy, scale=DH ** -0.5).then_inc(kt_taken, 1)
                for tt in range(3):
                    n = P if tt < 2 else NS
                    act.wait_ge(vt1_psum, 3 * h + tt + 1)
                    act.activation(vtk[0:n, tt], ps[0:n, 4 + tt, :], ACT.Copy).then_inc(vt1_taken, 1)
                act.wait_ge(bc_psum, h + 1)
                act.activation(bc[:, 0:512], ps[:, 0, :], ACT.Copy).then_inc(bc_taken, 1)
                act.activation(bc[:, 512:NROWS], ps[:, 1, 0:NROWS - 512], ACT.Copy).then_inc(bc_taken, 1)
                act.wait_ge(ew_arg, h + 1)
                act.activation(ew[:, 0:2 * P], ew[:, 0:2 * P], ACT.Exp, bias=tokg[:, 0, h:h + 1]).then_inc(ew_exp, 1)
                act.activation(ew[:, 2 * P:3 * P], ew[:, 2 * P:3 * P], ACT.Exp, bias=tokg[:, 1, h:h + 1]).then_inc(ew_exp, 1)
                act.activation(ew[0:NS, 3 * P:3 * P + NS], ew[0:NS, 3 * P:3 * P + NS], ACT.Exp,
                               bias=tokg[0:NS, 2, h:h + 1]).then_inc(ew_exp, 1)
                act.wait_ge(vt1_taken, 3 * h + 3)
                for tt in range(2):
                    act.activation(vw[:, tt], vtk[:, tt], ACT.Copy, scale=tokg[:, tt, NH + h:NH + h + 1]
                                   ).then_inc(vw_ready, 1)
                act.wait_ge(den_psum, h + 1)
                act.activation(ew[:, 0:T], ps[:, 3, 0:T], ACT.Abs).then_inc(den_abs, 1)
                for b in range(NB):
                    n = NB * h + b
                    if n >= 2:
                        act.wait_ge(c_mm, ITEMS * ((n - 2) // NB) + 2 * ((n - 2) % NB) + 2)
                    act.activation(vb[0:NS, b % 2], vtk[0:NS, 2], ACT.Copy, scale=wmask[:, h * NB + b:h * NB + b + 1]
                                   ).then_inc(vb_ready, 1)
                for e in range(ET):
                    act.wait_ge(h_ready, ET * h + e + 1)
                    act.activation(qf[:, e], hT[:, e], ACT.Square).then_inc(h_sq, 1)
                act.wait_ge(h_mean, h + 1)
                act.activation(ew[:, 0:T], ps[:, 2, 0:T], ACT.Sqrt, bias=tiny[:, 0:1], scale=1.0 / DH).then_inc(h_std, 1)
                for e in range(ET):
                    act.wait_ge(y1_full, ET * h + e + 1)
                    act.activation(y1_hi[:, ET * h + e], hT[:, e], ACT.Copy).then_inc(y1_hi_ready, 1)

            for s in range(C_SLOTS):
                act.wait_ge(c_out[s], 16 * len(range(s, NH * ITEMS, C_SLOTS)))
            block_out(OUT_C, 5, 2)
            norm_in(6, 3, "g_ffn_pre", 1)
            mlp_up(UP1, 1)
            block_out(DOWN1, 7, 4)

        @block.vector
        def _(dve):
            order = Tally(dve, v_order)

            def dve_lo(l, it, base):
                u = l // UM
                dve.wait_ge(hi_ready, base + 8 * it + l + 1)
                dve.tensor_tensor(w_lo[:, l % UM], w_raw[:, u % 2, l % UM], w_hi[:, l % UM], ALU.subtract
                                  ).then_inc(lo_ready, 1)

            def steps(ph, groups, evac, peel_first=False):
                base = STEP0[ph]

                def body(it):
                    for l in range(8 * groups):
                        if not (isinstance(it, int) and base + 8 * groups * it + l + 2 >= NSTEPS):
                            dve_lo(l + 2, groups * it, base)
                        evac(it, l)
                loop(dve, UNITS[ph] // (2 * groups), body, peel_first=peel_first, peel_last=ph == DOWN1)

            def scaled_out(ph, dst):
                def evac(it, l):
                    m = 8 * it + l
                    dve.wait_ge(step_done, STEP0[ph] + m + 1)
                    dst(it, l, m)
                return evac

            def stat_rstd(s):
                dve.wait_ge(std_ready, s + 1)
                dve.reciprocal(rstd, std).then_inc(rstd_ready, 1)
                dve.wait_ge(rstd_ready, s + 1)

            def norm_in(s, n, gain, layer, new=None):
                def low(m):
                    dve.wait_ge(xin_hi_ready, MT * n + m + 1)
                    dve.scalar_tensor_tensor(xin_lo[:, m], x[:, m], pcol(gain, layer * MT + m), xin_hi[:, m],
                                             ALU.mult, ALU.subtract).then_inc(xin_ready, 1)
                for m in range(MT):
                    if new:
                        new(m)
                        if m:
                            low(m - 1)
                    else:
                        low(m)
                if new:
                    low(MT - 1)
                stat_rstd(s)

            def residual(s, gain, layer):
                stat_rstd(s)
                order.after(dve.tensor_tensor(y, y, rstd.unsqueeze(1).to_broadcast([P, MT, T]), ALU.mult))

                def new(m):
                    dve.scalar_tensor_tensor(x[:, m], y[:, m], pcol(gain, layer * MT + m), x[:, m], ALU.mult, ALU.add
                                             ).then_inc(x_new, 1)
                    dve.wait_ge(x_new, 8 * ((s - 1) // 2) + m + 1)
                return new

            def mlp_up(ph, n):
                def evac(it, l):
                    m = 8 * it + l
                    dve.wait_ge(step_done, STEP0[ph] + m + 1)
                    if not (isinstance(it, int) and 32 * n + m < 2):
                        dve.wait_ge(relu2_ready, 32 * n + m - 1)
                    dve.scalar_tensor_tensor(relu[:, l % 2], ps[:, l % UM, 0:T], 0.0, rstd, ALU.max, ALU.mult
                                             ).then_inc(out_taken, 1)
                steps(ph, 1, evac, peel_first=True)

            dve.memset(tiny[:, 0:1], EPS).then_inc(tiny_ready, 1)
            dve.memset(tiny[:, 1:2], 1e-30).then_inc(tiny_ready, 1)
            dve.wait_ge(consts_in, 16 * 6)
            dve.wait_ge(x_in, 16)
            dve_lo(0, 0, 0)
            dve_lo(1, 0, 0)
            lam = par[:, AT["lru_lambda"]:AT["lru_lambda"] + MT]
            order.after(dve.tensor_scalar(lrut[:, 0], lam, -1.0, None, ALU.mult))
            dve.tensor_tensor(lrut[:, 1], lrut[:, 0], lam, ALU.max).then_inc(lam_v, 1)
            norm_in(0, 0, "g_mix_pre", 0)
            dve.wait_ge(lam_a, 1)
            dve.tensor_scalar(lrut[:, 3], lrut[:, 2], 1.0, None, ALU.add).then_inc(lam_v, 1)
            dve.wait_ge(lam_a, 2)
            dve.wait_ge(lam_v, 2)
            order.after(dve.tensor_scalar(lrut[:, 3], lrut[:, 3], -1.0, None, ALU.add))
            order.after(dve.tensor_scalar(lrut[:, 5], lrut[:, 3], 0.0, None, ALU.is_equal))
            order.after(dve.tensor_tensor(lrut[:, 3], lrut[:, 3], lrut[:, 5], ALU.add))
            order.after(dve.reciprocal(lrut[:, 3], lrut[:, 3]))
            order.after(dve.tensor_tensor(lrut[:, 4], lrut[:, 4], lrut[:, 3], ALU.mult))
            order.after(dve.tensor_tensor(lrut[:, 4], lrut[:, 4], lrut[:, 5], ALU.add))
            order.after(dve.tensor_tensor(lrut[:, 4], lrut[:, 4], lrut[:, 2], ALU.mult))
            order.after(dve.scalar_tensor_tensor(lrut[:, 4], lrut[:, 0], 0.0, lrut[:, 4], ALU.max, ALU.add))
            order.after(dve.tensor_scalar(lrut[:, 6], lrut[:, 4], -LRU_C, None, ALU.mult))
            dve.tensor_scalar(lrut[:, 7], lrut[:, 4], LRU_C, None, ALU.mult).then_inc(lam_v, 1)


            def dst_ab(it, l, m):
                src = ps[:, l % UM, 0:T]
                if isinstance(it, int):
                    dve.tensor_tensor(xa[:, l, PAD:S0], src[:, 0:SEQ], rstd[:, 0:SEQ], ALU.mult)
                    dve.tensor_tensor(samples(xa[:, l], PAD, NT), seqs(src[:, SEQ:T]), seqs(rstd[:, SEQ:T]), ALU.mult
                                      ).then_inc(out_taken, 1)
                else:
                    dve.tensor_tensor(gaqkv[:, bass.ds(m - 8, 1)].rearrange("p a t -> p (a t)"), src, rstd, ALU.mult
                                      ).then_inc(out_taken, 1)

            dve.wait_ge(pads_ready, 2)
            steps(IN_AB, 1, scaled_out(IN_AB, dst_ab), peel_first=True)

            cos4 = cosr.unsqueeze(1).to_broadcast([ROT, 4, T])
            sin4 = sinr.unsqueeze(1).to_broadcast([ROT, 4, T])
            dve.wait_ge(out_taken, OUT0[OUT_AB])
            for r in range(4):
                w = (q, k)[r // 2][0:ROT, 4 * (r % 2):4 * (r % 2) + 4]
                dve.wait_ge(rot_ready, r + 1)
                dve.tensor_tensor(rot[0:ROT], ps[0:ROT, 4:8, 0:T], sin4, ALU.mult).then_inc(rot_taken, 1)
                order.after(dve.tensor_tensor(w, w, cos4, ALU.mult))
                dve.wait_ge(rot_taken, r + 1)
                dve.tensor_tensor(w, w, rot[0:ROT], ALU.add).then_inc(rope_done, 1)
                dve.wait_ge(rope_done, r + 1)

            order.mark(dve.tensor_copy(pack_a[:, :, 0:PAD], xa[:, :, SEQ:SEQ + PAD]))
            order.mark(dve.tensor_copy(pack_a[:, :, CW:].rearrange("p m (b c) -> p m b c", c=CW)[:, :, :, 0:PAD],
                                       samples(xa, NT, PAD)))
            for c in range(2):
                for j in reversed(range(CW)):
                    for m in range(HM):
                        src = xa[:, c * HM + m, j:j + CONV]
                        dst = xc[:, m, PAD:ROW]
                        wj = pcol("conv_a_w", j * MT + c * HM + m)
                        if j == CW - 1:
                            ins = dve.tensor_scalar(dst, src, wj, pcol("conv_a_b", c * HM + m), ALU.mult, ALU.add)
                        else:
                            ins = dve.scalar_tensor_tensor(dst, src, wj, dst, ALU.mult, ALU.add)
                        if j:
                            order.mark(ins)
                        else:
                            ins.then_inc(conv_ready, 1)
                    order.wait()
                dve.wait_ge(th_ready, c + 1)
                order.after(dve.tensor_scalar(hp[:, :, PAD:ROW], tp[:, :, PAD:ROW], 1.0, None, ALU.add))
                order.after(dve.reciprocal(hp[:, :, PAD:ROW], hp[:, :, PAD:ROW]))
                dve.scalar_tensor_tensor(tp[:, :, PAD:ROW], tp[:, :, PAD:ROW], 2.0, hp[:, :, PAD:ROW],
                                         ALU.mult, ALU.mult).then_inc(b_arg, 1)
                order.after(dve.tensor_tensor(ip[:, :, PAD:ROW], ip[:, :, PAD:ROW], xc[:, :, PAD:ROW], ALU.mult))
                dve.wait_ge(b_root, c + 1)
                order.after(dve.tensor_tensor(ip[:, :, PAD:ROW], ip[:, :, PAD:ROW], tp[:, :, PAD:ROW], ALU.mult))
                h0 = par[:, AT["h0"] + c * HM * NB:AT["h0"] + (c + 1) * HM * NB].rearrange("p (m b) -> p m b", b=NB)
                order.mark(dve.memset(rp[:, :, PAD - 1:PAD], 0.0))
                order.mark(dve.memset(ip[:, :, PAD - 1:PAD], 0.0))
                order.mark(dve.memset(samples(rp, PAD - 1, 1), 0.0))
                order.after(dve.tensor_copy(samples(ip, PAD - 1, 1)[:, :, :, 0], h0))
                for m in range(HM):
                    order.mark(dve.tensor_tensor_scan(hp[:, m, PAD - 1:ROW], rp[:, m, PAD - 1:ROW],
                                                      ip[:, m, PAD - 1:ROW], 0.0, ALU.mult, ALU.add))
                order.wait()
                order.mark(dve.tensor_copy(pack_a[:, c * HM:c * HM + HM, PAD], hp[:, :, S0 - 1]))
                dve.tensor_copy(pack_a[:, c * HM:c * HM + HM, CW:].rearrange("p m (b c) -> p m b c", c=CW)[:, :, :, PAD],
                                samples(hp, LONG - 1, 1)[:, :, :, 0]).then_inc(scanned, 1)
                dve.wait_ge(gelu_ready, c + 1)
                order.mark(dve.tensor_tensor(gg[:, :, 0:SEQ], hp[:, :, PAD:S0], gelu[:, :, 0:SEQ], ALU.mult))
                dve.tensor_tensor(gg[:, :, SEQ:T].rearrange("p m (b t) -> p m b t", t=NT), samples(hp, PAD, NT),
                                  gelu[:, :, SEQ:T].rearrange("p m (b t) -> p m b t", t=NT), ALU.mult
                                  ).then_inc(ya_full, 1)
                dve.wait_ge(ya_hi_ready, c + 1)
                dve.tensor_tensor(ya_lo[:, c * HM:c * HM + HM], gg, ya_hi[:, c * HM:c * HM + HM], ALU.subtract
                                  ).then_inc(ya_ready, 1)

            dve.wait_ge(masks_in, 32)

            def prompt_softmax(h):
                f = h % 2
                dve.wait_ge(s_ready, h + 1)
                if h >= 2:
                    dve.wait_ge(pt_ready, h - 1)
                dve.scalar_tensor_tensor(pS[:, f], ps[:, 4 + f, 0:3 * P], HD ** -0.5, amask, ALU.mult, ALU.add
                                         ).then_inc(s_taken, 1)
                dve.wait_ge(s_taken, h + 1)
                order.mark(dve.tensor_reduce(att[:, f, 0:1], pS[:, f, 0:P], axis=AX.X, op=ALU.max, negate=True))
                dve.tensor_reduce(att[:, f, 1:2], pS[:, f, P:3 * P], axis=AX.X, op=ALU.max, negate=True
                                  ).then_inc(max_ready, 1)

            def prompt_scale(h):
                f = h % 2
                dve.wait_ge(exp_ready, h + 1)
                order.after(dve.reciprocal(att[:, f, 2:4], att[:, f, 2:4]))
                dve.tensor_scalar(pS[:, f, 0:P], pS[:, f, 0:P], att[:, f, 2:3], None, ALU.mult)
                dve.tensor_scalar(pS[:, f, P:3 * P], pS[:, f, P:3 * P], att[:, f, 3:4], None, ALU.mult
                                  ).then_inc(p_ready, 1)

            def prompt_low(h):
                f = h % 2
                dve.wait_ge(yb_hi_ready, h + 1)
                dve.tensor_tensor(yb_lo[:, h, 0:SEQ], ps[:, 7, SEQ * f:SEQ * f + SEQ], yb_hi[:, h, 0:SEQ], ALU.subtract
                                  ).then_inc(yb_ready, 1)

            prompt_softmax(0)
            for h in range(H):
                prompt_scale(h)
                if h + 1 < H:
                    prompt_softmax(h + 1)
                if h:
                    prompt_low(h - 1)
            prompt_low(H - 1)

            for f in range(2):
                dve.wait_ge(kv_free, HALF_B * H * (f + 1))
                if f:
                    dve.wait_ge(spt_ready, 2)
                own = smask[:, NK + NS * f:NK + NS * f + NS]
                dve.scalar_tensor_tensor(sS[:, 0:NK // 2], ps[:, 2 * f, 0:NK // 2], HD ** -0.5, smask[:, 0:NK // 2],
                                         ALU.mult, ALU.add).then_inc(ss_taken, 1)
                dve.scalar_tensor_tensor(sS[:, NK // 2:NK], ps[:, 2 * f + 1, 0:NK // 2], HD ** -0.5,
                                         smask[:, NK // 2:NK], ALU.mult, ALU.add).then_inc(ss_taken, 1)
                dve.scalar_tensor_tensor(sS[:, NK:NKS], ps[:, 2 * f + 1, NK // 2:NK // 2 + NS], HD ** -0.5, own,
                                         ALU.mult, ALU.add).then_inc(ss_taken, 1)
                dve.wait_ge(ss_taken, 3 * f + 3)
                dve.tensor_reduce(att[:, f, 4:5], sS, axis=AX.X, op=ALU.max, negate=True).then_inc(smax_ready, 1)
                dve.wait_ge(sexp_ready, f + 1)
                order.after(dve.reciprocal(att[:, f, 6:7], att[:, f, 5:6]))
                dve.tensor_scalar(sS, sS, att[:, f, 6:7], None, ALU.mult).then_inc(sp_ready, 1)
            dve.wait_ge(yb_hi_ready, H + 1)
            dve.tensor_tensor(yb_lo[:, :, SEQ:T], ps[:, 6, 0:H * NS].rearrange("p (h t) -> p h t", h=H),
                              yb_hi[:, :, SEQ:T], ALU.subtract).then_inc(yb_ready, 1)

            steps(OUT_AB, 1, lambda it, l: None)
            norm_in(2, 1, "g_ffn_pre", 0, residual(1, "g_mix_post", 0))
            mlp_up(UP0, 0)
            steps(DOWN0, 2, lambda it, l: None)
            norm_in(4, 2, "g_mix_pre", 1, residual(3, "g_ffn_post", 0))

            def dst_c(it, l, m):
                src = ps[:, l % UM, 0:T]
                if isinstance(it, int):
                    dve.tensor_tensor(xm[:, m, PAD:S0], src[:, 0:SEQ], rstd[:, 0:SEQ], ALU.mult)
                    dve.tensor_tensor(samples(xm[:, m], PAD, NT), seqs(src[:, SEQ:T]), seqs(rstd[:, SEQ:T]), ALU.mult)
                    dve.tensor_tensor(xms[:, m], src[:, SEQ:T], rstd[:, SEQ:T], ALU.mult).then_inc(out_taken, 1)
                else:
                    dve.tensor_tensor(z[:, bass.ds(m - CT, 1)].rearrange("p a t -> p (a t)"), src, rstd, ALU.mult
                                      ).then_inc(out_taken, 1)

            dve.wait_ge(xm_pads, 2)
            base = STEP0[IN_C]

            def body_c(it):
                for l in range(8):
                    dve_lo(l + 2, it, base)
                    m = 8 * it + l
                    dve.wait_ge(step_done, base + m + 1)
                    dst_c(it, l, m)
            body_c(0)
            body_c(1)
            with dve.Fori(2, UNITS[IN_C] // 2) as it:
                body_c(it)

            dve.wait_ge(fold_zero, 1)
            dve.wait_ge(bdT_used, 1)
            for c0 in (0, 32):
                dve.tensor_copy(fold[:, :, c0:c0 + NH], ps[:, 5, 0:2 * CT * 8].rearrange("p (m g) -> p m g", g=8)
                                [:, :, NH * (c0 // 32):NH * (c0 // 32) + NH]).then_inc(fold_ready, 1)
            dve.wait_ge(out_taken, OUT0[OUT_C])
            for c in range(CT // 4):
                for j in reversed(range(CW)):
                    for i in range(4):
                        m = 4 * c + i
                        src = xm[:, m, j:j + CONV]
                        dst = convt[:, i, 0:CONV]
                        wj = pcol("conv_c_w", j * CT + m)
                        if j == CW - 1:
                            if c:
                                dve.wait_ge(xcc_ready, m - 3)
                            ins = dve.tensor_scalar(dst, src, wj, pcol("conv_c_b", m), ALU.mult, ALU.add)
                        else:
                            ins = dve.scalar_tensor_tensor(dst, src, wj, dst, ALU.mult, ALU.add)
                        if j:
                            order.mark(ins)
                        else:
                            ins.then_inc(convc_ready, 1)
                    if j:
                        order.wait()
            order.mark(dve.tensor_copy(pack_c[:, :, 0:PAD], xm[:, :, SEQ:SEQ + PAD]))
            order.mark(dve.tensor_copy(pack_c[:, :, PAD:].rearrange("p m (b c) -> p m b c", c=PAD), samples(xm, NT, PAD)))

            dve.wait_ge(xcc_ready, CT)
            order.mark(dve.memset(gi, 0.0))
            order.mark(dve.memset(gb, 0.0))
            dve.memset(gf, 0.0).then_inc(gv, 1)
            m0 = gsml[:, 2:2 + NB]
            dve.wait_ge(gact, 1)
            dve.scalar_tensor_tensor(gt[:, PAD:ROW], gf[:, PAD:ROW], -1.0, gf[:, PAD:ROW], ALU.mult, ALU.max
                                     ).then_inc(gv, 1)
            dve.wait_ge(gact, 2)
            order.after(dve.scalar_tensor_tensor(gf[:, PAD:ROW], gf[:, PAD:ROW], 0.0, gt[:, PAD:ROW],
                                                 ALU.min, ALU.subtract))
            keep = ghist[:, 0:ROW]
            push = ghist[:, ROW:2 * ROW]
            order.mark(dve.memset(keep, 1.0))
            order.after(dve.memset(push, 0.0))
            order.mark(dve.memset(keep[:, PAD:PAD + 1], 0.0))
            order.mark(dve.memset(samples(keep, PAD, 1), 0.0))
            order.mark(dve.memset(push[:, PAD - 1:PAD], NEG))
            order.after(dve.memset(samples(push, PAD - 1, 1), NEG))
            order.after(dve.tensor_tensor_scan(gb[:, PAD:ROW], keep[:, PAD:ROW], gf[:, PAD:ROW], 0.0, ALU.mult, ALU.add))
            order.after(dve.tensor_tensor(gi[:, PAD:ROW], gi[:, PAD:ROW], gb[:, PAD:ROW], ALU.subtract))
            order.after(dve.tensor_copy(samples(gi, PAD - 1, 1)[:, :, 0], m0))
            order.after(dve.tensor_tensor_scan(gt[:, PAD - 1:ROW], push[:, PAD - 1:ROW], gi[:, PAD - 1:ROW], 0.0,
                                               ALU.add, ALU.max))
            gM, g = gt, gi
            order.mark(dve.tensor_scalar(rows[:, R_NEGM:R_NEGM + SEQ], gM[:, PAD:S0], -1.0, None, ALU.mult))
            order.mark(dve.tensor_scalar(seqs(rows[:, R_NEGM + SEQ:R_NEGM + T]), samples(gM, PAD, NT), -1.0, None, ALU.mult))
            order.mark(dve.tensor_copy(gg_c[:, 0:SEQ], g[:, PAD:S0]))
            order.mark(dve.tensor_copy(seqs(gg_c[:, SEQ:T]), samples(g, PAD, NT)))
            order.wait()
            order.mark(dve.tensor_tensor(rows[:, R_EN:R_EN + SEQ], rows[:, R_NEGM:R_NEGM + SEQ], gb[:, PAD:S0], ALU.subtract))
            order.mark(dve.tensor_tensor(seqs(rows[:, R_EN + SEQ:R_EN + T]), seqs(rows[:, R_NEGM + SEQ:R_NEGM + T]),
                                         samples(gb, PAD, NT), ALU.subtract))
            m0_t = m0.unsqueeze(2).to_broadcast([NH, NB, NT])
            order.mark(dve.tensor_tensor(seqs(rows[:, R_INTER:R_INTER + NS]), m0_t, samples(gM, PAD, NT), ALU.subtract))
            order.mark(dve.tensor_tensor(rows[:, R_DECAY:R_DECAY + NB], m0, samples(gM, LONG - 1, 1)[:, :, 0], ALU.subtract))
            order.mark(dve.tensor_scalar(gw_c[:, 0:SEQ], gg_c[:, 0:SEQ], gM[:, S0 - 1:S0], None, ALU.subtract))
            order.mark(dve.tensor_tensor(seqs(gw_c[:, SEQ:T]), seqs(gg_c[:, SEQ:T]),
                                         samples(gM, LONG - 1, 1).to_broadcast([NH, NB, NT]), ALU.subtract))
            order.mark(dve.tensor_tensor(pack_m[:, 0:1], gM[:, S0 - 1:S0], gb[:, S0 - 1:S0], ALU.add))
            dve.tensor_tensor(pack_m[:, 1:1 + NB], samples(gM, LONG - 1, 1)[:, :, 0],
                              samples(gb, LONG - 1, 1)[:, :, 0], ALU.add).then_inc(gv, 1)
            dve.wait_ge(gcol_taken, 1)
            for h in range(NH):
                last = dve.tensor_scalar(wmask[:, h * NB:(h + 1) * NB], selb, tokg[0:NS, 2, NH + h:NH + h + 1], None, ALU.mult)
            last.then_inc(wmask_ready, 1)

            dve.wait_ge(z_ready, 1)
            for h in range(NH):
                dve.wait_ge(bc_taken, 2 * h + 2)
                negm = bc[:, R_NEGM:R_NEGM + T]
                order.mark(dve.tensor_tensor(ew[:, 0:P], negm[:, 0:P], tri, ALU.add))
                order.mark(dve.tensor_copy(ew[:, P:2 * P], negm[:, P:2 * P]))
                order.mark(dve.tensor_tensor(ew[:, 2 * P:3 * P], negm[:, P:2 * P], tri, ALU.add))
                dve.tensor_tensor(ew[0:NS, 3 * P:3 * P + NS], negm[0:NS, SEQ:T], stri, ALU.add).then_inc(ew_arg, 1)
                inter = bc[:, R_INTER:R_INTER + NS].unsqueeze(1).to_broadcast([P, ET, NS])
                order.after(dve.tensor_tensor(qs, qf[:, :, SEQ:T], inter, ALU.mult))
                n0 = par[:, AT["n0"] + h * ET * NB:AT["n0"] + (h + 1) * ET * NB]
                n0_t = n0.rearrange("p (e b) -> p e b", b=NB).rearrange("p e b -> p (e b)").unsqueeze(2).to_broadcast([P, ET * NB, NT])
                dve.tensor_tensor(qn.rearrange("p e (b t) -> p (e b) t", t=NT), qs.rearrange("p e (b t) -> p (e b) t", t=NT),
                                  n0_t, ALU.mult).then_inc(qs_ready, 1)
                dve.wait_ge(ew_exp, 3 * h + 3)
                dve.wait_ge(s1_psum, h + 1)
                order.mark(dve.tensor_tensor(ew[:, 0:3 * P], ew[:, 0:3 * P], ps[:, 2, 0:3 * P], ALU.mult))
                dve.tensor_tensor(ew[0:NS, 3 * P:3 * P + NS], ew[0:NS, 3 * P:3 * P + NS],
                                  ps[0:NS, 2, 3 * P:3 * P + NS], ALU.mult).then_inc(ew_ready, 1)
                decay = bc[:, R_DECAY:R_DECAY + NB]
                dve.wait_ge(n_psum, h + 1)
                pn = ps[:, 2, 0:ET * (1 + NB)].rearrange("p (e b) -> p e b", b=1 + NB)
                kn = pack_n[:, h * ET:(h + 1) * ET]
                order.mark(dve.tensor_copy(kn[:, :, 0:1], pn[:, :, 0:1]))
                order.after(dve.tensor_tensor(kn[:, :, 1:], n0.rearrange("p (e b) -> p e b", b=NB),
                                              decay.unsqueeze(1).to_broadcast([P, ET, NB]), ALU.mult))
                dve.tensor_tensor(kn[:, :, 1:], kn[:, :, 1:], pn[:, :, 1:], ALU.add).then_inc(n_taken, 1)
                for r in range(ITEMS):
                    i = ITEMS * h + r
                    s = i % C_SLOTS
                    dve.wait_ge(c_mm, i + 1)
                    if r < 2 * NB:
                        dve.wait_ge(c_in[s], 16 * sum(1 for j in range(i + 1) if j % C_SLOTS == s and j % ITEMS < 2 * NB))
                        for e in range(HD2):
                            last = dve.scalar_tensor_tensor(cring[:, s, e], cring[:, s, e], decay[:, r // 2:r // 2 + 1],
                                                            ps[:, 2 * (r % 2) + e, :], ALU.mult, ALU.add)
                    else:
                        if i >= C_SLOTS:
                            dve.wait_ge(c_out[s], 16 * (i // C_SLOTS))
                        for e in range(HD2):
                            last = dve.tensor_copy(cring[:, s, e], ps[:, 2 * (r % 2) + e, :])
                    last.then_inc(c_new, 1)
                dve.wait_ge(den_abs, h + 1)
                order.after(dve.tensor_tensor(ew[:, 0:T], ew[:, 0:T], bc[:, R_EN:R_EN + T], ALU.max))
                order.after(dve.reciprocal(ew[:, 0:T], ew[:, 0:T]))
                dve.wait_ge(c_mm, ITEMS * (h + 1))
                for e in range(ET):
                    dve.tensor_tensor(hT[:, e], ps[:, 4 + e, 0:T], ew[:, 0:T], ALU.mult).then_inc(h_ready, 1)
                dve.wait_ge(h_std, h + 1)
                order.after(dve.reciprocal(ew[:, 0:T], ew[:, 0:T]))
                for e in range(ET):
                    m = ET * h + e
                    order.mark(dve.scalar_tensor_tensor(hT[:, e], hT[:, e], pcol("norm_w", m), ew[:, 0:T], ALU.mult, ALU.mult))
                order.wait()
                for e in range(ET):
                    m = ET * h + e
                    order.mark(dve.scalar_tensor_tensor(hT[:, e], xcc[:, m], pcol("skip", m), hT[:, e], ALU.mult, ALU.add))
                order.wait()
                for e in range(ET):
                    m = ET * h + e
                    dve.tensor_tensor(hT[:, e], hT[:, e], z[:, m], ALU.mult).then_inc(y1_full, 1)
                for e in range(ET):
                    m = ET * h + e
                    dve.wait_ge(y1_hi_ready, m + 1)
                    dve.tensor_tensor(y1_lo[:, m], hT[:, e], y1_hi[:, m], ALU.subtract).then_inc(y1_ready, 1)

            steps(OUT_C, 1, lambda it, l: None)
            norm_in(6, 3, "g_ffn_pre", 1, residual(5, "g_mix_post", 1))
            mlp_up(UP1, 1)
            steps(DOWN1, 2, lambda it, l: None)
            last_new = residual(7, "g_ffn_post", 1)
            for m in range(MT):
                last_new(m)

        @block.gpsimd
        def _(pool):
            order = Tally(pool, p_order)

            def square_sums(s):
                for m in range(MT):
                    if m == 0 and s:
                        pool.wait_ge(mean_ready, s)
                    pool.wait_ge(sq_ready, 8 * s + m + 1)
                    if m == 0:
                        pool.tensor_copy(sqsum, sq[:, 0]).then_inc(sq_added, 1)
                    else:
                        pool.wait_ge(sq_added, 8 * s + m)
                        pool.tensor_tensor(sqsum, sqsum, sq[:, m % 2], ALU.add).then_inc(sq_added, 1)

            def hidden_low(n):
                def body(it):
                    for l in range(2):
                        m = 2 * it + l
                        pool.wait_ge(hid_hi_ready, 32 * n + m + 1)
                        pool.tensor_tensor(hid_lo[:, bass.ds(m, 1)].rearrange("p a t -> p (a t)"), relu2[:, l],
                                           hid_hi[:, bass.ds(m, 1)].rearrange("p a t -> p (a t)"), ALU.subtract
                                           ).then_inc(hid_ready, 1)
                with pool.Fori(0, 16) as it:
                    body(it)

            pool.memset(lruw, 0.0).then_inc(lruw_zero, 1)
            pool.wait_ge(consts_in, 16 * 6)
            order.mark(pool.memset(xa[:, :, 0:PAD], 0.0))
            order.mark(pool.memset(qz, 0.0))
            order.wait()
            pool.tensor_copy(samples(xa, 0, PAD), par[:, AT["conv_a0"]:AT["conv_a0"] + MT * NB * PAD].rearrange(
                "p (m b c) -> p m b c", b=NB, c=PAD)).then_inc(pads_ready, 2)
            square_sums(0)
            pool.wait_ge(rope_done, 2)
            for b in range(NB):
                if b >= 2:
                    pool.wait_ge(kv_free, H * (b - 1))
                pool.tensor_copy(qz_diag[:, b % 2], q[:, :, SEQ + NT * b:SEQ + NT * b + NT]).then_inc(qz_ready, 1)
            square_sums(1)
            square_sums(2)
            hidden_low(0)
            square_sums(3)
            pool.wait_ge(step_done, STEP0[IN_C])
            order.mark(pool.memset(xm[:, :, 0:PAD], 0.0))
            order.wait()
            pool.tensor_copy(samples(xm, 0, PAD), par[:, AT["conv_c0"]:AT["conv_c0"] + CT * NB * PAD].rearrange(
                "p (m b c) -> p m b c", b=NB, c=PAD)).then_inc(xm_pads, 2)
            square_sums(4)
            pool.wait_ge(consts_c_in, 16 * 8)
            pool.memset(fold, 0.0).then_inc(fold_zero, 1)

            def diagonal(dst, which, m):
                return pool.tensor_tensor(dst.rearrange("p (i o) -> p i o", o=QB),
                                          qkvw[:, which, m:m + 1].to_broadcast([P, P // QB, QB]),
                                          bmask.rearrange("p (i o) -> p i o", o=QB), ALU.mult)

            for m in range(CT):
                for i in range(3):
                    diagonal(bdT[:, 3 * m + i], 3 + i, m).then_inc(bdT_ready, 1)
            pool.wait_ge(gcol_taken, 1)
            for h in range(NH):
                if h:
                    pool.wait_ge(vt1_psum, 3 * h)
                for i in range(3):
                    for e in range(ET):
                        ins = diagonal(bd[:, ET * i + e], i, ET * h + e)
                    ins.then_inc(bd_ready, 1)
            square_sums(5)
            square_sums(6)
            hidden_low(1)
            square_sums(7)

        @block.tensor
        def _(pe):
            def step(ph, g, l, parts, start, stop, first=None, o=None):
                pe.wait_ge(lo_ready, g + 1)
                if start and o is not None:
                    pe.wait_ge(out_taken, o - UM + 1)
                j = l % UM
                for kk in range(UK):
                    if first:
                        first(kk)
                    hi, lo = parts(kk)
                    ws = slice(kk * P, kk * P + P)
                    pe.matmul(ps[:, j, 0:T], w_hi[:, j, ws], hi, start=start and kk == 0, stop=False)
                    pe.matmul(ps[:, j, 0:T], w_hi[:, j, ws], lo, start=False, stop=False)
                    last = pe.matmul(ps[:, j, 0:T], w_lo[:, j, ws], hi, start=False, stop=stop and kk == UK - 1)
                last.then_inc(step_done, 1)

            def steps(ph, per, parts, after_first=None, first=None, peel=True, taken0=None):
                groups = max(1, per // 2)

                def body(it):
                    for l in range(8 * groups):
                        u = l // UM
                        kg = u % per
                        o = None
                        if kg == 0:
                            n = (8 // per * groups) * it + UM * (u // per) + l % UM
                            o = OUT0[ph] + n
                            if isinstance(o, int) and o < UM:
                                o = None
                        here = isinstance(it, int) and it == 0
                        step(ph, STEP0[ph] + 8 * groups * it + l, l, lambda kk: parts(UK * kg + kk),
                             kg == 0, kg == per - 1, first if here and l == 0 else None, o)
                        if here and l == 0 and after_first:
                            after_first()
                loop(pe, UNITS[ph] // (2 * groups), body, peel_first=peel)

            def mean(s):
                pe.wait_ge(sq_added, 8 * s + 8)
                if s:
                    pe.wait_ge(std_ready, s)
                pe.matmul(ps[:, 7, 0:T], ones, sqsum, start=True, stop=True).then_inc(mean_ready, 1)

            def from_norm(ph, n, s):
                steps(ph, 1, lambda kk: (xin_hi[:, kk], xin_lo[:, kk]), after_first=lambda: mean(s),
                      first=lambda kk: pe.wait_ge(xin_ready, MT * n + kk + 1))

            pe.wait_ge(consts_in, 16 * 6)
            from_norm(IN_AB, 0, 0)

            pe.wait_ge(out_taken, OUT0[OUT_AB])
            pe.wait_ge(std_ready, 1)
            for r in range(4):
                if r:
                    pe.wait_ge(rot_taken, r)
                w = (q, k)[r // 2]
                for i in range(4):
                    last = pe.matmul(ps[0:ROT, 4 + i, 0:T], rotm, w[0:ROT, 4 * (r % 2) + i], start=True, stop=True)
                last.then_inc(rot_ready, 1)

            def lru_gates(c, g):
                pe.wait_ge(conv_ready, HM * (c + 1))
                if c or g:
                    pe.wait_ge(gates_taken, HM * (2 * c + g))
                for m in range(HM):
                    last = pe.matmul(ps[:, 4 + m, 0:CONV], lruw[:, g * MT + c * HM + m], xc[:, m, PAD:ROW],
                                     start=True, stop=True)
                last.then_inc(gates_ready, 1)

            def sample_scores(b):
                f, rows4 = divmod(b, HALF_B)
                part = slice(32 * rows4, 32 * rows4 + 32)
                pe.wait_ge(qz_ready, b + 1)
                for h in range(H):
                    i = b * H + h
                    s = i % KV_SLOTS
                    pe.wait_ge(kv_in[s], 16 * (i // KV_SLOTS + 1))
                    lhs = qz_of[:, b % 2, h]
                    for c in range(2):
                        pe.matmul(ps[part, 2 * f + c, 0:NK // 2], lhs, kv[:, s, c * NK // 2:(c + 1) * NK // 2],
                                  start=h == 0, stop=h == H - 1, skip_group_check=True)
                    pe.matmul(ps[part, 2 * f + 1, NK // 2:NK // 2 + NS], lhs, k[:, h, SEQ:T],
                              start=False, stop=h == H - 1, skip_group_check=True).then_inc(kv_free, 1)

            pe.wait_ge(lruw_in, 16 * 4)
            pe.wait_ge(rot_taken, 4)
            pe.wait_ge(rope_done, 4)
            for b in range(NB):
                sample_scores(b)
                if b < 2:
                    lru_gates(0, b)
                if b in (4, 5):
                    lru_gates(1, b - 4)

            pe.wait_ge(gates_taken, 4 * HM)
            for r in range(6):
                tt, half = divmod(r, 2)
                n = P if tt < 2 else NS
                if r >= 4:
                    pe.wait_ge(vt_taken, r - 3)
                for i in range(4):
                    last = pe.transpose(ps[0:n, 4 + r % 4, P * i:P * i + P], v[:, 4 * half + i, P * tt:P * tt + n], ident)
                last.then_inc(vt_ready, 1)

            pe.wait_ge(vt_taken, 6)

            def prompt_scores(h):
                f = h % 2
                if h >= 2:
                    pe.wait_ge(s_taken, h - 1)
                pe.matmul(ps[:, 4 + f, 0:P], q[:, h, 0:P], k[:, h, 0:P], start=True, stop=True)
                pe.matmul(ps[:, 4 + f, P:3 * P], q[:, h, P:SEQ], k[:, h, 0:SEQ], start=True, stop=True
                          ).then_inc(s_ready, 1)

            prompt_scores(0)
            for h in range(H):
                f = h % 2
                if h + 1 < H:
                    prompt_scores(h + 1)
                pe.wait_ge(p_ready, h + 1)
                if h:
                    pe.wait_ge(pt_taken, h)
                for i in range(3):
                    last = pe.transpose(ps[:, 6, P * i:P * i + P], pS[:, f, P * i:P * i + P], ident)
                last.then_inc(pt_ready, 1)
                pe.wait_ge(pt_taken, h + 1)
                if h:
                    pe.wait_ge(yb_ready, h)
                out = ps[:, 7, SEQ * f:SEQ * f + SEQ]
                hs = slice(HD * h, HD * h + HD)
                pe.matmul(out[:, 0:P], vtok[:, 0, hs], pTp[:, f, 0:P], start=True, stop=True)
                pe.matmul(out[:, P:SEQ], vtok[:, 0, hs], pTp[:, f, P:2 * P], start=True, stop=False)
                pe.matmul(out[:, P:SEQ], vtok[:, 1, hs], pTp[:, f, 2 * P:3 * P], start=False, stop=True
                          ).then_inc(pv_ready, 1)

            for f in range(2):
                pe.wait_ge(sp_ready, f + 1)
                if f:
                    pe.wait_ge(spt_taken, 3)
                for kt in range(KT + 1):
                    n = P if kt < KT else NS
                    last = pe.transpose(ps[0:n, 4 + kt // 4, P * (kt % 4):P * (kt % 4) + P], sS[:, P * kt:P * kt + n], ident)
                    if kt % 4 == 3:
                        last.then_inc(spt_ready, 1)
            pe.wait_ge(spt_taken, 6)
            with pe.Fori(0, NB) as b:
                for h in range(H):
                    s = h % KV_SLOTS
                    pe.wait_ge(kv_in[s], 16 * ((NB * H) // KV_SLOTS + H // KV_SLOTS * b + h // KV_SLOTS + 1))
                    out = ps[:, 6, bass.ds(b * NT + h * NS, NT)]
                    for kt in range(KT + 1):
                        n = P if kt < KT else NS
                        lhs = kv[:, s, P * kt:P * kt + P] if kt < KT else vtok[0:NS, 2, HD * h:HD * h + HD]
                        last = pe.matmul(out, lhs, pT[0:n, kt, bass.ds(b * 32 + h * NT, NT)],
                                         start=kt == 0, stop=kt == KT)
                    last.then_inc(kv_free, 1)

            def ab(kk):
                return (ya_hi[:, kk], ya_lo[:, kk]) if kk < MT else (yb_hi[:, kk - MT], yb_lo[:, kk - MT])

            pe.wait_ge(yb_ready, H + 1)
            pe.wait_ge(ya_ready, 2)
            steps(OUT_AB, 2, ab, peel=False)
            mean(1)
            from_norm(UP0, 1, 2)
            pe.wait_ge(hid_ready, 32)
            steps(DOWN0, 4, lambda kk: (hid_hi[:, kk], hid_lo[:, kk]), peel=False)
            mean(3)
            from_norm(IN_C, 2, 4)

            pe.wait_ge(consts_c_in, 16 * 8)
            pe.wait_ge(out_taken, OUT0[OUT_C])
            for m in range(CT):
                pe.wait_ge(bdT_ready, 3 * m + 3)
                for i in range(3):
                    c0 = 8 * m if i < 2 else 8 * (CT + m)
                    last = pe.matmul(ps[:, 5, c0:c0 + 8], bdT[:, 3 * m + i], wgate[:, i * CT + m],
                                     start=i != 1, stop=i >= 1)
            last.then_inc(bdT_used, 1)
            pe.wait_ge(fold_ready, 2)
            pe.wait_ge(xcc_ready, CT)
            g = ps[0:GH, 4, :]
            for m in range(CT):
                pe.matmul(g[:, 0:T], fold[:, m], xcc[:, m], start=m == 0, stop=False, skip_group_check=True)
                pe.matmul(g[:, 0:SEQ], fold[:, CT + m], xm[:, m, PAD:S0], start=False, stop=False, skip_group_check=True)
                last = pe.matmul(g[:, SEQ:T], fold[:, CT + m], xms[:, m], start=False, stop=m == CT - 1,
                                 skip_group_check=True)
            last.then_inc(g_ready, 1)
            pe.wait_ge(gact, 3)
            for tt in range(3):
                n = P if tt < 2 else NS
                for i, src in enumerate((gg_c, gw_c)):
                    last = pe.transpose(ps[0:n, 5, 8 * tt + NH * i:8 * tt + NH * i + NH], src[:, P * tt:P * tt + n],
                                        ident[0:NH, 0:NH])
            last.then_inc(gcol_ready, 1)

            pe.wait_ge(gcol_taken, 1)
            for h in range(NH):
                if h:
                    pe.wait_ge(c_new, ITEMS * h)
                    pe.wait_ge(h_ready, ET * h)
                    pe.wait_ge(h_std, h)
                    pe.wait_ge(y1_ready, ET * h)
                pe.wait_ge(bd_ready, 3 * h + 3)
                hx = [xcc[:, ET * h + e] for e in range(ET)]
                for e in range(ET):
                    last = pe.matmul(ps[:, e, 0:T], bd[:, e], hx[e], start=True, stop=True)
                last.then_inc(q_psum, 1)
                for e in range(ET):
                    last = pe.matmul(ps[:, 4 + e, 0:T], bd[:, ET + e], hx[e], start=True, stop=True)
                last.then_inc(k_psum, 1)
                pe.wait_ge(q_taken, h + 1)
                for tt in range(3):
                    n = P if tt < 2 else NS
                    for e in range(ET):
                        last = pe.matmul(ps[0:n, tt, P * e:P * e + P], hx[e][:, P * tt:P * tt + n], bd[:, ET + e],
                                         start=True, stop=True)
                    last.then_inc(kt_psum, 1)
                pe.wait_ge(k_taken, h + 1)
                for tt in range(3):
                    n = P if tt < 2 else NS
                    for e in range(ET):
                        m = ET * h + e
                        lhs = xm[:, m, PAD + P * tt:PAD + P * tt + P] if tt < 2 else xms[:, m]
                        last = pe.matmul(ps[0:n, 4 + tt, P * e:P * e + P], lhs, bd[:, 2 * ET + e], start=True, stop=True)
                    last.then_inc(vt1_psum, 1)
                pe.wait_ge(kt_taken, 3 * h + 3)
                hsel = sel[:, P * h:P * h + P]
                pe.matmul(ps[:, 0, :], hsel, rows[:, 0:512], start=True, stop=True)
                pe.matmul(ps[:, 1, 0:NROWS - 512], hsel, rows[:, 512:NROWS], start=True, stop=True).then_inc(bc_psum, 1)
                for lo, hi, ks, c0 in ((0, SEQ, 0, 0), (P, SEQ, P, 2 * P)):
                    for e in range(ET):
                        pe.matmul(ps[:, 2, c0:c0 + hi - lo], kf[:, e, ks:ks + P], qf[:, e, lo:hi],
                                  start=e == 0, stop=e == ET - 1)
                for e in range(ET):
                    last = pe.matmul(ps[0:NS, 2, 3 * P:3 * P + NS], kf[:, e, SEQ:T], qf[:, e, SEQ:T],
                                     start=e == 0, stop=e == ET - 1)
                last.then_inc(s1_psum, 1)
                pe.wait_ge(ew_ready, h + 1)
                pe.wait_ge(qs_ready, h + 1)
                pe.wait_ge(vt1_taken, 3 * h + 3)
                for e in range(ET + 1):
                    bank = 4 + e if e < ET else 3
                    for tt, (c0, c1, w) in enumerate(((0, SEQ, ew[:, 0:2 * P]), (P, SEQ, ew[:, 2 * P:3 * P]),
                                                      (SEQ, T, ew[0:NS, 3 * P:3 * P + NS]))):
                        n = P if tt < 2 else NS
                        lhs = vtk[0:n, tt, P * e:P * e + P] if e < ET else ones[0:n]
                        last = pe.matmul(ps[:, bank, c0:c1], lhs, w, start=tt == 0, stop=False, skip_group_check=True)
                for e in range(ET):
                    last = pe.matmul(ps[:, 3, SEQ:T], ones, qn[:, e], start=False, stop=e == ET - 1,
                                     skip_group_check=True)
                last.then_inc(den_psum, 1)
                pe.wait_ge(wmask_ready, 1)
                for e in range(ET):
                    c0 = (1 + NB) * e
                    es = slice(P * e, P * e + P)
                    for tt in range(2):
                        pe.matmul(ps[:, 2, c0:c0 + 1], ktok[:, tt, es], tokg[:, tt, NH + h:NH + h + 1],
                                  start=tt == 0, stop=tt == 1)
                    last = pe.matmul(ps[:, 2, c0 + 1:c0 + 1 + NB], ktok[0:NS, 2, es], wmask[:, h * NB:(h + 1) * NB],
                                     start=True, stop=True)
                last.then_inc(n_psum, 1)
                pe.wait_ge(bc_taken, 2 * h + 2)
                pe.wait_ge(vw_ready, 2 * h + 2)
                for r in range(ITEMS):
                    i = ITEMS * h + r
                    s = i % C_SLOTS
                    b, half = divmod(r, 2)
                    up = 2 * (r % 2)
                    if r < 2 * NB:
                        pe.wait_ge(c_in[s], 16 * sum(1 for j in range(i + 1) if j % C_SLOTS == s and j % ITEMS < 2 * NB))
                        for e in range(ET):
                            for d in range(HD2):
                                pe.matmul(ps[:, 4 + e, SEQ + NT * b:SEQ + NT * b + NT], cring[:, s, d, P * e:P * e + P],
                                          qs[:, HD2 * half + d, NT * b:NT * b + NT], start=False,
                                          stop=half == 1 and d == HD2 - 1, skip_group_check=True)
                        pe.wait_ge(vb_ready, NB * h + b + 1)
                    if r == 1:
                        pe.wait_ge(n_taken, h + 1)
                        pe.wait_ge(den_abs, h + 1)
                    if r >= 2:
                        pe.wait_ge(c_new, i - 1)
                    for d in range(HD2):
                        ds = slice(P * (HD2 * half + d), P * (HD2 * half + d) + P)
                        if r < 2 * NB:
                            last = pe.matmul(ps[:, up + d, :], ktok[0:NS, 2, ds], vb[0:NS, b % 2], start=True, stop=True)
                        else:
                            for tt in range(2):
                                last = pe.matmul(ps[:, up + d, :], ktok[:, tt, ds], vw[:, tt], start=tt == 0, stop=tt == 1)
                    last.then_inc(c_mm, 1)
                pe.wait_ge(c_new, ITEMS * (h + 1))
                for e in range(ET):
                    pe.wait_ge(h_sq, ET * h + e + 1)
                    last = pe.matmul(ps[:, 2, 0:T], ones, qf[:, e], start=e == 0, stop=e == ET - 1)
                last.then_inc(h_mean, 1)

            pe.wait_ge(y1_ready, CT)
            steps(OUT_C, 2, lambda kk: (y1_hi[:, kk], y1_lo[:, kk]), peel=False)
            mean(5)
            from_norm(UP1, 3, 6)
            pe.wait_ge(hid_ready, 64)
            steps(DOWN1, 4, lambda kk: (hid_hi[:, kk], hid_lo[:, kk]), peel=False)
            mean(7)


def constants():
    f = np.float32

    def held(delta):
        n = sum((delta >= 0) & (delta <= w) & (delta % d == 0) for w, d in DIL)
        return np.where(n > 0, np.log(np.maximum(n, 1)), NEG).astype(f)

    i = np.arange(P)[:, None]
    c = {"ident": np.eye(P, dtype=f), "ones": np.ones((P, P), f)}
    c["amask"] = np.concatenate([held(i - np.arange(P)), held(P + i - np.arange(2 * P))], 1)
    b4, t = i // 32, i % NT
    own = np.arange(NS)[None]
    parts = [held(PAST + t - np.array(KEYS)[None])]
    for f4 in (0, HALF_B):
        parts.append(np.where(own // NT == b4 + f4, held(t - own % NT), f(NEG)))
    c["smask"] = np.concatenate(parts, 1)
    pos = np.concatenate([np.arange(SEQ), np.tile(PAST + np.arange(NT), NB)]).astype(f)
    inv = f(THETA) ** (-np.arange(0, ROT, 2, dtype=f) / f(ROT))
    ang = np.tile(inv, 2)[:, None] * pos[None]
    c["cosr"], c["sinr"] = np.cos(ang), np.sin(ang)
    m = np.zeros((ROT, ROT), f)
    for o in range(ROT // 2):
        m[o + ROT // 2, o], m[o, o + ROT // 2] = -1, 1
    c["rotm"] = m
    c["bmask"] = (i // QB == np.arange(P) // QB).astype(f)
    c["tri"] = np.where(i <= np.arange(P), 0, NEG).astype(f)
    s = np.arange(NS)[:, None]
    c["stri"] = np.where((s // NT == own // NT) & (s <= own), 0, NEG).astype(f)
    c["selb"] = (s // NT == np.arange(NB)).astype(f)
    c["sel"] = np.repeat(np.eye(NH, dtype=f), P, 1)
    return c


def cols(a):
    a = np.asarray(a)
    a = a.reshape(-1, a.shape[-1] // P, P)
    return a.transpose(2, 0, 1)


def lay_out(i):
    f = {n: np.asarray(a) for n, a in i.items()}
    one = lambda a: a.reshape(P, -1)
    x = np.concatenate([f["x_prompt"].reshape(SEQ, D), f["x_sample"].reshape(NS, D)])
    par = [one(cols(f[n])) for n in ("norm_mix_pre", "norm_mix_post", "norm_ffn_pre", "norm_ffn_post",
                                     "conv_a_w", "conv_a_b", "lru_ba", "lru_bx", "lru_lambda")]
    by_tile = lambda a: one(cols(a).transpose(0, 2, 1))
    par += [by_tile(f["state_rglru_h"][0]), by_tile(f["state_rglru_conv"][0])]
    par += [one(cols(f[n])) for n in ("conv_c_w", "conv_c_b", "mlstm_norm", "mlstm_skip")]
    n0 = f["state_mlstm_n"][0].transpose(1, 2, 0).reshape(NH, ET, P, NB)
    par += [one(n0.transpose(2, 0, 1, 3)), by_tile(f["state_mlstm_conv"][0])]
    mats = [f["w_in_ab"][0], f["w_out_ab"][0], f["w_ffn_up"][0], f["w_ffn_down"][0],
            f["w_in_c"][0], f["w_out_c"][0], f["w_ffn_up"][1], f["w_ffn_down"][1]]
    units = []
    for w in mats:
        k, m = w.shape
        w = w.reshape(k // (UK * P), UK, P, m // (UM * P), UM, P)
        units.append(w.transpose(3, 0, 2, 4, 1, 5).reshape(-1, P, UM * TILE))
    keys = f["cache_swa_k"][0][:, KEYS].transpose(0, 2, 3, 1).reshape(NB * H, P, NK)
    vals = f["cache_swa_v"][0][:, KEYS].reshape(NB, KT, P, H, HD).transpose(0, 3, 2, 1, 4).reshape(NB * H, P, NK)
    blocks = [f[n][0] for n in ("mlstm_wq", "mlstm_wk", "mlstm_wv")]
    blocks += [w.transpose(0, 2, 1) for w in blocks]
    blocks = [w.reshape(CT, P, QB).transpose(1, 0, 2).reshape(P, -1) for w in blocks]
    gate = f["mlstm_w_gate"][0].reshape(3 * CT, P, 2 * NH).transpose(1, 0, 2)
    small = np.concatenate([f["mlstm_b_gate"][0].reshape(2, NH).T, f["state_mlstm_m"][0].T], 1)
    arrays = {"x": one(cols(x).transpose(0, 2, 1)), "par": np.concatenate(par, 1), "weights": np.concatenate(units),
              "kv": np.concatenate([keys, vals]), "qkvw": np.concatenate(blocks, 1), "wgate": one(gate),
              "gsml": small, "lru_wa": f["lru_wa"][0], "lru_wx": f["lru_wx"][0], "C0": f["state_mlstm_C"][0]}
    arrays.update(constants())
    return {n: np.ascontiguousarray(a, dtype=np.float32) for n, a in arrays.items()}


OUTS = {"x": (P, MT * T), "k": (P, H * T), "v": (P, H * T), "pack_a": (P, MT * (1 + NB) * CW),
        "pack_c": (P, CT * (1 + NB) * PAD), "pack_n": (P, NH * ET * (1 + NB)), "pack_m": (NH, 1 + NB),
        "Cs": (NB, NH, DH, DH), "Cp": (NH, DH, DH)}


def lay_back(o):
    def tokens(a):
        a = a.reshape(P, -1, T).transpose(2, 1, 0)
        return a[:SEQ], a[SEQ:].reshape(NB, NT, -1, P)

    xp, xs = tokens(o["x"])
    kp, ks = tokens(o["k"])
    vp, vs = tokens(o["v"])
    a = o["pack_a"].reshape(P, MT, 1 + NB, CW).transpose(2, 3, 1, 0).reshape(1 + NB, CW, D)
    c = o["pack_c"].reshape(P, CT, 1 + NB, PAD).transpose(2, 3, 1, 0).reshape(1 + NB, PAD, DC)
    n = o["pack_n"].reshape(P, NH, ET, 1 + NB).transpose(3, 1, 2, 0).reshape(1 + NB, NH, DH)
    m = o["pack_m"].T
    out = (xp.reshape(1, SEQ, D), xs.reshape(NB, NT, D),
           a[None, :1, :PAD], a[None, 1:, :PAD], a[None, :1, PAD], a[None, 1:, PAD],
           kp[None, None], ks[None], vp[None, None], vs[None],
           c[None, :1], c[None, 1:], o["Cp"][None, None], o["Cs"][None],
           n[None, :1], n[None, 1:], m[None, :1], m[None, 1:])
    return tuple(np.ascontiguousarray(t) for t in out)


def kernel(**inputs):
    import concourse.bacc as bacc
    from concourse.bass_utils import run_bass_kernel_spmd

    nc = bacc.Bacc("TRN2", target_bir_lowering=False, num_devices=1)
    arrays = lay_out(inputs)
    A = {n: nc.dram_tensor(f"in_{n}", a.shape, F32, kind="ExternalInput").ap() for n, a in arrays.items()}
    O = {n: nc.dram_tensor(f"out_{n}", s, F32, kind="ExternalOutput").ap() for n, s in OUTS.items()}
    program(nc, A, O)
    r = run_bass_kernel_spmd(nc, [{f"in_{n}": a for n, a in arrays.items()}], core_ids=[0])
    return lay_back({n: r.results[0][f"out_{n}"] for n in OUTS})
```

```python
from contextlib import ExitStack

import numpy as np

import concourse.bass as bass
from concourse import mybir

F32 = mybir.dt.float32
F32R = mybir.dt.float32r
ALU = mybir.AluOpType
ACT = mybir.ActivationFunctionType
AX = mybir.AxisListType

P = 128
D = 1024
SEQ = 256
NB = 8
NT = 4
NS = NB * NT
T = SEQ + NS
CW = 4
PAD = CW - 1
S0 = PAD + SEQ
LONG = PAD + NT
ROW = S0 + NB * LONG
CONV = ROW - PAD
EPS = 1e-6
MT = D // P
H = 8
HD = 128
ROT = HD // 4
THETA = 500000.0
PAST = 2048
DIL = ((128, 1), (512, 4), (2048, 16))
LRU_C = 8.0
NBLK = 16
DC = 2 * D
CT = DC // P
NH = 4
DH = DC // NH
ET = DH // P
QB = 4
FF = 4 * D
NEG = -1e30

KEYS = [p for p in range(PAST) if p >= PAST - DIL[1][0] or p % DIL[2][1] < NT]
NK = len(KEYS)
KT = NK // P
NKS = NK + NS
KV_SLOTS = 4
HALF_B = NB // 2

DENSE = [(D, 5 * D), (2 * D, D), (D, FF), (FF, D), (D, 4 * D), (2 * D, D), (D, FF), (FF, D)]
IN_AB, OUT_AB, UP0, DOWN0, IN_C, OUT_C, UP1, DOWN1 = range(8)
UK = 8
UM = 4
UNITS = [k // (UK * P) * (m // (UM * P)) for k, m in DENSE]
STEP0 = [UM * sum(UNITS[:i]) for i in range(8)]
OUT0 = [sum(m // P for _, m in DENSE[:i]) for i in range(8)]
NUNITS = sum(UNITS)
NSTEPS = UM * NUNITS
TILE = UK * P

PARTS = [("g_mix_pre", 2 * MT), ("g_mix_post", 2 * MT), ("g_ffn_pre", 2 * MT), ("g_ffn_post", 2 * MT),
         ("conv_a_w", CW * MT), ("conv_a_b", MT), ("lru_ba", MT), ("lru_bx", MT), ("lru_lambda", MT),
         ("h0", MT * NB), ("conv_a0", MT * NB * PAD),
         ("conv_c_w", CW * CT), ("conv_c_b", CT), ("norm_w", CT), ("skip", CT),
         ("n0", NH * ET * NB), ("conv_c0", CT * NB * PAD)]
NPAR = sum(w for _, w in PARTS)
AT = {name: sum(w for _, w in PARTS[:i]) for i, (name, _) in enumerate(PARTS)}
R_NEGM, R_EN, R_NEGMS = 0, SEQ, 2 * SEQ
R_INTER, R_DECAY = R_NEGMS + NS, R_NEGMS + 2 * NS
NBC = R_DECAY + NB
R_ENS, NROWS = NBC, NBC + NS
GH = 36
C_SLOTS = 8
HD2 = ET // 2
ORDER = [(b, half) for b in range(NB) for half in range(2)]
ORDER.insert(ORDER.index((2, 1)) + 1, (NB, 0))
ORDER.insert(ORDER.index((3, 1)) + 1, (NB, 1))
ITEMS = len(ORDER)
USES = ["q0", "q1", "q2", "q3", "k0", "k1", "k2", "k3", "kt0", "kt1", "ks", "vt0", "vt1", "vs",
        "bc0", "bc1", "sc", "n", "mean"]
DVE_READS = ("ks", "vs", "sc", "n")
STOPS = (STEP0[OUT_C], STEP0[OUT_C] + 1, NSTEPS, NSTEPS + 1)


class Tally:

    def __init__(self, eng, sem):
        self.eng, self.sem, self.n = eng, sem, 0

    def mark(self, ins):
        ins.then_inc(self.sem, 1)
        self.n = self.n + 1

    def wait(self):
        self.eng.wait_ge(self.sem, self.n)

    def after(self, ins):
        self.mark(ins)
        self.wait()


def program(nc, A, O):
    ctx = ExitStack()
    with ctx:
        ARENA = 212000 // 32 * 32
        ctx.enter_context(nc.sbuf_tensor("arena", [P, ARENA // 4], F32))
        arena0 = nc.sbuf_base - ARENA

        def at(name, off, *dims, dt=F32, parts=P):
            off = (off + 31) // 32 * 32
            n = int(np.prod(dims))
            assert off + 4 * n <= ARENA, (name, off + 4 * n - ARENA)
            t = nc.alloc_sbuf_tensor_at(name, [parts, n], dt, offset=arena0 + off)[:, :]
            if len(dims) == 2:
                t = t.rearrange("p (a b) -> p a b", b=dims[1])
            if len(dims) == 3:
                t = t.rearrange("p (a b c) -> p a b c", b=dims[1], c=dims[2])
            return t, (off + 4 * n + 31) // 32 * 32

        par, o = at("par", 0, NPAR)
        ident, o = at("ident", o, P)
        ones, o = at("ones", o, P)
        tiny, o = at("tiny", o, 2)
        w_raw_at = o
        w_raw, o = at("w_raw", o, 2, UM, TILE)
        w_hi, o = at("w_hi", o, UM, TILE, dt=F32R)
        w_lo, o = at("w_lo", o, UM, TILE, dt=F32R)
        w_parts_end = o
        x, o = at("x", o, MT, T)
        rstd_at = o
        rstd, o = at("rstd", o, T)
        std, o = at("std", o, T)
        sqsum, o = at("sqsum", o, T)
        sq_at = o
        sq, o = at("sq", o, 2, T)
        phase = o
        y, _ = at("y", ARENA - 4 * MT * T, MT, T)
        xin_hi, o = at("xin_hi", phase, MT, T, dt=F32R)
        xin_lo, behind_xin = at("xin_lo", o, MT, T, dt=F32R)
        hid_hi, o = at("hid_hi", behind_xin, FF // P, T, dt=F32R)
        hid_lo, o = at("hid_lo", o, FF // P, T, dt=F32R)
        relu, o = at("relu", o, 2, T)
        relu2, o = at("relu2", o, 2, T)

        xa, o = at("xa", behind_xin, MT, ROW)
        behind_ga = o + 4 * MT * T
        v_at = o + 3 * 4 * MT * T
        gaqkv, o = at("gaqkv", o, 4 * MT, T)
        ga, q, k, v = (gaqkv[:, MT * i:MT * i + MT] for i in range(4))
        ya_hi, o = at("ya_hi", o, MT, T, dt=F32R)
        ya_lo, o = at("ya_lo", o, MT, T, dt=F32R)
        kv, o = at("kv", o, KV_SLOTS, NK)
        cosr, o = at("cosr", o, T, parts=ROT)
        sinr, o = at("sinr", o, T, parts=ROT)
        rotm, o = at("rotm", o, ROT, parts=ROT)
        qz, o = at("qz", o, 2, H * (32 + NT))
        qz_of = qz[:, :, 0:H * 32].rearrange("p s (h c) -> p s h c", c=32)
        qz_diag = qz.rearrange("p s (h c) -> p s h c", c=32 + NT)[:, :, :, 0:NT]
        att, o = at("att", o, 2, 8)
        pack_a, o = at("pack_a", o, MT, (1 + NB) * CW)
        lruw_at = o
        lruw, o = at("lruw", o, 2 * MT, P)
        lrut, o = at("lrut", o, 8, MT)
        HM = MT // 2
        ip, late = at("ip", o, HM, ROW)
        hp, late = at("hp", late, HM, ROW)
        gg, _ = at("gg", o, HM, T)
        rot, _ = at("rot", o, HM, T)
        xc, o = at("xc", phase, HM, ROW)
        rp, o = at("rp", o, HM, ROW)
        tp, o = at("tp", o, HM, ROW)
        assert o <= behind_xin
        gelu, _ = at("gelu", phase + 4 * HM * ROW, HM, T)
        yb_hi, o = at("yb_hi", behind_xin, H, T, dt=F32R)
        yb_lo, o = at("yb_lo", o, H, T, dt=F32R)
        assert o <= behind_ga
        vtok, o = at("vtok", phase, 3, D)
        sS, o = at("sS", o, NKS)
        assert o <= behind_xin
        pT, o = at("pT", v_at, KT + 1, 2 * P)
        assert o <= v_at + 4 * H * T
        amask, o = at("amask", lruw_at, 3 * P)
        smask, o = at("smask", o, NK + 2 * NS)
        pvs, _ = at("pvs", o, D)
        pS, o = at("pS", o, 2, 3 * P)
        pTp, o = at("pTp", o, 2, 3 * P)

        xm, o = at("xm", behind_xin, CT, ROW)
        behind_xm = o
        z, o = at("z", o, CT, T)
        y1_hi, _ = at("y1_hi", behind_xm, CT, T, dt=F32R)
        y1_lo, _ = at("y1_lo", behind_xin, CT, T, dt=F32R)
        xms, o = at("xms", o, CT, NS)
        qkvw, o = at("qkvw", o, 6, CT, QB)
        bmask, o = at("bmask", o, P)
        fold, o = at("fold", o, 2 * CT, GH)
        sel, o = at("sel", o, NH * P, parts=NH)
        tri, o = at("tri", o, P)
        stri, o = at("stri", o, NS, parts=NS)
        sel3, o = at("sel3", o, 2, NB, parts=3 * NS)
        seln, o = at("seln", o, NB, dt=F32R, parts=3 * NS)
        gsml, o = at("gsml", o, 2 + NB, parts=NH)
        tokg, o = at("tokg", o, 2, 2 * NH)
        tokg_s, o = at("tokg_s", o, 2, NH, parts=NS)
        w3, o = at("w3", o, NH, parts=3 * NS)
        stok, o = at("stok", o, 5, NH, parts=NS)
        pack_c, o = at("pack_c", o, CT, (1 + NB) * PAD)
        pack_n, o = at("pack_n", o, NH * ET, 1 + NB)
        pack_m, o = at("pack_m", o, 1 + NB, parts=NH)
        rows, o = at("rows", o, NROWS, parts=NH)
        work = o
        wgate, _ = at("wgate", work, 3 * CT, 2 * NH)
        bdT, o = at("bdT", work + 4 * 3 * CT * 2 * NH, 3 * CT, P)
        convt, convt_end = at("convt", o, 4, CONV + 4)
        xcc, tail = at("xcc", convt_end, CT, T)
        ew, _ = at("ew", tail, 3 * P + NS)
        qf, o = at("qf", work, ET, T)
        kf, o = at("kf", o, ET, T)
        ktok, o = at("ktok", o, 2, DH)
        vtk, o = at("vtk", o, 2, DH)
        gates_at = o
        vw, o = at("vw", o, 2, DH)
        dn, o = at("dn", o, SEQ)
        hs, o = at("hs", o, NH, DH, parts=NS)
        assert o <= convt_end
        gi, o = at("gi", gates_at, ROW, parts=NH)
        gf, o = at("gf", o, ROW, parts=NH)
        gt, o = at("gt", o, ROW, parts=NH)
        gb, o = at("gb", o, ROW, parts=NH)
        gg_c, o = at("gg_c", o, T, parts=NH)
        gw_c, o = at("gw_c", o, SEQ + 3 * NS, parts=NH)
        ghist, o = at("ghist", o, 2 * ROW, parts=NH)
        assert o <= convt_end
        xcs3, o = at("xcs3", phase, CT, 3 * NS)
        xms3, o = at("xms3", o, CT, 3 * NS)
        hs_f, _ = at("hs_f", o, CT, NS)
        hT, o = at("hT", o, ET, SEQ)
        vtk_s, o = at("vtk_s", o, DH, parts=NS)
        assert o <= behind_xin
        bc, o = at("bc", rstd_at, 2, NBC)
        qn, o = at("qn", o, ET, NS)
        assert o <= phase
        cring, o = at("cring", w_raw_at, C_SLOTS, HD2, DH)
        bd, o = at("bd", o, 2 * 3 * ET, P)
        qz1, o = at("qz1", o, 2, ET * NB * NS)
        kst, o = at("kst", o, 2, DH, dt=F32R, parts=3 * NS)
        vst, o = at("vst", o, 2, DH, dt=F32R, parts=3 * NS)
        vb, o = at("vb", o, 2, DH, dt=F32R, parts=3 * NS)
        assert o <= w_parts_end, o - w_parts_end
        ps = ctx.enter_context(nc.psum_tensor("ps", [P, 8, 512], F32))

        def qz_of1(h, e, b):
            return qz1[:, h % 2, NS * (NB * e + b):NS * (NB * e + b) + NS]

        def qz_own(h, e):
            c0 = NS * NB * e
            last = c0 + (NB - 1) * (NS + NT)
            return (qz1[:, h % 2, c0:last].rearrange("p (b c) -> p b c", c=NS + NT)[:, :, 0:NT],
                    qz1[:, h % 2, last:last + NT])

        def pcol(name, i):
            return par[:, AT[name] + i:AT[name] + i + 1]

        def samples(row_ap, lo, n):
            if len(row_ap.shape) == 2:
                return row_ap[:, S0:ROW].rearrange("p (b c) -> p b c", c=LONG)[:, :, lo:lo + n]
            return row_ap[:, :, S0:ROW].rearrange("p m (b c) -> p m b c", c=LONG)[:, :, :, lo:lo + n]

        def seqs(ap):
            return ap.rearrange("p (b t) -> p b t", t=NT)

        sems = {}

        def sem(name):
            sems[name] = ctx.enter_context(nc.semaphore(name))
            return sems[name]

        consts_in = sem("consts_in")
        x_in = sem("x_in")
        masks_in = sem("masks_in")
        consts_c_in = sem("consts_c_in")
        raw_in = [sem(f"raw_in{s}") for s in range(2)]
        hi_ready = sem("hi_ready")
        lo_ready = sem("lo_ready")
        step_done = sem("step_done")
        out_taken = sem("out_taken")
        sq_ready = sem("sq_ready")
        sq_added = sem("sq_added")
        mean_ready = sem("mean_ready")
        std_ready = sem("std_ready")
        rstd_ready = sem("rstd_ready")
        x_new = sem("x_new")
        xin_hi_ready = sem("xin_hi_ready")
        xin_ready = sem("xin_ready")
        relu2_ready = sem("relu2_ready")
        hid_hi_ready = sem("hid_hi_ready")
        hid_ready = sem("hid_ready")
        v_order = sem("v_order")
        a_order = sem("a_order")
        p_order = sem("p_order")
        tiny_ready = sem("tiny_ready")
        lam_v = sem("lam_v")
        lam_a = sem("lam_a")
        lruw_zero = sem("lruw_zero")
        lruw_in = sem("lruw_in")
        pads_ready = sem("pads_ready")
        rot_ready = sem("rot_ready")
        rot_taken = sem("rot_taken")
        rope_done = sem("rope_done")
        conv_ready = sem("conv_ready")
        gates_ready = sem("gates_ready")
        gates_taken = sem("gates_taken")
        th_ready = sem("th_ready")
        b_arg = sem("b_arg")
        b_root = sem("b_root")
        scanned = sem("scanned")
        gelu_ready = sem("gelu_ready")
        ya_full = sem("ya_full")
        ya_hi_ready = sem("ya_hi_ready")
        ya_ready = sem("ya_ready")
        vt_ready = sem("vt_ready")
        vt_taken = sem("vt_taken")
        kv_in = [sem(f"kv_in{s}") for s in range(KV_SLOTS)]
        kv_free = sem("kv_free")
        qz_ready = sem("qz_ready")
        s_ready = sem("s_ready")
        s_taken = sem("s_taken")
        max_ready = sem("max_ready")
        exp_ready = sem("exp_ready")
        p_ready = sem("p_ready")
        pt_ready = sem("pt_ready")
        pt_taken = sem("pt_taken")
        pv_ready = sem("pv_ready")
        yb_hi_ready = sem("yb_hi_ready")
        yb_ready = sem("yb_ready")
        ss_taken = sem("ss_taken")
        smax_ready = sem("smax_ready")
        sexp_ready = sem("sexp_ready")
        sp_ready = sem("sp_ready")
        spt_ready = sem("spt_ready")
        spt_taken = sem("spt_taken")
        spv_taken = sem("spv_taken")
        syb_ready = sem("syb_ready")
        v_stored = sem("v_stored")
        stored = sem("stored")
        bdT_ready = sem("bdT_ready")
        bdT_used = sem("bdT_used")
        fold_zero = sem("fold_zero")
        fold_ready = sem("fold_ready")
        xm_pads = sem("xm_pads")
        conv0_ready = sem("conv0_ready")
        convc_ready = sem("convc_ready")
        xcc_ready = sem("xcc_ready")
        z_ready = sem("z_ready")
        g_ready = sem("g_ready")
        gv = sem("gv")
        gact = sem("gact")
        gcol_ready = sem("gcol_ready")
        gcol_taken = sem("gcol_taken")
        tok3_ready = sem("tok3_ready")
        qz1_zero = sem("qz1_zero")
        bd_ready = sem("bd_ready")
        stage_full = sem("stage_full")
        stage_read_a = sem("stage_read_a")
        stage_read_v = sem("stage_read_v")
        kst_hi_ready = sem("kst_hi_ready")
        vst_hi_ready = sem("vst_hi_ready")
        vb_ready = sem("vb_ready")
        ew_arg = sem("ew_arg")
        ew_exp = sem("ew_exp")
        qs_ready = sem("qs_ready")
        c_in = [sem(f"c_in{s}") for s in range(C_SLOTS)]
        c_out = [sem(f"c_out{s}") for s in range(C_SLOTS)]
        c_mm = sem("c_mm")
        c_new = sem("c_new")
        den_psum = sem("den_psum")
        den_abs = sem("den_abs")
        num_psum = sem("num_psum")
        h_ready = sem("h_ready")
        h_sq = sem("h_sq")
        hs_psum = sem("hs_psum")
        hs_taken = sem("hs_taken")
        hs_sq = sem("hs_sq")
        hs_mean = sem("hs_mean")
        hs_std = sem("hs_std")
        hs_scaled = sem("hs_scaled")
        hst_ready = sem("hst_ready")
        y1s_full = sem("y1s_full")
        y1s_hi = sem("y1s_hi")
        y1_full = sem("y1_full")
        y1_hi_ready = sem("y1_hi_ready")
        y1_ready = sem("y1_ready")

        block = ctx.enter_context(nc.Block())

        def loop(eng, n, body, peel_first=True, peel_last=False):
            a, b = (1 if peel_first else 0), (n - 1 if peel_last else n)
            if peel_first:
                body(0)
            if b - a > 1:
                with eng.Fori(a, b) as i:
                    body(i)
            elif b > a:
                body(a)
            if peel_last and n - 1 >= a:
                body(n - 1)

        def use(h, name):
            return len(USES) * h + USES.index(name)

        def reads(u):
            by_dve = USES[u % len(USES)] in DVE_READS
            n = sum(1 for j in range(u + 1) if (USES[j % len(USES)] in DVE_READS) == by_dve)
            return (stage_read_v if by_dve else stage_read_a), n

        def item(h, b, half):
            return ITEMS * h + ORDER.index((b, half))

        def loads(i):
            return sum(1 for j in range(i % C_SLOTS, i + 1, C_SLOTS) if ORDER[j % ITEMS][0] < NB)

        def store_cols(sp, out, src):
            sp.dma_start(out, src).then_inc(stored, 16)

        @block.sync
        def _(sp):
            def const(dst, name):
                sp.dma_start(dst, A[name]).then_inc(consts_in, 16)

            def unit(u, count):
                s = count
                sp.dma_start(w_raw[:, s], A["weights"][bass.ds(u, 1)].rearrange("u p (j c) -> (u p) j c", j=UM)
                             ).then_inc(raw_in[s], 16)

            def unit_pairs(a, b):
                with sp.Fori(a, b) as i:
                    for s in range(2):
                        sp.wait_ge(lo_ready, UM * (2 * i + s - 1))
                        unit(2 * i + s, s)

            def cache(i, s):
                sp.dma_start(kv[:, s], A["kv"][bass.ds(i, 1)].rearrange("u p c -> (u p) c")
                             ).then_inc(kv_in[s], 16)

            sp.dma_start(x, A["x"]).then_inc(x_in, 16)
            for dst, name in ((par, "par"), (ones, "ones"), (ident, "ident"), (cosr, "cosr"), (sinr, "sinr"),
                              (rotm, "rotm")):
                const(dst, name)
            unit(0, 0)
            unit(1, 1)
            sp.wait_ge(lruw_zero, 1)
            for g, name in enumerate(("lru_wa", "lru_wx")):
                for e in range(2):
                    src = A[name].rearrange("(m e) i o -> e i m o", e=2)[e]
                    sp.dma_start(lruw[64 * e:64 * e + 64, g * MT:(g + 1) * MT, 64 * e:64 * e + 64], src
                                 ).then_inc(lruw_in, 16)
            for s in range(KV_SLOTS):
                cache(s, s)
            unit_pairs(1, UNITS[0] // 2 + 1)
            sp.wait_ge(out_taken, OUT0[OUT_AB])
            sp.dma_start(O["v"], v.rearrange("p h t -> p (h t)")).then_inc(v_stored, 16)

            def cache_group(i):
                for s in range(KV_SLOTS):
                    sp.wait_ge(kv_free, KV_SLOTS * i + s - (KV_SLOTS - 1))
                    cache(KV_SLOTS * i + s, s)

            with sp.Fori(1, NB * H // KV_SLOTS) as i:
                cache_group(i)
            sp.wait_ge(rope_done, 4)
            store_cols(sp, O["k"], k.rearrange("p h t -> p (h t)"))
            sp.wait_ge(ya_ready, 2)
            store_cols(sp, O["pack_a"], pack_a.rearrange("p m c -> p (m c)"))
            sp.dma_start(amask, A["amask"]).then_inc(masks_in, 16)
            sp.dma_start(smask, A["smask"]).then_inc(masks_in, 16)
            with sp.Fori(NB * H // KV_SLOTS, 2 * NB * H // KV_SLOTS) as i:
                cache_group(i)
            unit_pairs(UNITS[0] // 2 + 1, STEP0[IN_C] // (2 * UM) + 1)
            sp.wait_ge(step_done, STEP0[IN_C])
            sp.wait_ge(x_new, 2 * MT)
            for dst, name in ((qkvw, "qkvw"), (bmask, "bmask"), (sel, "sel"), (tri, "tri"), (stri, "stri"),
                              (sel3, "sel3"), (gsml, "gsml"), (wgate, "wgate")):
                sp.dma_start(dst, A[name]).then_inc(consts_c_in, 16)
            unit_pairs(STEP0[IN_C] // (2 * UM) + 1, STEP0[OUT_C] // (2 * UM))

            def c_load(i):
                h, r = divmod(i, ITEMS)
                b, half = ORDER[r]
                s = i % C_SLOTS
                if b < NB:
                    if i >= C_SLOTS:
                        sp.wait_ge(c_out[s], 16 * (i // C_SLOTS))
                    src = A["C0"][b, h].rearrange("(t p) e -> p t e", p=P)
                    sp.dma_start(cring[:, s], src[:, HD2 * half:HD2 * half + HD2]).then_inc(c_in[s], 16)

            def c_store(i):
                h, r = divmod(i, ITEMS)
                b, half = ORDER[r]
                s = i % C_SLOTS
                sp.wait_ge(c_new, i + 1)
                dst = O["Cs"][b, h] if b < NB else O["Cp"][h]
                dst = dst.rearrange("(t p) e -> p t e", p=P)
                sp.dma_start(dst[:, HD2 * half:HD2 * half + HD2], cring[:, s]).then_inc(c_out[s], 16)

            sp.wait_ge(lo_ready, STEP0[OUT_C])
            for i in range(C_SLOTS - 2):
                c_load(i)

            def unit_back(s):
                for j in range(C_SLOTS // 2 * s, C_SLOTS // 2 * (s + 1)):
                    sp.wait_ge(c_out[j], 16 * len(range(j, NH * ITEMS, C_SLOTS)))
                sp.dma_start(w_raw[:, s], A["weights"][STEP0[OUT_C] // UM + s].rearrange("p (j c) -> p j c", j=UM)
                             ).then_inc(raw_in[s], 16)

            for i in range(NH * ITEMS):
                if i == NH * ITEMS - 2:
                    unit_back(0)
                c_store(i)
                if i + C_SLOTS - 2 < NH * ITEMS:
                    c_load(i + C_SLOTS - 2)
            unit_back(1)
            sp.wait_ge(y1_ready, NH + 1)
            store_cols(sp, O["pack_c"], pack_c.rearrange("p m c -> p (m c)"))
            store_cols(sp, O["pack_n"], pack_n.rearrange("p m c -> p (m c)"))
            store_cols(sp, O["pack_m"], pack_m)
            unit_pairs(STEP0[OUT_C] // (2 * UM) + 1, NUNITS // 2)
            sp.wait_ge(x_new, 4 * MT)
            store_cols(sp, O["x"], x.rearrange("p m t -> p (m t)"))
            sp.wait_ge(v_stored, 16)
            for s in range(C_SLOTS):
                sp.wait_ge(c_out[s], 16 * len(range(s, NH * ITEMS, C_SLOTS)))
            sp.wait_ge(stored, 16 * 6)

        @block.scalar
        def _(act):
            order = Tally(act, a_order)

            def act_hi(l, it, base):
                u = l // UM
                g = base + 8 * it + l
                if not (isinstance(g, int) and g < UM):
                    act.wait_ge(step_done, g - UM + 1)
                if l % UM == 0:
                    act.wait_ge(raw_in[u % 2], 16 * (base // 8 + it + u // 2 + 1))
                act.activation(w_hi[:, l % UM], w_raw[:, u % 2, l % UM], ACT.Copy).then_inc(hi_ready, 1)

            def steps(ph, groups, evac):
                base = STEP0[ph]

                def body(it):
                    for l in range(8 * groups):
                        if not (isinstance(it, int) and base + 8 * groups * it + l + 2 in STOPS):
                            act_hi(l + 2, groups * it, base)
                        evac(it, l)
                last = ph in (IN_C, DOWN1)
                loop(act, UNITS[ph] // (2 * groups), body, peel_first=ph == IN_AB, peel_last=last)

            def stat_squares(s, get, ready):
                for m in range(MT):
                    ready(m)
                    if 8 * s + m >= 2:
                        act.wait_ge(sq_added, 8 * s + m - 1)
                    act.activation(sq[:, m % 2], get(m), ACT.Square).then_inc(sq_ready, 1)

            def stat_std(s):
                act.wait_ge(mean_ready, s + 1)
                if s >= 1:
                    act.wait_ge(rstd_ready, s)
                act.activation(std, ps[:, 7, 0:T], ACT.Sqrt, bias=tiny[:, 0:1], scale=1.0 / D).then_inc(std_ready, 1)

            def norm_in(s, n, gain, layer, between=None):
                for m in range(MT):
                    if n:
                        act.wait_ge(x_new, MT * (n - 1) + m + 1)
                    act.activation(xin_hi[:, m], x[:, m], ACT.Copy, scale=pcol(gain, layer * MT + m)
                                   ).then_inc(xin_hi_ready, 1)
                    if 8 * s + m >= 2:
                        act.wait_ge(sq_added, 8 * s + m - 1)
                    act.activation(sq[:, m % 2], x[:, m], ACT.Square).then_inc(sq_ready, 1)
                if between:
                    between()
                stat_std(s)

            def block_out(ph, s, per):
                groups = max(1, per // 2)

                def evac(it, l):
                    if l // UM % per != per - 1:
                        return
                    j = l % UM
                    m = it * UM + j
                    act.wait_ge(step_done, STEP0[ph] + 8 * groups * it + l + 1)
                    act.wait_ge(sq_added, 8 * s + it * UM + j - 1)
                    act.activation(sq[:, j % 2], ps[:, j, 0:T], ACT.Square).then_inc(sq_ready, 1)
                    act.activation(y[:, bass.ds(m, 1)].rearrange("p a t -> p (a t)"), ps[:, j, 0:T], ACT.Copy
                                   ).then_inc(out_taken, 1)
                steps(ph, groups, evac)
                stat_std(s)

            def mlp_up(ph, n):
                def evac(it, l):
                    m = 8 * it + l
                    act.wait_ge(out_taken, OUT0[ph] + m + 1)
                    if not (isinstance(it, int) and 32 * n + m < 2):
                        act.wait_ge(hid_ready, 32 * n + m - 1)
                    act.activation(relu2[:, l % 2], relu[:, l % 2], ACT.Square).then_inc(relu2_ready, 1)
                    act.wait_ge(relu2_ready, 32 * n + m + 1)
                    act.activation(hid_hi[:, bass.ds(m, 1)].rearrange("p a t -> p (a t)"), relu2[:, l % 2], ACT.Copy
                                   ).then_inc(hid_hi_ready, 1)
                base = STEP0[ph]

                act_hi(2, 0, base)

                def body(it):
                    for l in range(8):
                        if not (isinstance(it, int) and it > 0 and l == 7):
                            act_hi(l + 3, it, base)
                        evac(it, l)
                loop(act, UNITS[ph] // 2, body, peel_first=True, peel_last=True)

            act.wait_ge(consts_in, 16 * 6)
            act.wait_ge(tiny_ready, 2)
            act.wait_ge(x_in, 16)

            def first_steps():
                act_hi(0, 0, 0)
                act_hi(1, 0, 0)
            norm_in(0, 0, "g_mix_pre", 0, first_steps)
            act.wait_ge(lam_v, 1)
            act.activation(lrut[:, 2], lrut[:, 1], ACT.Exp, scale=-1.0).then_inc(lam_a, 1)
            act.wait_ge(lam_v, 2)
            act.activation(lrut[:, 4], lrut[:, 3], ACT.Ln).then_inc(lam_a, 1)
            steps(IN_AB, 1, lambda it, l: None)

            act.wait_ge(lam_v, 3)
            for c in range(2):
                for g, dst in ((0, rp), (1, ip)):
                    act.wait_ge(gates_ready, 2 * c + g + 1)
                    for m in range(HM):
                        act.activation(dst[:, m, PAD:ROW], ps[:, 4 + m, 0:CONV], ACT.Sigmoid,
                                       bias=pcol(("lru_ba", "lru_bx")[g], c * HM + m)).then_inc(gates_taken, 1)
                act.wait_ge(gates_taken, HM * (2 * c + 2))
                for m in range(HM):
                    order.mark(act.activation(tp[:, m, PAD:ROW], rp[:, m, PAD:ROW], ACT.Tanh,
                                              scale=lrut[:, 7, c * HM + m:c * HM + m + 1]))
                order.wait()
                for m in range(HM):
                    last = act.activation(rp[:, m, PAD:ROW], rp[:, m, PAD:ROW], ACT.Exp,
                                          scale=lrut[:, 6, c * HM + m:c * HM + m + 1])
                last.then_inc(th_ready, 1)
                act.wait_ge(b_arg, c + 1)
                act.activation(tp[:, :, PAD:ROW], tp[:, :, PAD:ROW], ACT.Sqrt, bias=tiny[:, 1:2]).then_inc(b_root, 1)
                act.wait_ge(scanned, c + 1)
                act.activation(gelu, ga[:, c * HM:c * HM + HM], ACT.Gelu_apprx_tanh).then_inc(gelu_ready, 1)
                act.wait_ge(ya_full, c + 1)
                act.activation(ya_hi[:, c * HM:c * HM + HM], gg, ACT.Copy).then_inc(ya_hi_ready, 1)

            act.wait_ge(ya_ready, 2)
            for r in range(6):
                tt, half = divmod(r, 2)
                n = P if tt < 2 else NS
                act.wait_ge(vt_ready, r + 1)
                act.activation(vtok[0:n, tt, 512 * half:512 * half + 512], ps[0:n, 4 + r % 4, :], ACT.Copy
                               ).then_inc(vt_taken, 1)

            for f in range(2):
                act.wait_ge(smax_ready, f + 1)
                act.activation(sS, sS, ACT.Exp, bias=att[:, f, 4:5], accum_out=att[:, f, 5:6]).then_inc(sexp_ready, 1)
                if f == 0:
                    act.wait_ge(v_stored, 16)
                for i in range(2):
                    act.wait_ge(spt_ready, 2 * f + i + 1)
                    if i == 0:
                        act.activation(pT[:, 0:4, P * f:P * f + P], ps[:, 4, :].rearrange("p (k r) -> p k r", k=4),
                                       ACT.Copy).then_inc(spt_taken, 1)
                    else:
                        act.activation(pT[:, 4:7, P * f:P * f + P],
                                       ps[:, 5, 0:3 * P].rearrange("p (k r) -> p k r", k=3), ACT.Copy
                                       ).then_inc(spt_taken, 1)
                        act.activation(pT[0:NS, 7, P * f:P * f + P], ps[0:NS, 5, 3 * P:4 * P], ACT.Copy
                                       ).then_inc(spt_taken, 1)
            for h in range(H):
                act.wait_ge(max_ready, h + 1)
                f = h % 2
                for i, (a, b) in enumerate(((0, P), (P, 3 * P))):
                    last = act.activation(pS[:, f, a:b], pS[:, f, a:b], ACT.Exp, bias=att[:, f, i:i + 1],
                                          accum_out=att[:, f, 2 + i:3 + i])
                last.then_inc(exp_ready, 1)
                act.wait_ge(pt_ready, h + 1)
                if h >= 2:
                    act.wait_ge(pv_ready, h - 1)
                act.activation(pTp[:, f], ps[:, 6, 0:3 * P], ACT.Copy).then_inc(pt_taken, 1)
                act.wait_ge(pv_ready, h + 1)
                act.activation(yb_hi[:, h, 0:SEQ], ps[:, 7, SEQ * f:SEQ * f + SEQ], ACT.Copy).then_inc(yb_hi_ready, 1)

            for f in range(2):
                act.wait_ge(kv_free, NB * H + HALF_B * H * (f + 1))
                if f:
                    act.wait_ge(syb_ready, f)
                act.activation(pvs.rearrange("p (a b) -> p a b", a=2), ps[:, 2 * f:2 * f + 2, :], ACT.Copy
                               ).then_inc(spv_taken, 1)
            act.wait_ge(syb_ready, 2)
            act.activation(yb_hi[:, :, SEQ:T], ps[:, 6, 0:H * NS].rearrange("p (h t) -> p h t", h=H), ACT.Copy
                           ).then_inc(yb_hi_ready, 1)

            block_out(OUT_AB, 1, 2)
            norm_in(2, 1, "g_ffn_pre", 0)
            mlp_up(UP0, 0)
            block_out(DOWN0, 3, 4)
            norm_in(4, 2, "g_mix_pre", 1)

            def conv_first(m):
                if m >= 4:
                    act.wait_ge(xcc_ready, m - 3)
                act.activation(convt[:, m % 4, 0:CONV], xm[:, m, PAD:ROW], ACT.Identity,
                               scale=pcol("conv_c_w", (CW - 1) * CT + m), bias=pcol("conv_c_b", m)
                               ).then_inc(conv0_ready, 1)

            def conv_silu(m):
                act.wait_ge(convc_ready, m + 1)
                c = convt[:, m % 4, 0:CONV]
                act.activation(xcc[:, m, 0:SEQ], c[:, 0:SEQ], ACT.Silu)
                act.activation(seqs(xcc[:, m, SEQ:T]),
                               c[:, SEQ:SEQ + NB * LONG].rearrange("p (b c) -> p b c", c=LONG)[:, :, PAD:LONG],
                               ACT.Silu).then_inc(xcc_ready, 1)

            base = STEP0[IN_C]
            halves = UNITS[IN_C] // 2
            with act.Fori(0, halves // 2) as it:
                for l in range(8):
                    act_hi(l + 2, it, base)
            for it in range(halves // 2, halves):
                for l in range(8):
                    if base + 8 * it + l + 2 not in STOPS:
                        act_hi(l + 2, it, base)
                    m = 8 * it + l - CT
                    if m == 0:
                        act.wait_ge(xm_pads, 2)
                    act.wait_ge(out_taken, OUT0[IN_C] + CT)
                    conv_first(m)
                    if m:
                        conv_silu(m - 1)
            conv_silu(CT - 1)

            def staged(h, name):
                u = use(h, name)
                act.wait_ge(stage_full, u + 1)
                return ps[:, 6 + u % 2]

            def qk(h):
                for e in range(ET):
                    act.activation(qf[:, e], staged(h, f"q{e}")[:, 0:T], ACT.Copy).then_inc(stage_read_a, 1)
                for e in range(ET):
                    act.activation(kf[:, e], staged(h, f"k{e}")[:, 0:T], ACT.Copy, scale=DH ** -0.5
                                   ).then_inc(stage_read_a, 1)

            def keys_by_token(h):
                for tt in range(2):
                    act.activation(ktok[:, tt], staged(h, f"kt{tt}"), ACT.Copy, scale=DH ** -0.5
                                   ).then_inc(stage_read_a, 1)

            act.activation(z, z, ACT.Silu).then_inc(z_ready, 1)
            act.wait_ge(g_ready, 1)
            act.wait_ge(gv, 1)
            for r, dst in ((0, gi), (32, gf)):
                bias = gsml[:, 0:1] if r == 0 else gsml[:, 1:2]
                order.mark(act.activation(dst[:, PAD:S0], ps[r:r + NH, 4, 0:SEQ], ACT.Identity))
                order.mark(act.activation(samples(dst, PAD, NT), seqs(ps[r:r + NH, 4, SEQ:T]), ACT.Identity))
            order.wait()
            order.mark(act.activation(gi[:, PAD:ROW], gi[:, PAD:ROW], ACT.Identity, bias=gsml[:, 0:1]))
            act.activation(gf[:, PAD:ROW], gf[:, PAD:ROW], ACT.Identity, bias=gsml[:, 1:2]).then_inc(gact, 1)
            act.wait_ge(gv, 2)
            order.after(act.activation(gt[:, PAD:ROW], gt[:, PAD:ROW], ACT.Exp, scale=-1.0))
            act.activation(gt[:, PAD:ROW], gt[:, PAD:ROW], ACT.Ln, bias=1.0).then_inc(gact, 1)
            qk(0)
            keys_by_token(0)
            act.wait_ge(gv, 3)
            act.activation(rows[:, R_EN:R_EN + SEQ], rows[:, R_EN:R_EN + SEQ], ACT.Exp)
            act.activation(rows[:, R_INTER:NROWS], rows[:, R_INTER:NROWS], ACT.Exp)
            act.activation(gw_c, gw_c, ACT.Exp).then_inc(gact, 1)
            act.wait_ge(gcol_ready, 1)
            act.activation(tokg.rearrange("p a b -> p (a b)"), ps[:, 5, 0:4 * NH], ACT.Copy)
            act.activation(tokg_s.rearrange("p a b -> p (a b)"), ps[0:NS, 5, 4 * NH:6 * NH], ACT.Copy)
            act.activation(w3, ps[0:3 * NS, 5, 6 * NH:7 * NH], ACT.Copy, scale=DH ** -0.5)
            act.activation(seln, sel3[:, 1], ACT.Copy).then_inc(gcol_taken, 1)
            act.wait_ge(gcol_taken, 1)

            def own_keys(h):
                act.activation(kst[:, h % 2], staged(h, "ks")[0:3 * NS], ACT.Copy, scale=w3[:, h:h + 1]
                               ).then_inc(kst_hi_ready, 1)

            def values_by_token(h):
                for tt in range(2):
                    src = staged(h, f"vt{tt}")
                    act.activation(vtk[:, tt], src, ACT.Copy)
                    act.activation(vw[:, tt], src, ACT.Copy, scale=tokg[:, tt, NH + h:NH + h + 1]
                                   ).then_inc(stage_read_a, 1)
                src = staged(h, "vs")
                act.activation(vtk_s, src[0:NS], ACT.Copy)
                act.activation(vst[:, h % 2], src[0:3 * NS], ACT.Copy).then_inc(vst_hi_ready, 1)

            def head_rows(h):
                act.activation(bc[:, h % 2, 0:512], staged(h, "bc0"), ACT.Copy).then_inc(stage_read_a, 1)
                act.activation(bc[:, h % 2, 512:NBC], staged(h, "bc1")[:, 0:NBC - 512], ACT.Copy
                               ).then_inc(stage_read_a, 1)

            def exps(h):
                act.wait_ge(ew_arg, h + 1)
                act.activation(ew[:, 0:2 * P], ew[:, 0:2 * P], ACT.Exp, bias=tokg[:, 0, h:h + 1])
                act.activation(ew[:, 2 * P:3 * P], ew[:, 2 * P:3 * P], ACT.Exp, bias=tokg[:, 1, h:h + 1])
                act.activation(ew[0:NS, 3 * P:3 * P + NS], ew[0:NS, 3 * P:3 * P + NS], ACT.Exp,
                               bias=tokg_s[:, 0, h:h + 1]).then_inc(ew_exp, 1)

            def own_values(h, b):
                n = NB * h + b
                act.wait_ge(stage_read_v, reads(use(h, "vs"))[1])
                if n >= 2:
                    ho, bo = divmod(n - 2, NB)
                    act.wait_ge(c_mm, item(ho, bo, 1) + 1)
                act.activation(vb[:, n % 2], vst[:, h % 2], ACT.Copy, scale=sel3[:, 0, b:b + 1]).then_inc(vb_ready, 1)

            def chunk(h, b):
                if b == 0:
                    act.wait_ge(den_psum, h + 1)
                    act.activation(stok[:, 0, h:h + 1], ps[0:NS, 3, SEQ:SEQ + 1], ACT.Abs)
                    act.activation(dn, ps[:, 3, 0:SEQ], ACT.Abs).then_inc(den_abs, 1)
                if b == 1:
                    act.wait_ge(h_ready, h + 1)
                    act.activation(qf[:, :, 0:SEQ], hT, ACT.Square).then_inc(h_sq, 1)
                if b == 3:
                    act.activation(dn, staged(h, "mean")[:, 0:SEQ], ACT.Sqrt, bias=tiny[:, 0:1], scale=1.0 / DH
                                   ).then_inc(stage_read_a, 1)
                if b == 4 and h + 1 < NH:
                    qk(h + 1)
                if b == 5 and h + 1 < NH:
                    keys_by_token(h + 1)
                    own_keys(h + 1)
                if b == 6:
                    if h + 1 < NH:
                        values_by_token(h + 1)
                    act.wait_ge(y1_full, h + 1)
                    act.activation(y1_hi[:, ET * h:ET * h + ET, 0:SEQ], hT, ACT.Copy).then_inc(y1_hi_ready, 1)
                if b == 7:
                    if h + 1 < NH:
                        head_rows(h + 1)
                    act.wait_ge(hs_psum, h + 1)
                    act.activation(hs[:, h], ps[0:NS, 2, :], ACT.Copy).then_inc(hs_taken, 1)
                    act.wait_ge(hs_taken, h + 1)
                    act.activation(fold[0:NS].rearrange("p a b -> p (a b)")[:, 0:DH], hs[:, h], ACT.Square, accum_out=stok[:, 1, h:h + 1]).then_inc(hs_sq, 1)
                    if h + 1 < NH:
                        exps(h + 1)

            own_keys(0)
            values_by_token(0)
            head_rows(0)
            exps(0)
            own_values(0, 0)
            for h in range(NH):
                for b in range(NB):
                    if b + 1 < NB:
                        own_values(h, b + 1)
                    elif h + 1 < NH:
                        own_values(h + 1, 0)
                    chunk(h, b)
            act.wait_ge(hs_mean, 1)
            act.activation(stok[:, 3], stok[:, 3], ACT.Sqrt, bias=tiny[0:NS, 0:1], scale=1.0 / DH).then_inc(hs_std, 1)
            act_hi(0, 0, STEP0[OUT_C])
            act_hi(1, 0, STEP0[OUT_C])
            act.wait_ge(y1s_full, 1)
            act.activation(y1_hi[:, :, SEQ:T], hs_f, ACT.Copy).then_inc(y1s_hi, 1)

            block_out(OUT_C, 5, 2)
            norm_in(6, 3, "g_ffn_pre", 1)
            mlp_up(UP1, 1)
            block_out(DOWN1, 7, 4)

        @block.vector
        def _(dve):
            order = Tally(dve, v_order)

            def dve_lo(l, it, base):
                u = l // UM
                dve.wait_ge(hi_ready, base + 8 * it + l + 1)
                dve.tensor_tensor(w_lo[:, l % UM], w_raw[:, u % 2, l % UM], w_hi[:, l % UM], ALU.subtract
                                  ).then_inc(lo_ready, 1)

            def steps(ph, groups, evac, peel_first=False):
                base = STEP0[ph]

                def body(it):
                    for l in range(8 * groups):
                        if not (isinstance(it, int) and base + 8 * groups * it + l + 2 in STOPS):
                            dve_lo(l + 2, groups * it, base)
                        evac(it, l)
                loop(dve, UNITS[ph] // (2 * groups), body, peel_first=peel_first, peel_last=ph == DOWN1)

            def scaled_out(ph, dst):
                def evac(it, l):
                    m = 8 * it + l
                    dve.wait_ge(step_done, STEP0[ph] + m + 1)
                    dst(it, l, m)
                return evac

            def stat_rstd(s):
                dve.wait_ge(std_ready, s + 1)
                dve.reciprocal(rstd, std).then_inc(rstd_ready, 1)
                dve.wait_ge(rstd_ready, s + 1)

            def norm_in(s, n, gain, layer, new=None, between=None):
                def low(m):
                    dve.wait_ge(xin_hi_ready, MT * n + m + 1)
                    dve.scalar_tensor_tensor(xin_lo[:, m], x[:, m], pcol(gain, layer * MT + m), xin_hi[:, m],
                                             ALU.mult, ALU.subtract).then_inc(xin_ready, 1)
                for m in range(MT):
                    if new:
                        new(m)
                        if m:
                            low(m - 1)
                    else:
                        low(m)
                if new:
                    low(MT - 1)
                if between:
                    between()
                stat_rstd(s)

            def residual(s, gain, layer):
                stat_rstd(s)
                order.after(dve.tensor_tensor(y, y, rstd.unsqueeze(1).to_broadcast([P, MT, T]), ALU.mult))

                def new(m):
                    dve.scalar_tensor_tensor(x[:, m], y[:, m], pcol(gain, layer * MT + m), x[:, m], ALU.mult, ALU.add
                                             ).then_inc(x_new, 1)
                    dve.wait_ge(x_new, 8 * ((s - 1) // 2) + m + 1)
                return new

            def mlp_up(ph, n):
                def evac(it, l):
                    m = 8 * it + l
                    dve.wait_ge(step_done, STEP0[ph] + m + 1)
                    if not (isinstance(it, int) and 32 * n + m < 2):
                        dve.wait_ge(relu2_ready, 32 * n + m - 1)
                    dve.scalar_tensor_tensor(relu[:, l % 2], ps[:, l % UM, 0:T], 0.0, rstd, ALU.max, ALU.mult
                                             ).then_inc(out_taken, 1)
                steps(ph, 1, evac, peel_first=True)

            dve.memset(tiny[:, 0:1], EPS).then_inc(tiny_ready, 1)
            dve.memset(tiny[:, 1:2], 1e-30).then_inc(tiny_ready, 1)
            dve.wait_ge(consts_in, 16 * 6)
            dve.wait_ge(x_in, 16)
            lam = par[:, AT["lru_lambda"]:AT["lru_lambda"] + MT]
            order.after(dve.tensor_scalar(lrut[:, 0], lam, -1.0, None, ALU.mult))
            dve.tensor_tensor(lrut[:, 1], lrut[:, 0], lam, ALU.max).then_inc(lam_v, 1)

            def first_steps():
                dve_lo(0, 0, 0)
                dve_lo(1, 0, 0)
            norm_in(0, 0, "g_mix_pre", 0, between=first_steps)
            dve.wait_ge(lam_a, 1)
            dve.tensor_scalar(lrut[:, 3], lrut[:, 2], 1.0, None, ALU.add).then_inc(lam_v, 1)
            dve.wait_ge(lam_a, 2)
            dve.wait_ge(lam_v, 2)
            order.after(dve.tensor_scalar(lrut[:, 3], lrut[:, 3], -1.0, None, ALU.add))
            order.after(dve.tensor_scalar(lrut[:, 5], lrut[:, 3], 0.0, None, ALU.is_equal))
            order.after(dve.tensor_tensor(lrut[:, 3], lrut[:, 3], lrut[:, 5], ALU.add))
            order.after(dve.reciprocal(lrut[:, 3], lrut[:, 3]))
            order.after(dve.tensor_tensor(lrut[:, 4], lrut[:, 4], lrut[:, 3], ALU.mult))
            order.after(dve.tensor_tensor(lrut[:, 4], lrut[:, 4], lrut[:, 5], ALU.add))
            order.after(dve.tensor_tensor(lrut[:, 4], lrut[:, 4], lrut[:, 2], ALU.mult))
            order.after(dve.scalar_tensor_tensor(lrut[:, 4], lrut[:, 0], 0.0, lrut[:, 4], ALU.max, ALU.add))
            order.after(dve.tensor_scalar(lrut[:, 6], lrut[:, 4], -LRU_C, None, ALU.mult))
            dve.tensor_scalar(lrut[:, 7], lrut[:, 4], LRU_C, None, ALU.mult).then_inc(lam_v, 1)


            def dst_ab(it, l, m):
                src = ps[:, l % UM, 0:T]
                if isinstance(it, int):
                    dve.tensor_tensor(xa[:, l, PAD:S0], src[:, 0:SEQ], rstd[:, 0:SEQ], ALU.mult)
                    dve.tensor_tensor(samples(xa[:, l], PAD, NT), seqs(src[:, SEQ:T]), seqs(rstd[:, SEQ:T]), ALU.mult
                                      ).then_inc(out_taken, 1)
                else:
                    dve.tensor_tensor(gaqkv[:, bass.ds(m - 8, 1)].rearrange("p a t -> p (a t)"), src, rstd, ALU.mult
                                      ).then_inc(out_taken, 1)

            dve.wait_ge(pads_ready, 2)
            steps(IN_AB, 1, scaled_out(IN_AB, dst_ab), peel_first=True)

            cos4 = cosr.unsqueeze(1).to_broadcast([ROT, 4, T])
            sin4 = sinr.unsqueeze(1).to_broadcast([ROT, 4, T])
            dve.wait_ge(out_taken, OUT0[OUT_AB])
            for r in range(4):
                w = (q, k)[r // 2][0:ROT, 4 * (r % 2):4 * (r % 2) + 4]
                dve.wait_ge(rot_ready, r + 1)
                dve.tensor_tensor(rot[0:ROT], ps[0:ROT, 4:8, 0:T], sin4, ALU.mult).then_inc(rot_taken, 1)
                order.after(dve.tensor_tensor(w, w, cos4, ALU.mult))
                dve.wait_ge(rot_taken, r + 1)
                dve.tensor_tensor(w, w, rot[0:ROT], ALU.add).then_inc(rope_done, 1)
                dve.wait_ge(rope_done, r + 1)

            order.mark(dve.tensor_copy(pack_a[:, :, 0:PAD], xa[:, :, SEQ:SEQ + PAD]))
            order.mark(dve.tensor_copy(pack_a[:, :, CW:].rearrange("p m (b c) -> p m b c", c=CW)[:, :, :, 0:PAD],
                                       samples(xa, NT, PAD)))
            for c in range(2):
                for j in reversed(range(CW)):
                    for m in range(HM):
                        src = xa[:, c * HM + m, j:j + CONV]
                        dst = xc[:, m, PAD:ROW]
                        wj = pcol("conv_a_w", j * MT + c * HM + m)
                        if j == CW - 1:
                            ins = dve.tensor_scalar(dst, src, wj, pcol("conv_a_b", c * HM + m), ALU.mult, ALU.add)
                        else:
                            ins = dve.scalar_tensor_tensor(dst, src, wj, dst, ALU.mult, ALU.add)
                        if j:
                            order.mark(ins)
                        else:
                            ins.then_inc(conv_ready, 1)
                    order.wait()
                dve.wait_ge(th_ready, c + 1)
                order.after(dve.tensor_scalar(hp[:, :, PAD:ROW], tp[:, :, PAD:ROW], 1.0, None, ALU.add))
                order.after(dve.reciprocal(hp[:, :, PAD:ROW], hp[:, :, PAD:ROW]))
                dve.scalar_tensor_tensor(tp[:, :, PAD:ROW], tp[:, :, PAD:ROW], 2.0, hp[:, :, PAD:ROW],
                                         ALU.mult, ALU.mult).then_inc(b_arg, 1)
                order.after(dve.tensor_tensor(ip[:, :, PAD:ROW], ip[:, :, PAD:ROW], xc[:, :, PAD:ROW], ALU.mult))
                dve.wait_ge(b_root, c + 1)
                order.after(dve.tensor_tensor(ip[:, :, PAD:ROW], ip[:, :, PAD:ROW], tp[:, :, PAD:ROW], ALU.mult))
                h0 = par[:, AT["h0"] + c * HM * NB:AT["h0"] + (c + 1) * HM * NB].rearrange("p (m b) -> p m b", b=NB)
                order.mark(dve.memset(rp[:, :, PAD - 1:PAD], 0.0))
                order.mark(dve.memset(ip[:, :, PAD - 1:PAD], 0.0))
                order.mark(dve.memset(samples(rp, PAD - 1, 1), 0.0))
                order.after(dve.tensor_copy(samples(ip, PAD - 1, 1)[:, :, :, 0], h0))
                for m in range(HM):
                    order.mark(dve.tensor_tensor_scan(hp[:, m, PAD - 1:ROW], rp[:, m, PAD - 1:ROW],
                                                      ip[:, m, PAD - 1:ROW], 0.0, ALU.mult, ALU.add))
                order.wait()
                order.mark(dve.tensor_copy(pack_a[:, c * HM:c * HM + HM, PAD], hp[:, :, S0 - 1]))
                dve.tensor_copy(pack_a[:, c * HM:c * HM + HM, CW:].rearrange("p m (b c) -> p m b c", c=CW)[:, :, :, PAD],
                                samples(hp, LONG - 1, 1)[:, :, :, 0]).then_inc(scanned, 1)
                dve.wait_ge(gelu_ready, c + 1)
                order.mark(dve.tensor_tensor(gg[:, :, 0:SEQ], hp[:, :, PAD:S0], gelu[:, :, 0:SEQ], ALU.mult))
                dve.tensor_tensor(gg[:, :, SEQ:T].rearrange("p m (b t) -> p m b t", t=NT), samples(hp, PAD, NT),
                                  gelu[:, :, SEQ:T].rearrange("p m (b t) -> p m b t", t=NT), ALU.mult
                                  ).then_inc(ya_full, 1)
                dve.wait_ge(ya_hi_ready, c + 1)
                dve.tensor_tensor(ya_lo[:, c * HM:c * HM + HM], gg, ya_hi[:, c * HM:c * HM + HM], ALU.subtract
                                  ).then_inc(ya_ready, 1)

            dve.wait_ge(masks_in, 32)
            for f in range(2):
                dve.wait_ge(kv_free, HALF_B * H * (f + 1))
                if f:
                    dve.wait_ge(spt_ready, 2)
                own = smask[:, NK + NS * f:NK + NS * f + NS]
                dve.scalar_tensor_tensor(sS[:, 0:NK // 2], ps[:, 2 * f, 0:NK // 2], HD ** -0.5, smask[:, 0:NK // 2],
                                         ALU.mult, ALU.add).then_inc(ss_taken, 1)
                dve.scalar_tensor_tensor(sS[:, NK // 2:NK], ps[:, 2 * f + 1, 0:NK // 2], HD ** -0.5,
                                         smask[:, NK // 2:NK], ALU.mult, ALU.add).then_inc(ss_taken, 1)
                dve.scalar_tensor_tensor(sS[:, NK:NKS], ps[:, 2 * f + 1, NK // 2:NK // 2 + NS], HD ** -0.5, own,
                                         ALU.mult, ALU.add).then_inc(ss_taken, 1)
                dve.wait_ge(ss_taken, 3 * f + 3)
                dve.tensor_reduce(att[:, f, 4:5], sS, axis=AX.X, op=ALU.max, negate=True).then_inc(smax_ready, 1)
                dve.wait_ge(sexp_ready, f + 1)
                order.after(dve.reciprocal(att[:, f, 6:7], att[:, f, 5:6]))
                dve.tensor_scalar(sS, sS, att[:, f, 6:7], None, ALU.mult).then_inc(sp_ready, 1)


            def prompt_softmax(h):
                f = h % 2
                dve.wait_ge(s_ready, h + 1)
                if h >= 2:
                    dve.wait_ge(pt_ready, h - 1)
                dve.scalar_tensor_tensor(pS[:, f], ps[:, 4 + f, 0:3 * P], HD ** -0.5, amask, ALU.mult, ALU.add
                                         ).then_inc(s_taken, 1)
                dve.wait_ge(s_taken, h + 1)
                order.mark(dve.tensor_reduce(att[:, f, 0:1], pS[:, f, 0:P], axis=AX.X, op=ALU.max, negate=True))
                dve.tensor_reduce(att[:, f, 1:2], pS[:, f, P:3 * P], axis=AX.X, op=ALU.max, negate=True
                                  ).then_inc(max_ready, 1)

            def prompt_scale(h):
                f = h % 2
                dve.wait_ge(exp_ready, h + 1)
                order.after(dve.reciprocal(att[:, f, 2:4], att[:, f, 2:4]))
                dve.tensor_scalar(pS[:, f, 0:P], pS[:, f, 0:P], att[:, f, 2:3], None, ALU.mult)
                dve.tensor_scalar(pS[:, f, P:3 * P], pS[:, f, P:3 * P], att[:, f, 3:4], None, ALU.mult
                                  ).then_inc(p_ready, 1)

            def prompt_low(h):
                f = h % 2
                dve.wait_ge(yb_hi_ready, h + 1)
                dve.tensor_tensor(yb_lo[:, h, 0:SEQ], ps[:, 7, SEQ * f:SEQ * f + SEQ], yb_hi[:, h, 0:SEQ], ALU.subtract
                                  ).then_inc(yb_ready, 1)

            prompt_softmax(0)
            for h in range(H):
                prompt_scale(h)
                if h + 1 < H:
                    prompt_softmax(h + 1)
                if h:
                    prompt_low(h - 1)
            prompt_low(H - 1)

            dve.wait_ge(yb_hi_ready, H + 1)
            dve.tensor_tensor(yb_lo[:, :, SEQ:T], ps[:, 6, 0:H * NS].rearrange("p (h t) -> p h t", h=H),
                              yb_hi[:, :, SEQ:T], ALU.subtract).then_inc(yb_ready, 1)

            steps(OUT_AB, 1, lambda it, l: None)
            norm_in(2, 1, "g_ffn_pre", 0, residual(1, "g_mix_post", 0))
            mlp_up(UP0, 0)
            steps(DOWN0, 2, lambda it, l: None)
            norm_in(4, 2, "g_mix_pre", 1, residual(3, "g_ffn_post", 0))

            def dst_c(it, l, m):
                src = ps[:, l % UM, 0:T]
                if isinstance(it, int) and it < 2:
                    dve.tensor_tensor(xm[:, m, PAD:S0], src[:, 0:SEQ], rstd[:, 0:SEQ], ALU.mult)
                    dve.tensor_tensor(samples(xm[:, m], PAD, NT), seqs(src[:, SEQ:T]), seqs(rstd[:, SEQ:T]), ALU.mult)
                    dve.tensor_tensor(xms[:, m], src[:, SEQ:T], rstd[:, SEQ:T], ALU.mult).then_inc(out_taken, 1)
                else:
                    dve.tensor_tensor(z[:, bass.ds(m - CT, 1)].rearrange("p a t -> p (a t)"), src, rstd, ALU.mult
                                      ).then_inc(out_taken, 1)

            dve.wait_ge(xm_pads, 2)
            base = STEP0[IN_C]

            def body_c(it):
                for l in range(8):
                    if not (isinstance(it, int) and base + 8 * it + l + 2 in STOPS):
                        dve_lo(l + 2, it, base)
                    m = 8 * it + l
                    dve.wait_ge(step_done, base + m + 1)
                    dst_c(it, l, m)
                    if m >= CT:
                        conv_rest(m - CT)
            def conv_rest(m):
                dst = convt[:, m % 4, 0:CONV]
                dve.wait_ge(conv0_ready, m + 1)
                for j in reversed(range(CW - 1)):
                    ins = dve.scalar_tensor_tensor(dst, xm[:, m, j:j + CONV], pcol("conv_c_w", j * CT + m), dst,
                                                   ALU.mult, ALU.add)
                    if j:
                        order.after(ins)
                    else:
                        ins.then_inc(convc_ready, 1)

            for it in range(UNITS[IN_C] // 2):
                body_c(it)

            dve.wait_ge(fold_zero, 1)
            dve.wait_ge(bdT_used, 1)
            for c0 in (0, 32):
                dve.tensor_copy(fold[:, :, c0:c0 + NH], ps[:, 5, 0:2 * CT * 8].rearrange("p (m g) -> p m g", g=8)
                                [:, :, NH * (c0 // 32):NH * (c0 // 32) + NH]).then_inc(fold_ready, 1)
            dve.wait_ge(xcc_ready, CT)
            dve.tensor_copy(xcs3.rearrange("p m (r t) -> p m r t", r=3),
                            xcc[:, :, SEQ:T].unsqueeze(2).to_broadcast([P, CT, 3, NS])).then_inc(tok3_ready, 1)
            dve.tensor_copy(xms3.rearrange("p m (r t) -> p m r t", r=3),
                            xms.unsqueeze(2).to_broadcast([P, CT, 3, NS])).then_inc(tok3_ready, 1)
            order.mark(dve.tensor_copy(pack_c[:, :, 0:PAD], xm[:, :, SEQ:SEQ + PAD]))
            order.mark(dve.tensor_copy(pack_c[:, :, PAD:].rearrange("p m (b c) -> p m b c", c=PAD), samples(xm, NT, PAD)))

            dve.wait_ge(xcc_ready, CT)
            order.mark(dve.memset(gi, 0.0))
            order.mark(dve.memset(gb, 0.0))
            dve.memset(gf, 0.0).then_inc(gv, 1)
            m0 = gsml[:, 2:2 + NB]
            dve.wait_ge(gact, 1)
            dve.scalar_tensor_tensor(gt[:, PAD:ROW], gf[:, PAD:ROW], -1.0, gf[:, PAD:ROW], ALU.mult, ALU.max
                                     ).then_inc(gv, 1)
            dve.wait_ge(gact, 2)
            order.after(dve.scalar_tensor_tensor(gf[:, PAD:ROW], gf[:, PAD:ROW], 0.0, gt[:, PAD:ROW],
                                                 ALU.min, ALU.subtract))
            keep = ghist[:, 0:ROW]
            push = ghist[:, ROW:2 * ROW]
            order.mark(dve.memset(keep, 1.0))
            order.after(dve.memset(push, 0.0))
            order.mark(dve.memset(keep[:, PAD:PAD + 1], 0.0))
            order.mark(dve.memset(samples(keep, PAD, 1), 0.0))
            order.mark(dve.memset(push[:, PAD - 1:PAD], NEG))
            order.after(dve.memset(samples(push, PAD - 1, 1), NEG))
            order.after(dve.tensor_tensor_scan(gb[:, PAD:ROW], keep[:, PAD:ROW], gf[:, PAD:ROW], 0.0, ALU.mult, ALU.add))
            order.after(dve.tensor_tensor(gi[:, PAD:ROW], gi[:, PAD:ROW], gb[:, PAD:ROW], ALU.subtract))
            order.after(dve.tensor_copy(samples(gi, PAD - 1, 1)[:, :, 0], m0))
            order.after(dve.tensor_tensor_scan(gt[:, PAD - 1:ROW], push[:, PAD - 1:ROW], gi[:, PAD - 1:ROW], 0.0,
                                               ALU.add, ALU.max))
            gM, g = gt, gi
            ens = slice(R_ENS, R_ENS + NS)
            nms = slice(R_NEGMS, R_NEGMS + NS)
            order.mark(dve.tensor_scalar(rows[:, R_NEGM:R_NEGM + SEQ], gM[:, PAD:S0], -1.0, None, ALU.mult))
            order.mark(dve.tensor_scalar(seqs(rows[:, nms]), samples(gM, PAD, NT), -1.0, None, ALU.mult))
            order.mark(dve.tensor_copy(gg_c[:, 0:SEQ], g[:, PAD:S0]))
            order.mark(dve.tensor_copy(seqs(gg_c[:, SEQ:T]), samples(g, PAD, NT)))
            order.wait()
            order.mark(dve.tensor_tensor(rows[:, R_EN:R_EN + SEQ], rows[:, R_NEGM:R_NEGM + SEQ], gb[:, PAD:S0], ALU.subtract))
            order.mark(dve.tensor_tensor(seqs(rows[:, ens]), seqs(rows[:, nms]), samples(gb, PAD, NT), ALU.subtract))
            m0_t = m0.unsqueeze(2).to_broadcast([NH, NB, NT])
            order.mark(dve.tensor_tensor(seqs(rows[:, R_INTER:R_INTER + NS]), m0_t, samples(gM, PAD, NT), ALU.subtract))
            order.mark(dve.tensor_tensor(rows[:, R_DECAY:R_DECAY + NB], m0, samples(gM, LONG - 1, 1)[:, :, 0], ALU.subtract))
            order.mark(dve.tensor_scalar(gw_c[:, 0:SEQ], gg_c[:, 0:SEQ], gM[:, S0 - 1:S0], None, ALU.subtract))
            for i in range(3):
                order.mark(dve.tensor_tensor(seqs(gw_c[:, SEQ + NS * i:SEQ + NS * i + NS]), seqs(gg_c[:, SEQ:T]),
                                             samples(gM, LONG - 1, 1).to_broadcast([NH, NB, NT]), ALU.subtract))
            order.mark(dve.tensor_tensor(pack_m[:, 0:1], gM[:, S0 - 1:S0], gb[:, S0 - 1:S0], ALU.add))
            dve.tensor_tensor(pack_m[:, 1:1 + NB], samples(gM, LONG - 1, 1)[:, :, 0],
                              samples(gb, LONG - 1, 1)[:, :, 0], ALU.add).then_inc(gv, 1)

            def staged_v(h, name):
                u = use(h, name)
                dve.wait_ge(stage_full, u + 1)
                return ps[:, 6 + u % 2]

            def keys_low(h):
                dve.wait_ge(kst_hi_ready, h + 1)
                q2 = slice(2 * NS, 3 * NS)
                dve.scalar_tensor_tensor(kst[q2, h % 2], staged_v(h, "ks")[q2], w3[q2, h:h + 1], kst[q2, h % 2],
                                         ALU.mult, ALU.subtract).then_inc(stage_read_v, 1)

            def values_low(h):
                dve.wait_ge(vst_hi_ready, h + 1)
                q1 = slice(NS, 2 * NS)
                dve.tensor_tensor(vst[q1, h % 2], staged_v(h, "vs")[q1], vst[q1, h % 2], ALU.subtract
                                  ).then_inc(stage_read_v, 1)

            def queries(h):
                dve.wait_ge(stage_read_a, reads(use(h, "bc1"))[1])
                inter = bc[:, h % 2, R_INTER:R_INTER + NS].unsqueeze(1).to_broadcast([P, ET, NS])
                order.after(dve.tensor_tensor(qn, qf[:, :, SEQ:T], inter, ALU.mult))
                if h == 0:
                    dve.wait_ge(qz1_zero, 1)
                for e in range(ET):
                    most, last = qz_own(h, e)
                    order.mark(dve.tensor_copy(most, seqs(qn[:, e, 0:NS - NT])))
                    order.mark(dve.tensor_copy(last, qn[:, e, NS - NT:NS]))
                order.wait()
                n0_t = n0_of(h).unsqueeze(2).to_broadcast([P, ET * NB, NT])
                qn_t = qn.rearrange("p e (b t) -> p (e b) t", t=NT)
                dve.tensor_tensor(qn_t, qn_t, n0_t, ALU.mult).then_inc(qs_ready, 1)

            def arguments(h):
                negm = bc[:, h % 2, R_NEGM:R_NEGM + SEQ]
                order.mark(dve.tensor_tensor(ew[:, 0:P], negm[:, 0:P], tri, ALU.add))
                order.mark(dve.tensor_copy(ew[:, P:2 * P], negm[:, P:2 * P]))
                order.mark(dve.tensor_tensor(ew[:, 2 * P:3 * P], negm[:, P:2 * P], tri, ALU.add))
                dve.tensor_tensor(ew[0:NS, 3 * P:3 * P + NS], bc[0:NS, h % 2, R_NEGMS:R_NEGMS + NS], stri, ALU.add
                                  ).then_inc(ew_arg, 1)

            def weights(h):
                dve.wait_ge(ew_exp, h + 1)
                sc = staged_v(h, "sc")
                order.mark(dve.tensor_tensor(ew[:, 0:3 * P], ew[:, 0:3 * P], sc[:, 0:3 * P], ALU.mult))
                dve.tensor_tensor(ew[0:NS, 3 * P:3 * P + NS], ew[0:NS, 3 * P:3 * P + NS], sc[0:NS, 3 * P:3 * P + NS],
                                  ALU.mult).then_inc(stage_read_v, 1)

            def n0_of(h):
                return par[:, AT["n0"] + h * ET * NB:AT["n0"] + (h + 1) * ET * NB]

            def new_n(h):
                decay = bc[:, h % 2, R_DECAY:R_DECAY + NB]
                pn = staged_v(h, "n")[:, 0:ET * (NB + 2)].rearrange("p (e b) -> p e b", b=NB + 2)
                kn = pack_n[:, h * ET:(h + 1) * ET]
                order.mark(dve.tensor_copy(kn[:, :, 0:1], pn[:, :, NB:NB + 1]))
                order.after(dve.tensor_tensor(kn[:, :, 1:], n0_of(h).rearrange("p (e b) -> p e b", b=NB),
                                              decay.unsqueeze(1).to_broadcast([P, ET, NB]), ALU.mult))
                dve.tensor_tensor(kn[:, :, 1:], kn[:, :, 1:], pn[:, :, 0:NB], ALU.add).then_inc(stage_read_v, 1)

            def new_state(h, b, half):
                i = item(h, b, half)
                s = i % C_SLOTS
                dve.wait_ge(c_mm, i + 1)
                if b < NB:
                    dve.wait_ge(c_in[s], 16 * loads(i))
                    for e in range(HD2):
                        last = dve.scalar_tensor_tensor(cring[:, s, e], cring[:, s, e],
                                                        bc[:, h % 2, R_DECAY + b:R_DECAY + b + 1], ps[:, e, :],
                                                        ALU.mult, ALU.add)
                else:
                    if i >= C_SLOTS:
                        dve.wait_ge(c_out[s], 16 * (i // C_SLOTS))
                    for e in range(HD2):
                        last = dve.tensor_copy(cring[:, s, e], ps[:, e, :])
                last.then_inc(c_new, 1)

            def chunk(h, b):
                if b == 0:
                    dve.wait_ge(den_abs, h + 1)
                    order.after(dve.tensor_tensor(dn, dn, bc[:, h % 2, R_EN:R_EN + SEQ], ALU.max))
                    order.after(dve.reciprocal(dn, dn))
                    dve.wait_ge(num_psum, h + 1)
                    dve.tensor_tensor(hT, ps[:, 4:6, :].rearrange("p a (c t) -> p (a c) t", t=SEQ),
                                      dn.unsqueeze(1).to_broadcast([P, ET, SEQ]), ALU.mult).then_inc(h_ready, 1)
                if b == 1:
                    new_n(h)
                if b == 2:
                    new_state(h, NB, 0)
                if b == 3:
                    new_state(h, NB, 1)
                if b == 4:
                    dve.wait_ge(stage_read_a, reads(use(h, "mean"))[1])
                    order.after(dve.reciprocal(dn, dn))
                    for e in range(ET):
                        order.mark(dve.scalar_tensor_tensor(hT[:, e], hT[:, e], pcol("norm_w", ET * h + e), dn,
                                                            ALU.mult, ALU.mult))
                if b == 5:
                    order.wait()
                    for e in range(ET):
                        m = ET * h + e
                        order.mark(dve.scalar_tensor_tensor(hT[:, e], xcc[:, m, 0:SEQ], pcol("skip", m), hT[:, e],
                                                            ALU.mult, ALU.add))
                    if h + 1 < NH:
                        keys_low(h + 1)
                    order.wait()
                    dve.tensor_tensor(hT, hT, z[:, ET * h:ET * h + ET, 0:SEQ], ALU.mult).then_inc(y1_full, 1)
                if b == 6 and h + 1 < NH:
                    values_low(h + 1)
                if b == 7:
                    dve.wait_ge(y1_hi_ready, h + 1)
                    dve.tensor_tensor(y1_lo[:, ET * h:ET * h + ET, 0:SEQ], hT, y1_hi[:, ET * h:ET * h + ET, 0:SEQ],
                                      ALU.subtract).then_inc(y1_ready, 1)
                    if h + 1 < NH:
                        queries(h + 1)
                        arguments(h + 1)
                        weights(h + 1)

            dve.wait_ge(gcol_taken, 1)
            dve.wait_ge(z_ready, 1)
            keys_low(0)
            values_low(0)
            queries(0)
            arguments(0)
            weights(0)
            for h in range(NH):
                for b in range(NB):
                    for half in range(2):
                        new_state(h, b, half)
                    chunk(h, b)
            order.after(dve.tensor_tensor(stok[:, 2], stok[:, 0], tokg_s[:, 1], ALU.max))
            order.after(dve.reciprocal(stok[:, 2], stok[:, 2]))
            dve.wait_ge(hs_sq, NH)
            order.after(dve.tensor_tensor(stok[:, 3], stok[:, 1], stok[:, 2], ALU.mult))
            dve.tensor_tensor(stok[:, 3], stok[:, 3], stok[:, 2], ALU.mult).then_inc(hs_mean, 1)
            dve.wait_ge(hs_std, 1)
            order.after(dve.reciprocal(stok[:, 3], stok[:, 3]))
            order.after(dve.tensor_tensor(stok[:, 4], stok[:, 3], stok[:, 2], ALU.mult))
            for h in range(NH):
                dve.tensor_scalar(hs[:, h], hs[:, h], stok[:, 4, h:h + 1], None, ALU.mult).then_inc(hs_scaled, 1)
            norm_w = par[:, AT["norm_w"]:AT["norm_w"] + CT].unsqueeze(2).to_broadcast([P, CT, NS])
            skip = par[:, AT["skip"]:AT["skip"] + CT].unsqueeze(2).to_broadcast([P, CT, NS])
            xs = xcc[:, :, SEQ:T]
            order.mark(dve.tensor_tensor(xs, xs, skip, ALU.mult))
            dve.wait_ge(hst_ready, 1)
            order.after(dve.tensor_tensor(hs_f, ps[:, 2, :].rearrange("p (m t) -> p m t", t=NS), norm_w, ALU.mult))
            order.after(dve.tensor_tensor(hs_f, hs_f, xs, ALU.add))
            dve.tensor_tensor(hs_f, hs_f, z[:, :, SEQ:T], ALU.mult).then_inc(y1s_full, 1)
            dve_lo(0, 0, STEP0[OUT_C])
            dve_lo(1, 0, STEP0[OUT_C])
            dve.wait_ge(y1s_hi, 1)
            dve.tensor_tensor(y1_lo[:, :, SEQ:T], hs_f, y1_hi[:, :, SEQ:T], ALU.subtract).then_inc(y1_ready, 1)

            steps(OUT_C, 1, lambda it, l: None)
            norm_in(6, 3, "g_ffn_pre", 1, residual(5, "g_mix_post", 1))
            mlp_up(UP1, 1)
            steps(DOWN1, 2, lambda it, l: None)
            last_new = residual(7, "g_ffn_post", 1)
            for m in range(MT):
                last_new(m)

        @block.gpsimd
        def _(pool):
            order = Tally(pool, p_order)

            def square_sums(s):
                for m in range(MT):
                    if m == 0 and s:
                        pool.wait_ge(mean_ready, s)
                    pool.wait_ge(sq_ready, 8 * s + m + 1)
                    if m == 0:
                        pool.tensor_copy(sqsum, sq[:, 0]).then_inc(sq_added, 1)
                    else:
                        pool.wait_ge(sq_added, 8 * s + m)
                        pool.tensor_tensor(sqsum, sqsum, sq[:, m % 2], ALU.add).then_inc(sq_added, 1)

            def hidden_low(n):
                def body(it):
                    for l in range(2):
                        m = 2 * it + l
                        pool.wait_ge(hid_hi_ready, 32 * n + m + 1)
                        pool.tensor_tensor(hid_lo[:, bass.ds(m, 1)].rearrange("p a t -> p (a t)"), relu2[:, l],
                                           hid_hi[:, bass.ds(m, 1)].rearrange("p a t -> p (a t)"), ALU.subtract
                                           ).then_inc(hid_ready, 1)
                with pool.Fori(0, 16) as it:
                    body(it)

            pool.memset(lruw, 0.0).then_inc(lruw_zero, 1)
            pool.wait_ge(consts_in, 16 * 6)
            order.mark(pool.memset(xa[:, :, 0:PAD], 0.0))
            order.mark(pool.memset(qz, 0.0))
            order.wait()
            pool.tensor_copy(samples(xa, 0, PAD), par[:, AT["conv_a0"]:AT["conv_a0"] + MT * NB * PAD].rearrange(
                "p (m b c) -> p m b c", b=NB, c=PAD)).then_inc(pads_ready, 2)
            square_sums(0)
            pool.wait_ge(rope_done, 2)
            for b in range(NB):
                if b >= 2:
                    pool.wait_ge(kv_free, H * (b - 1))
                pool.tensor_copy(qz_diag[:, b % 2], q[:, :, SEQ + NT * b:SEQ + NT * b + NT]).then_inc(qz_ready, 1)
            square_sums(1)
            square_sums(2)
            hidden_low(0)
            square_sums(3)
            pool.wait_ge(step_done, STEP0[IN_C])
            order.mark(pool.memset(xm[:, :, 0:PAD], 0.0))
            order.wait()
            pool.tensor_copy(samples(xm, 0, PAD), par[:, AT["conv_c0"]:AT["conv_c0"] + CT * NB * PAD].rearrange(
                "p (m b c) -> p m b c", b=NB, c=PAD)).then_inc(xm_pads, 2)
            square_sums(4)
            pool.wait_ge(consts_c_in, 16 * 8)
            pool.memset(fold, 0.0).then_inc(fold_zero, 1)

            def diagonal(dst, which, m):
                return pool.tensor_tensor(dst.rearrange("p (i o) -> p i o", o=QB),
                                          qkvw[:, which, m:m + 1].to_broadcast([P, P // QB, QB]),
                                          bmask.rearrange("p (i o) -> p i o", o=QB), ALU.mult)

            for m in range(CT):
                for i in range(3):
                    diagonal(bdT[:, 3 * m + i], 3 + i, m).then_inc(bdT_ready, 1)
            pool.wait_ge(step_done, STEP0[OUT_C])
            pool.memset(qz1, 0.0).then_inc(qz1_zero, 1)

            def head_diagonals(h):
                for i in range(3):
                    for e in range(ET):
                        ins = diagonal(bd[:, 3 * ET * (h % 2) + ET * i + e], i, ET * h + e)
                    ins.then_inc(bd_ready, 1)

            head_diagonals(0)
            for h in range(1, NH):
                if h >= 2:
                    pool.wait_ge(stage_full, use(h - 2, "vs") + 1)
                head_diagonals(h)
            square_sums(5)
            square_sums(6)
            hidden_low(1)
            square_sums(7)

        @block.tensor
        def _(pe):
            def step(ph, g, l, parts, start, stop, first=None, o=None):
                pe.wait_ge(lo_ready, g + 1)
                if start and o is not None:
                    pe.wait_ge(out_taken, o - UM + 1)
                j = l % UM
                for kk in range(UK):
                    if first:
                        first(kk)
                    hi, lo = parts(kk)
                    ws = slice(kk * P, kk * P + P)
                    pe.matmul(ps[:, j, 0:T], w_hi[:, j, ws], hi, start=start and kk == 0, stop=False)
                    pe.matmul(ps[:, j, 0:T], w_hi[:, j, ws], lo, start=False, stop=False)
                    last = pe.matmul(ps[:, j, 0:T], w_lo[:, j, ws], hi, start=False, stop=stop and kk == UK - 1)
                last.then_inc(step_done, 1)

            def steps(ph, per, parts, after_first=None, first=None, peel=True):
                groups = max(1, per // 2)

                def body(it):
                    if ph == IN_C and isinstance(it, int) and it:
                        fold_gates()
                    for l in range(8 * groups):
                        u = l // UM
                        kg = u % per
                        o = None
                        if kg == 0:
                            n = (8 // per * groups) * it + UM * (u // per) + l % UM
                            o = OUT0[ph] + n
                            if isinstance(o, int) and o < UM:
                                o = None
                        here = isinstance(it, int) and it == 0
                        step(ph, STEP0[ph] + 8 * groups * it + l, l, lambda kk: parts(UK * kg + kk),
                             kg == 0, kg == per - 1, first if here and l == 0 else None, o)
                        if here and l == 0 and after_first:
                            after_first()
                loop(pe, UNITS[ph] // (2 * groups), body, peel_first=peel, peel_last=ph == IN_C)

            def mean(s):
                pe.wait_ge(sq_added, 8 * s + 8)
                if s:
                    pe.wait_ge(std_ready, s)
                pe.matmul(ps[:, 7, 0:T], ones, sqsum, start=True, stop=True).then_inc(mean_ready, 1)

            def fold_gates():
                pe.wait_ge(consts_c_in, 16 * 8)
                for m in range(CT):
                    pe.wait_ge(bdT_ready, 3 * m + 3)
                    for i in range(3):
                        c0 = 8 * m if i < 2 else 8 * (CT + m)
                        last = pe.matmul(ps[:, 5, c0:c0 + 8], bdT[:, 3 * m + i], wgate[:, i * CT + m],
                                         start=i != 1, stop=i >= 1)
                last.then_inc(bdT_used, 1)

            def from_norm(ph, n, s):
                steps(ph, 1, lambda kk: (xin_hi[:, kk], xin_lo[:, kk]), after_first=lambda: mean(s),
                      first=lambda kk: pe.wait_ge(xin_ready, MT * n + kk + 1))

            pe.wait_ge(consts_in, 16 * 6)
            from_norm(IN_AB, 0, 0)

            pe.wait_ge(out_taken, OUT0[OUT_AB])
            pe.wait_ge(std_ready, 1)
            for r in range(4):
                if r:
                    pe.wait_ge(rot_taken, r)
                w = (q, k)[r // 2]
                for i in range(4):
                    last = pe.matmul(ps[0:ROT, 4 + i, 0:T], rotm, w[0:ROT, 4 * (r % 2) + i], start=True, stop=True)
                last.then_inc(rot_ready, 1)

            def lru_gates(c, g):
                pe.wait_ge(conv_ready, HM * (c + 1))
                if c or g:
                    pe.wait_ge(gates_taken, HM * (2 * c + g))
                for m in range(HM):
                    last = pe.matmul(ps[:, 4 + m, 0:CONV], lruw[:, g * MT + c * HM + m], xc[:, m, PAD:ROW],
                                     start=True, stop=True)
                last.then_inc(gates_ready, 1)

            def sample_scores(b):
                f, rows4 = divmod(b, HALF_B)
                part = slice(32 * rows4, 32 * rows4 + 32)
                pe.wait_ge(qz_ready, b + 1)
                for h in range(H):
                    i = b * H + h
                    s = i % KV_SLOTS
                    pe.wait_ge(kv_in[s], 16 * (i // KV_SLOTS + 1))
                    lhs = qz_of[:, b % 2, h]
                    for c in range(2):
                        pe.matmul(ps[part, 2 * f + c, 0:NK // 2], lhs, kv[:, s, c * NK // 2:(c + 1) * NK // 2],
                                  start=h == 0, stop=h == H - 1, skip_group_check=True)
                    pe.matmul(ps[part, 2 * f + 1, NK // 2:NK // 2 + NS], lhs, k[:, h, SEQ:T],
                              start=False, stop=h == H - 1, skip_group_check=True).then_inc(kv_free, 1)

            pe.wait_ge(lruw_in, 16 * 4)
            pe.wait_ge(rot_taken, 4)
            pe.wait_ge(rope_done, 4)
            for b in range(NB):
                sample_scores(b)
                if b < 2:
                    lru_gates(0, b)
                if b in (4, 5):
                    lru_gates(1, b - 4)

            pe.wait_ge(gates_taken, 4 * HM)
            for r in range(6):
                tt, half = divmod(r, 2)
                n = P if tt < 2 else NS
                if r >= 4:
                    pe.wait_ge(vt_taken, r - 3)
                for i in range(4):
                    last = pe.transpose(ps[0:n, 4 + r % 4, P * i:P * i + P], v[:, 4 * half + i, P * tt:P * tt + n], ident)
                last.then_inc(vt_ready, 1)

            pe.wait_ge(vt_taken, 6)
            for f in range(2):
                pe.wait_ge(sp_ready, f + 1)
                if f:
                    pe.wait_ge(spt_taken, 3)
                for kt in range(KT + 1):
                    n = P if kt < KT else NS
                    last = pe.transpose(ps[0:n, 4 + kt // 4, P * (kt % 4):P * (kt % 4) + P], sS[:, P * kt:P * kt + n], ident)
                    if kt % 4 == 3:
                        last.then_inc(spt_ready, 1)

            def sample_values(n):
                b, h = divmod(n, H)
                f, b4 = divmod(b, HALF_B)
                c0 = P * f + 32 * b4
                if h == b4 == 0:
                    for half in range(2):
                        pe.matmul(ps[:, 2 * f + half, :], pT[0:NS, KT, P * f:P * f + P],
                                  vtok[0:NS, 2, 512 * half:512 * half + 512], start=True, stop=False,
                                  skip_group_check=True)
                i = NB * H + n
                s = i % KV_SLOTS
                pe.wait_ge(kv_in[s], 16 * (i // KV_SLOTS + 1))
                out = ps[32 * b4:32 * b4 + 32, 2 * f + h // 4, HD * (h % 4):HD * (h % 4) + HD]
                for kt in range(KT):
                    last = pe.matmul(out, pT[:, kt, c0:c0 + 32], kv[:, s, P * kt:P * kt + P],
                                     start=False, stop=kt == KT - 1, skip_group_check=True)
                last.then_inc(kv_free, 1)

            pe.wait_ge(spt_taken, 6)

            def prompt_scores(h):
                f = h % 2
                if h >= 2:
                    pe.wait_ge(s_taken, h - 1)
                pe.matmul(ps[:, 4 + f, 0:P], q[:, h, 0:P], k[:, h, 0:P], start=True, stop=True)
                pe.matmul(ps[:, 4 + f, P:3 * P], q[:, h, P:SEQ], k[:, h, 0:SEQ], start=True, stop=True
                          ).then_inc(s_ready, 1)

            prompt_scores(0)
            for h in range(H):
                f = h % 2
                if h + 1 < H:
                    prompt_scores(h + 1)
                for n in range(4):
                    sample_values(NB * h + n)
                pe.wait_ge(p_ready, h + 1)
                if h:
                    pe.wait_ge(pt_taken, h)
                for i in range(3):
                    last = pe.transpose(ps[:, 6, P * i:P * i + P], pS[:, f, P * i:P * i + P], ident)
                last.then_inc(pt_ready, 1)
                for n in range(4, NB):
                    sample_values(NB * h + n)
                pe.wait_ge(pt_taken, h + 1)
                if h:
                    pe.wait_ge(yb_ready, h)
                out = ps[:, 7, SEQ * f:SEQ * f + SEQ]
                own = slice(HD * h, HD * h + HD)
                pe.matmul(out[:, 0:P], vtok[:, 0, own], pTp[:, f, 0:P], start=True, stop=True)
                pe.matmul(out[:, P:SEQ], vtok[:, 0, own], pTp[:, f, P:2 * P], start=True, stop=False)
                pe.matmul(out[:, P:SEQ], vtok[:, 1, own], pTp[:, f, 2 * P:3 * P], start=False, stop=True
                          ).then_inc(pv_ready, 1)

            for f in range(2):
                pe.wait_ge(spv_taken, f + 1)
                for h in range(H):
                    last = pe.matmul(ps[:, 6, NS * h + NS // 2 * f:NS * h + NS // 2 * (f + 1)],
                                     pvs[:, HD * h:HD * h + HD],
                                     ident.rearrange("p (b c) -> p b c", c=32)[:, :, NT * h:NT * h + NT],
                                     start=True, stop=True)
                last.then_inc(syb_ready, 1)

            def ab(kk):
                return (ya_hi[:, kk], ya_lo[:, kk]) if kk < MT else (yb_hi[:, kk - MT], yb_lo[:, kk - MT])

            pe.wait_ge(yb_ready, H + 1)
            pe.wait_ge(ya_ready, 2)
            steps(OUT_AB, 2, ab, peel=False)
            mean(1)
            from_norm(UP0, 1, 2)
            pe.wait_ge(hid_ready, 32)
            steps(DOWN0, 4, lambda kk: (hid_hi[:, kk], hid_lo[:, kk]), peel=False)
            mean(3)
            from_norm(IN_C, 2, 4)

            pe.wait_ge(fold_ready, 2)
            pe.wait_ge(xcc_ready, CT)
            g = ps[0:GH, 4, :]
            for m in range(CT):
                pe.matmul(g[:, 0:T], fold[:, m], xcc[:, m], start=m == 0, stop=False, skip_group_check=True)
                pe.matmul(g[:, 0:SEQ], fold[:, CT + m], xm[:, m, PAD:S0], start=False, stop=False, skip_group_check=True)
                last = pe.matmul(g[:, SEQ:T], fold[:, CT + m], xms[:, m], start=False, stop=m == CT - 1,
                                 skip_group_check=True)
            last.then_inc(g_ready, 1)
            def staged(h, name):
                u = use(h, name)
                if u >= 2:
                    pe.wait_ge(*reads(u - 2))
                return ps[:, 6 + u % 2]

            def weights_of(h, i, e):
                return bd[:, 3 * ET * (h % 2) + ET * i + e]

            def qk(h):
                pe.wait_ge(bd_ready, 3 * h + 3)
                for i, name in enumerate("qk"):
                    for e in range(ET):
                        pe.matmul(staged(h, f"{name}{e}")[:, 0:T], weights_of(h, i, e), xcc[:, ET * h + e],
                                  start=True, stop=True).then_inc(stage_full, 1)

            def by_token(h, name, i, lhs):
                out = staged(h, name)
                for e in range(ET):
                    rows_of = lhs(ET * h + e)
                    n = rows_of.shape[1]
                    last = pe.matmul(out[0:n, P * e:P * e + P], rows_of, weights_of(h, i, e), start=True, stop=True)
                last.then_inc(stage_full, 1)

            def keys_by_token(h):
                for tt in range(2):
                    by_token(h, f"kt{tt}", 1, lambda m: xcc[:, m, P * tt:P * tt + P])
                by_token(h, "ks", 1, lambda m: xcs3[:, m])

            pe.wait_ge(tok3_ready, 2)
            qk(0)
            keys_by_token(0)
            pe.wait_ge(gact, 3)
            four = ident[0:NH, 0:NH]
            for tt in range(2):
                for i, src in enumerate((gg_c, gw_c)):
                    c0 = 2 * NH * tt + NH * i
                    pe.transpose(ps[:, 5, c0:c0 + NH], src[:, P * tt:P * tt + P], four)
            pe.transpose(ps[0:NS, 5, 4 * NH:5 * NH], gg_c[:, SEQ:T], four)
            pe.transpose(ps[0:NS, 5, 5 * NH:6 * NH], rows[:, R_ENS:R_ENS + NS], four)
            pe.transpose(ps[0:3 * NS, 5, 6 * NH:7 * NH], gw_c[:, SEQ:SEQ + 3 * NS], four).then_inc(gcol_ready, 1)

            def values_by_token(h):
                for tt in range(2):
                    by_token(h, f"vt{tt}", 2, lambda m: xm[:, m, PAD + P * tt:PAD + P * tt + P])
                by_token(h, "vs", 2, lambda m: xms3[:, m])

            def head_rows(h):
                hsel = sel[:, P * h:P * h + P]
                pe.matmul(staged(h, "bc0"), hsel, rows[:, 0:512], start=True, stop=True).then_inc(stage_full, 1)
                pe.matmul(staged(h, "bc1")[:, 0:NBC - 512], hsel, rows[:, 512:NBC], start=True, stop=True
                          ).then_inc(stage_full, 1)

            def scores(h):
                pe.wait_ge(stage_read_a, reads(use(h, "k3"))[1])
                out = staged(h, "sc")
                for lo, hi, ks, c0 in ((0, SEQ, 0, 0), (P, SEQ, P, 2 * P)):
                    for e in range(ET):
                        pe.matmul(out[:, c0:c0 + hi - lo], kf[:, e, ks:ks + P], qf[:, e, lo:hi],
                                  start=e == 0, stop=e == ET - 1)
                for e in range(ET):
                    last = pe.matmul(out[0:NS, 3 * P:3 * P + NS], kf[:, e, SEQ:T], qf[:, e, SEQ:T],
                                     start=e == 0, stop=e == ET - 1)
                last.then_inc(stage_full, 1)

            def denominators(h):
                if h:
                    pe.wait_ge(den_abs, h)
                pe.wait_ge(stage_read_v, reads(use(h, "sc"))[1])
                pe.wait_ge(qs_ready, h + 1)
                den = ps[:, 3, :]
                pe.matmul(den[:, 0:SEQ], ones, ew[:, 0:2 * P], start=True, stop=False, skip_group_check=True)
                pe.matmul(den[:, P:SEQ], ones, ew[:, 2 * P:3 * P], start=False, stop=True, skip_group_check=True)
                pe.matmul(den[0:NS, SEQ:SEQ + 1], ew[0:NS, 3 * P:3 * P + NS], ones[0:NS, 0:1], start=True, stop=False)
                for e in range(ET):
                    last = pe.matmul(den[0:NS, SEQ:SEQ + 1], qn[:, e], ones[:, 0:1], start=False, stop=e == ET - 1)
                last.then_inc(den_psum, 1)

            def numerators(h):
                pe.wait_ge(stage_read_a, reads(use(h, "vt1"))[1])
                if h:
                    pe.wait_ge(h_ready, h)
                for e in range(ET):
                    out = ps[:, 4 + e // 2, SEQ * (e % 2):SEQ * (e % 2) + SEQ]
                    es = slice(P * e, P * e + P)
                    pe.matmul(out, vtk[:, 0, es], ew[:, 0:2 * P], start=True, stop=False, skip_group_check=True)
                    last = pe.matmul(out[:, P:SEQ], vtk[:, 1, es], ew[:, 2 * P:3 * P], start=False, stop=True,
                                     skip_group_check=True)
                last.then_inc(num_psum, 1)

            def key_sums(h):
                out = staged(h, "n")
                for e in range(ET):
                    c0 = (NB + 2) * e
                    es = slice(P * e, P * e + P)
                    for tt in range(2):
                        pe.matmul(out[:, c0 + NB:c0 + NB + 1], ktok[:, tt, es], tokg[:, tt, NH + h:NH + h + 1],
                                  start=tt == 0, stop=tt == 1)
                    last = pe.matmul(out[:, c0:c0 + NB], kst[:, h % 2, es], seln, start=True, stop=True)
                last.then_inc(stage_full, 1)

            def old_state(h, b, half):
                i = item(h, b, half)
                s = i % C_SLOTS
                if h and b == half == 0:
                    pe.wait_ge(hs_taken, h)
                pe.wait_ge(qs_ready, h + 1)
                pe.wait_ge(c_in[s], 16 * loads(i))
                for d in range(HD2):
                    e = HD2 * half + d
                    last = pe.matmul(ps[0:NS, 2, :], qz_of1(h, e, b), cring[:, s, d], start=b == e == 0,
                                     stop=b == NB - 1 and e == ET - 1, skip_group_check=True)
                return last

            def outer(h, b, half):
                i = item(h, b, half)
                if i:
                    pe.wait_ge(c_new, i)
                if b < NB:
                    pe.wait_ge(stage_read_v, reads(use(h, "ks"))[1])
                    pe.wait_ge(vb_ready, NB * h + b + 1)
                for d in range(HD2):
                    e = HD2 * half + d
                    es = slice(P * e, P * e + P)
                    if b < NB:
                        last = pe.matmul(ps[:, d, :], kst[:, h % 2, es], vb[:, (NB * h + b) % 2], start=True, stop=True)
                    else:
                        for tt in range(2):
                            last = pe.matmul(ps[:, d, :], ktok[:, tt, es], vw[:, tt], start=tt == 0, stop=tt == 1)
                last.then_inc(c_mm, 1)

            def chunk(h, b):
                if b == 0:
                    denominators(h)
                    numerators(h)
                    pe.matmul(ps[0:NS, 2, :], ew[0:NS, 3 * P:3 * P + NS], vtk_s, start=False, stop=False,
                              skip_group_check=True)
                if b == 1:
                    key_sums(h)
                if b == 2:
                    outer(h, NB, 0)
                if b == 3:
                    outer(h, NB, 1)
                    pe.wait_ge(h_sq, h + 1)
                    out = staged(h, "mean")
                    for e in range(ET):
                        last = pe.matmul(out[:, 0:SEQ], ones, qf[:, e, 0:SEQ], start=e == 0, stop=e == ET - 1)
                    last.then_inc(stage_full, 1)
                if h + 1 < NH:
                    if b == 4:
                        qk(h + 1)
                    if b == 5:
                        keys_by_token(h + 1)
                    if b == 6:
                        values_by_token(h + 1)
                    if b == 7:
                        head_rows(h + 1)
                        scores(h + 1)

            pe.wait_ge(gcol_taken, 1)
            values_by_token(0)
            head_rows(0)
            scores(0)
            for h in range(NH):
                for b in range(NB):
                    for half in range(2):
                        last = old_state(h, b, half)
                        if b == NB - 1 and half == 1:
                            last.then_inc(hs_psum, 1)
                        outer(h, b, half)
                    chunk(h, b)
            pe.wait_ge(hs_taken, NH)
            for h in range(NH):
                pe.wait_ge(hs_scaled, h + 1)
                for e in range(ET):
                    m = ET * h + e
                    last = pe.transpose(ps[:, 2, NS * m:NS * m + NS], hs[:, h, P * e:P * e + P], ident[0:NS, 0:NS])
            last.then_inc(hst_ready, 1)

            pe.wait_ge(y1_ready, NH + 1)
            steps(OUT_C, 2, lambda kk: (y1_hi[:, kk], y1_lo[:, kk]), peel=False)
            mean(5)
            from_norm(UP1, 3, 6)
            pe.wait_ge(hid_ready, 64)
            steps(DOWN1, 4, lambda kk: (hid_hi[:, kk], hid_lo[:, kk]), peel=False)
            mean(7)


def constants():
    f = np.float32

    def held(delta):
        n = sum((delta >= 0) & (delta <= w) & (delta % d == 0) for w, d in DIL)
        return np.where(n > 0, np.log(np.maximum(n, 1)), NEG).astype(f)

    i = np.arange(P)[:, None]
    c = {"ident": np.eye(P, dtype=f), "ones": np.ones((P, P), f)}
    c["amask"] = np.concatenate([held(i - np.arange(P)), held(P + i - np.arange(2 * P))], 1)
    b4, t = i // 32, i % NT
    own = np.arange(NS)[None]
    parts = [held(PAST + t - np.array(KEYS)[None])]
    for f4 in (0, HALF_B):
        parts.append(np.where(own // NT == b4 + f4, held(t - own % NT), f(NEG)))
    c["smask"] = np.concatenate(parts, 1)
    pos = np.concatenate([np.arange(SEQ), np.tile(PAST + np.arange(NT), NB)]).astype(f)
    inv = f(THETA) ** (-np.arange(0, ROT, 2, dtype=f) / f(ROT))
    ang = np.tile(inv, 2)[:, None] * pos[None]
    c["cosr"], c["sinr"] = np.cos(ang), np.sin(ang)
    m = np.zeros((ROT, ROT), f)
    for o in range(ROT // 2):
        m[o + ROT // 2, o], m[o, o + ROT // 2] = -1, 1
    c["rotm"] = m
    c["bmask"] = (i // QB == np.arange(P) // QB).astype(f)
    c["tri"] = np.where(i <= np.arange(P), 0, NEG).astype(f)
    s = np.arange(NS)[:, None]
    c["stri"] = np.where((s // NT == own // NT) & (s <= own), 0, NEG).astype(f)
    own3 = np.tile(s // NT == np.arange(NB), (3, 1)).astype(f)
    once = own3 * (np.arange(3 * NS) // NS != 1)[:, None]
    c["sel3"] = np.concatenate([own3, once], 1)
    c["sel"] = np.repeat(np.eye(NH, dtype=f), P, 1)
    return c


def cols(a):
    a = np.asarray(a)
    a = a.reshape(-1, a.shape[-1] // P, P)
    return a.transpose(2, 0, 1)


def lay_out(i):
    f = {n: np.asarray(a) for n, a in i.items()}
    one = lambda a: a.reshape(P, -1)
    x = np.concatenate([f["x_prompt"].reshape(SEQ, D), f["x_sample"].reshape(NS, D)])
    par = [one(cols(f[n])) for n in ("norm_mix_pre", "norm_mix_post", "norm_ffn_pre", "norm_ffn_post",
                                     "conv_a_w", "conv_a_b", "lru_ba", "lru_bx", "lru_lambda")]
    by_tile = lambda a: one(cols(a).transpose(0, 2, 1))
    par += [by_tile(f["state_rglru_h"][0]), by_tile(f["state_rglru_conv"][0])]
    par += [one(cols(f[n])) for n in ("conv_c_w", "conv_c_b", "mlstm_norm", "mlstm_skip")]
    n0 = f["state_mlstm_n"][0].transpose(1, 2, 0).reshape(NH, ET, P, NB)
    par += [one(n0.transpose(2, 0, 1, 3)), by_tile(f["state_mlstm_conv"][0])]
    mats = [f["w_in_ab"][0], f["w_out_ab"][0], f["w_ffn_up"][0], f["w_ffn_down"][0],
            f["w_in_c"][0], f["w_out_c"][0], f["w_ffn_up"][1], f["w_ffn_down"][1]]
    units = []
    for w in mats:
        k, m = w.shape
        w = w.reshape(k // (UK * P), UK, P, m // (UM * P), UM, P)
        units.append(w.transpose(3, 0, 2, 4, 1, 5).reshape(-1, P, UM * TILE))
    keys = f["cache_swa_k"][0][:, KEYS].transpose(0, 2, 3, 1).reshape(NB * H, P, NK)
    vals = f["cache_swa_v"][0][:, KEYS].reshape(NB, KT, P, H, HD).transpose(0, 3, 2, 1, 4).reshape(NB * H, P, NK)
    blocks = [f[n][0] for n in ("mlstm_wq", "mlstm_wk", "mlstm_wv")]
    blocks += [w.transpose(0, 2, 1) for w in blocks]
    blocks = [w.reshape(CT, P, QB).transpose(1, 0, 2).reshape(P, -1) for w in blocks]
    gate = f["mlstm_w_gate"][0].reshape(3 * CT, P, 2 * NH).transpose(1, 0, 2)
    small = np.concatenate([f["mlstm_b_gate"][0].reshape(2, NH).T, f["state_mlstm_m"][0].T], 1)
    arrays = {"x": one(cols(x).transpose(0, 2, 1)), "par": np.concatenate(par, 1), "weights": np.concatenate(units),
              "kv": np.concatenate([keys, vals]), "qkvw": np.concatenate(blocks, 1), "wgate": one(gate),
              "gsml": small, "lru_wa": f["lru_wa"][0], "lru_wx": f["lru_wx"][0], "C0": f["state_mlstm_C"][0]}
    arrays.update(constants())
    return {n: np.ascontiguousarray(a, dtype=np.float32) for n, a in arrays.items()}


OUTS = {"x": (P, MT * T), "k": (P, H * T), "v": (P, H * T), "pack_a": (P, MT * (1 + NB) * CW),
        "pack_c": (P, CT * (1 + NB) * PAD), "pack_n": (P, NH * ET * (1 + NB)), "pack_m": (NH, 1 + NB),
        "Cs": (NB, NH, DH, DH), "Cp": (NH, DH, DH)}


def lay_back(o):
    def tokens(a):
        a = a.reshape(P, -1, T).transpose(2, 1, 0)
        return a[:SEQ], a[SEQ:].reshape(NB, NT, -1, P)

    xp, xs = tokens(o["x"])
    kp, ks = tokens(o["k"])
    vp, vs = tokens(o["v"])
    a = o["pack_a"].reshape(P, MT, 1 + NB, CW).transpose(2, 3, 1, 0).reshape(1 + NB, CW, D)
    c = o["pack_c"].reshape(P, CT, 1 + NB, PAD).transpose(2, 3, 1, 0).reshape(1 + NB, PAD, DC)
    n = o["pack_n"].reshape(P, NH, ET, 1 + NB).transpose(3, 1, 2, 0).reshape(1 + NB, NH, DH)
    m = o["pack_m"].T
    out = (xp.reshape(1, SEQ, D), xs.reshape(NB, NT, D),
           a[None, :1, :PAD], a[None, 1:, :PAD], a[None, :1, PAD], a[None, 1:, PAD],
           kp[None, None], ks[None], vp[None, None], vs[None],
           c[None, :1], c[None, 1:], o["Cp"][None, None], o["Cs"][None],
           n[None, :1], n[None, 1:], m[None, :1], m[None, 1:])
    return tuple(np.ascontiguousarray(t) for t in out)


def kernel(**inputs):
    import concourse.bacc as bacc
    from concourse.bass_utils import run_bass_kernel_spmd

    nc = bacc.Bacc("TRN2", target_bir_lowering=False, num_devices=1)
    arrays = lay_out(inputs)
    A = {n: nc.dram_tensor(f"in_{n}", a.shape, F32, kind="ExternalInput").ap() for n, a in arrays.items()}
    O = {n: nc.dram_tensor(f"out_{n}", s, F32, kind="ExternalOutput").ap() for n, s in OUTS.items()}
    program(nc, A, O)
    r = run_bass_kernel_spmd(nc, [{f"in_{n}": a for n, a in arrays.items()}], core_ids=[0])
    return lay_back({n: r.results[0][f"out_{n}"] for n in OUTS})
```
